# Optimizing a Trainium2 kernel written in Bass

```python
import math
import jax
import jax.numpy as jnp
from jax import lax
import numpy as np
import jax, jax.numpy as jnp

D_MODEL = 1024
BATCH = 1
SEQ = 512
DEPTH = 2

GRID_W = 64
CTX_LEN = 256
N_MIXERS = 3
DN_ALPHA = (2 * DEPTH) ** 0.25
DN_BETA = (8 * DEPTH) ** -0.25
LN_EPS = 1e-5

RK_HEAD = 64
RK_HEADS = D_MODEL // RK_HEAD
RK_DECAY_LORA = 64
RK_ICLR_LORA = 64
RK_GATE_LORA = 128
RK_DECAY_SCALE = math.exp(-0.5)
RK_GN_EPS = 64e-5

POOL_WINDOWS = (2, 4, 8, 16)
POOL_GROUP = D_MODEL // len(POOL_WINDOWS)

GDN_HEAD = 128
GDN_HEADS = D_MODEL // GDN_HEAD
GDN_CONV = 4
GDN_CHUNK = 64
GDN_NORM_EPS = 1e-6
GDN_IN = 4 * D_MODEL + 4 * GDN_HEADS

D_FF = 2816
N_EXPERTS = 8
TOP_K = 2
D_FF_EXPERT = 1408

N_RWKV_LAYERS = len(range(0, DEPTH, N_MIXERS))
N_POOL_LAYERS = len(range(1, DEPTH, N_MIXERS))
N_GDN_LAYERS = len(range(2, DEPTH, N_MIXERS))
N_DENSE_LAYERS = len(range(0, DEPTH, 2))
N_MOE_LAYERS = len(range(1, DEPTH, 2))


def layer_norm(x, g, b):
    xf = x.astype(jnp.float32)
    mean = jnp.mean(xf, axis=-1, keepdims=True)
    var = jnp.mean(jnp.square(xf - mean), axis=-1, keepdims=True)
    return ((xf - mean) * lax.rsqrt(var + LN_EPS) * g + b).astype(x.dtype)

def flip_time(t):
    return jnp.flip(t, axis=1)

def identity(t):
    return t

def qshift_grid(h, n_rows):
    b, n, d = h.shape
    q = d // 4
    grid = h.reshape(b, n_rows, GRID_W, d)
    left = jnp.pad(grid[:, :, :-1, :q], ((0, 0), (0, 0), (1, 0), (0, 0)))
    right = jnp.pad(grid[:, :, 1:, q:2 * q], ((0, 0), (0, 0), (0, 1), (0, 0)))
    up = jnp.pad(grid[:, :-1, :, 2 * q:3 * q], ((0, 0), (1, 0), (0, 0), (0, 0)))
    down = jnp.pad(grid[:, 1:, :, 3 * q:], ((0, 0), (0, 1), (0, 0), (0, 0)))
    return jnp.concatenate([left, right, up, down], axis=-1).reshape(b, n, d)

def bishift_seq(h):
    half = h.shape[-1] // 2
    prev = jnp.pad(h[:, :-1, :half], ((0, 0), (1, 0), (0, 0)))
    nxt = jnp.pad(h[:, 1:, half:], ((0, 0), (0, 1), (0, 0)))
    return jnp.concatenate([prev, nxt], axis=-1)

def to_heads(t, n_heads, head_dim):
    return t.reshape(*t.shape[:-1], n_heads, head_dim)

def rwkv7_branch(h, shifted, mu, w_rkv, w0, w1, w2, a0, a1, a2, k_k, k_a):
    f32 = jnp.float32
    xx = shifted - h
    xr, xw, xk, xv, xa, xg = (h + xx * mu[m] for m in range(6))
    r = (xr @ w_rkv[0]).astype(f32)
    k = (xk @ w_rkv[1]).astype(f32)
    v = (xv @ w_rkv[2]).astype(f32)
    d_lora = jnp.einsum('zbtr,zrd->zbtd', jnp.tanh(jnp.einsum('btd,zdr->zbtr', xw, w1)), w2)
    log_w = -RK_DECAY_SCALE * jax.nn.sigmoid((w0[:, None, None, :] + d_lora).astype(f32))
    a_lora = jnp.einsum('zbtr,zrd->zbtd', jnp.einsum('btd,zdr->zbtr', xa, a1), a2)
    a = jax.nn.sigmoid((a0[:, None, None, :] + a_lora).astype(f32))
    kk = to_heads(k * k_k.astype(f32), RK_HEADS, RK_HEAD)
    kk = kk / jnp.maximum(jnp.sqrt(jnp.sum(kk * kk, axis=-1, keepdims=True)), 1e-12)
    k_dir = k[None] * (1.0 + (a - 1.0) * k_a.astype(f32))
    hd = lambda t: to_heads(t, RK_HEADS, RK_HEAD)
    return (hd(r), hd(log_w), kk, hd(a), hd(k_dir), hd(v), xg)

def wkv7_scan(s0, r, w, kk, a, k, v):
    def step(s, inp):
        r_t, w_t, kk_t, a_t, k_t, v_t = inp
        s_kk = jnp.einsum('bhvk,bhk->bhv', s, kk_t)
        s = (s * w_t[:, :, None, :] - s_kk[..., None] * (kk_t * a_t)[:, :, None, :]
             + v_t[..., None] * k_t[:, :, None, :])
        return s, jnp.einsum('bhvk,bhk->bhv', s, r_t)
    xs = tuple(jnp.moveaxis(t, 1, 0) for t in (r, w, kk, a, k, v))
    s_final, ys = lax.scan(step, s0, xs)
    return jnp.moveaxis(ys, 0, 1), s_final

def rwkv7_dir_inputs(feats, d, flip):
    r, log_w, kk, a, k_dir, v, _ = feats
    return [flip(t) for t in (r, jnp.exp(log_w[d]), kk, a[d], k_dir[d], v)]

def rwkv7_out(y, feats, r_k, g1, g2, lnx_g, lnx_b, w_o):
    r, _, _, _, k_dir, v, xg = feats
    b, n = y.shape[:2]
    mean = jnp.mean(y, axis=-1, keepdims=True)
    var = jnp.mean(jnp.square(y - mean), axis=-1, keepdims=True)
    yn = ((y - mean) * lax.rsqrt(var + RK_GN_EPS)).reshape(b, n, D_MODEL) * lnx_g + lnx_b
    coef = jnp.einsum('bthn,zbthn,hn->bth', r, k_dir, r_k.astype(jnp.float32))
    bonus = (coef[..., None] * v).reshape(b, n, D_MODEL)
    gate = jax.nn.sigmoid(xg @ g1) @ g2
    return ((yn + bonus).astype(xg.dtype) * gate) @ w_o

def rwkv7_mixer(h, hc, n_rows, mu, w_rkv, w0, w1, w2, a0, a1, a2, g1, g2, k_k, k_a, r_k,
                lnx_g, lnx_b, w_o, want_ctx):
    lat = rwkv7_branch(h, qshift_grid(h, n_rows), mu, w_rkv, w0, w1, w2, a0, a1, a2, k_k, k_a)
    cx = rwkv7_branch(hc, bishift_seq(hc), mu, w_rkv, w0, w1, w2, a0, a1, a2, k_k, k_a)
    zero_state = jnp.zeros((h.shape[0], RK_HEADS, RK_HEAD, RK_HEAD), jnp.float32)
    y_lat = 0.0
    y_ctx = 0.0
    for d in range(2):
        flip = flip_time if d == 1 else identity
        yc, s_ctx = wkv7_scan(zero_state, *rwkv7_dir_inputs(cx, d, flip))
        yl, _ = wkv7_scan(s_ctx, *rwkv7_dir_inputs(lat, d, flip))
        y_lat = y_lat + flip(yl)
        y_ctx = y_ctx + flip(yc)
    out_lat = rwkv7_out(y_lat, lat, r_k, g1, g2, lnx_g, lnx_b, w_o)
    out_ctx = rwkv7_out(y_ctx, cx, r_k, g1, g2, lnx_g, lnx_b, w_o) if want_ctx else None
    return out_lat, out_ctx

def centred_pool_minus_self(x, window):
    n = x.shape[-2]
    xf = x.astype(jnp.float32)
    csum = jnp.cumsum(xf, axis=-2)
    csum = jnp.concatenate([jnp.zeros_like(csum[..., :1, :]), csum], axis=-2)
    t = jnp.arange(n)
    lo = jnp.clip(t - window // 2, 0, n)
    hi = jnp.clip(t + window // 2, 0, n)
    total = jnp.take(csum, hi, axis=-2) - jnp.take(csum, lo, axis=-2)
    count = (hi - lo).astype(jnp.float32)[:, None]
    return (total / count - xf).astype(x.dtype)

def pool_mixer(h, pool_w, pool_scale):
    outs = []
    for gi, win in enumerate(POOL_WINDOWS):
        xg = h[..., gi * POOL_GROUP:(gi + 1) * POOL_GROUP]
        outs.append(centred_pool_minus_self(xg, win) @ pool_w[gi])
    return jnp.concatenate(outs, axis=-1) * pool_scale

def depthwise_conv_centred(x, w):
    left = GDN_CONV // 2
    right = GDN_CONV - 1 - left
    return lax.conv_general_dilated(x, w[:, None, :], window_strides=(1,), padding=[(left, right)],
                                    dimension_numbers=('NWC', 'WIO', 'NWC'),
                                    feature_group_count=x.shape[-1])

def l2_normalize(t, eps):
    return t * lax.rsqrt(jnp.sum(t * t, axis=-1, keepdims=True) + eps)

def gdn_features(h, w_in, conv_w, a_log, dt_bias):
    f32 = jnp.float32
    b, n, d = h.shape
    proj = h @ w_in
    qkv = jax.nn.silu(depthwise_conv_centred(proj[..., :3 * d], conv_w)).astype(f32)
    q, k, v = (to_heads(t, GDN_HEADS, GDN_HEAD) for t in jnp.split(qkv, 3, axis=-1))
    q = l2_normalize(q, 1e-6) * GDN_HEAD ** -0.5
    k = l2_normalize(k, 1e-6)
    z = proj[..., 3 * d:4 * d]
    a_pre = proj[..., 4 * d:4 * d + 2 * GDN_HEADS].astype(f32).reshape(b, n, 2, GDN_HEADS)
    b_pre = proj[..., 4 * d + 2 * GDN_HEADS:].astype(f32).reshape(b, n, 2, GDN_HEADS)
    g = -jnp.exp(a_log.astype(f32)) * jax.nn.softplus(a_pre + dt_bias.astype(f32))
    beta = jax.nn.sigmoid(b_pre)
    return q, k, v, z, g, beta

def gated_delta_chunked(q, k, v, g, beta, s0):
    b, n, nh, dk = k.shape
    c = GDN_CHUNK
    nc = n // c

    def chunks(t):
        t = jnp.moveaxis(t, 2, 1)
        return t.reshape(b, nh, nc, c, *t.shape[3:])

    q, k, v, g, beta = chunks(q), chunks(k), chunks(v), chunks(g), chunks(beta)
    gc = jnp.cumsum(g, axis=-1)
    causal = jnp.tril(jnp.ones((c, c), bool))
    strict = jnp.tril(jnp.ones((c, c), bool), -1)
    decay = jnp.exp(jnp.where(causal, gc[..., :, None] - gc[..., None, :], -jnp.inf))
    kb = k * beta[..., None]
    vb = v * beta[..., None]
    lower = jnp.where(strict, jnp.einsum('bhnid,bhnjd->bhnij', kb, k) * decay, 0.0)
    eye = jnp.eye(c, dtype=lower.dtype)
    tmat = lax.linalg.triangular_solve(eye + lower, jnp.broadcast_to(eye, lower.shape),
                                       left_side=True, lower=True)
    u = tmat @ vb
    w = tmat @ (kb * jnp.exp(gc)[..., None])
    a_qk = jnp.where(causal, jnp.einsum('bhnid,bhnjd->bhnij', q, k) * decay, 0.0)
    q_dec = q * jnp.exp(gc)[..., None]
    k_dec = k * jnp.exp(gc[..., -1:] - gc)[..., None]
    g_last = jnp.exp(gc[..., -1])

    def step(s, inp):
        u_i, w_i, q_i, k_i, a_i, gl_i = inp
        v_new = u_i - w_i @ s
        o_i = q_i @ s + a_i @ v_new
        s = s * gl_i[..., None, None] + jnp.swapaxes(k_i, -1, -2) @ v_new
        return s, o_i

    xs = tuple(jnp.moveaxis(t, 2, 0) for t in (u, w, q_dec, k_dec, a_qk, g_last))
    s_final, o = lax.scan(step, s0, xs)
    o = jnp.moveaxis(o, 0, 2).reshape(b, nh, n, -1)
    return jnp.moveaxis(o, 1, 2), s_final

def gdn_out(o, z, norm_w, w_o):
    b, n = z.shape[:2]
    on = o * lax.rsqrt(jnp.mean(o * o, axis=-1, keepdims=True) + GDN_NORM_EPS) * norm_w.astype(jnp.float32)
    zf = to_heads(z.astype(jnp.float32), GDN_HEADS, GDN_HEAD)
    y = (on * jax.nn.silu(zf)).reshape(b, n, D_MODEL).astype(z.dtype)
    return y @ w_o

def gdn_mixer(h, hc, w_in, conv_w, a_log, dt_bias, norm_w, w_o, want_ctx):
    lq, lk, lv, lz, lg, lb = gdn_features(h, w_in, conv_w, a_log, dt_bias)
    cq, ck, cv, cz, cg, cb = gdn_features(hc, w_in, conv_w, a_log, dt_bias)
    zero_state = jnp.zeros((h.shape[0], GDN_HEADS, GDN_HEAD, GDN_HEAD), jnp.float32)
    o_lat = 0.0
    o_ctx = 0.0
    for d in range(2):
        flip = flip_time if d == 1 else identity
        oc, s_ctx = gated_delta_chunked(flip(cq), flip(ck), flip(cv), flip(cg[:, :, d]), flip(cb[:, :, d]),
                                        zero_state)
        ol, _ = gated_delta_chunked(flip(lq), flip(lk), flip(lv), flip(lg[:, :, d]), flip(lb[:, :, d]), s_ctx)
        o_lat = o_lat + flip(ol)
        o_ctx = o_ctx + flip(oc)
    y_lat = gdn_out(o_lat, lz, norm_w, w_o)
    y_ctx = gdn_out(o_ctx, cz, norm_w, w_o) if want_ctx else None
    return y_lat, y_ctx

def swiglu(h, w1, w3, w2):
    return (jax.nn.silu(h @ w1) * (h @ w3)) @ w2

def moe_swiglu(h, router_w, router_b, w1, w3, w2):
    logits = (h @ router_w).astype(jnp.float32) + router_b.astype(jnp.float32)
    top_logit, top_idx = lax.top_k(logits, TOP_K)
    top_p = jax.nn.softmax(top_logit, axis=-1)
    gates = jnp.einsum('btk,btke->bte', top_p,
                       jax.nn.one_hot(top_idx, N_EXPERTS, dtype=jnp.float32)).astype(h.dtype)
    y = jnp.zeros_like(h)
    for e in range(N_EXPERTS):
        y = y + gates[..., e:e + 1] * swiglu(h, w1[e], w3[e], w2[e])
    return y

def first_inputs(seed: int = 0) -> dict:
    key = jax.random.key(seed)
    ks = iter(jax.random.split(key, 64))
    f32 = jnp.float32

    def nrm(shape, std):
        return jax.random.normal(next(ks), shape, f32) * std

    def near_one(shape):
        return 1.0 + nrm(shape, 0.1)

    D, H, N = D_MODEL, RK_HEADS, RK_HEAD
    NA, NB, NC, ND, NM = N_RWKV_LAYERS, N_POOL_LAYERS, N_GDN_LAYERS, N_DENSE_LAYERS, N_MOE_LAYERS
    dt = jnp.exp(jax.random.uniform(next(ks), (NC, 2, GDN_HEADS), f32, math.log(1e-3), math.log(1e-1)))
    gdn_dt_bias = dt + jnp.log(-jnp.expm1(-dt))
    return {
        'x': nrm((BATCH, SEQ, D), 1.0),
        'c': nrm((BATCH, D), 1.0),
        'ctx': nrm((BATCH, CTX_LEN, D), 1.0),
        'c_ctx': nrm((D,), 1.0),
        'ada_w': nrm((DEPTH, D, 6 * D), D ** -0.5),
        'ada_b': nrm((DEPTH, 6 * D), 0.02),
        'ln_g': near_one((DEPTH, 2, D)),
        'ln_b': nrm((DEPTH, 2, D), 0.02),
        'rk_mu': jax.random.uniform(next(ks), (NA, 6, D), f32),
        'rk_w_rkv': nrm((NA, 3, D, D), D ** -0.5),
        'rk_w0': nrm((NA, 2, D), 1.0),
        'rk_w1': nrm((NA, 2, D, RK_DECAY_LORA), D ** -0.5),
        'rk_w2': nrm((NA, 2, RK_DECAY_LORA, D), 0.5 * RK_DECAY_LORA ** -0.5),
        'rk_a0': nrm((NA, 2, D), 0.5),
        'rk_a1': nrm((NA, 2, D, RK_ICLR_LORA), D ** -0.5),
        'rk_a2': nrm((NA, 2, RK_ICLR_LORA, D), 0.5 * RK_ICLR_LORA ** -0.5),
        'rk_g1': nrm((NA, D, RK_GATE_LORA), D ** -0.5),
        'rk_g2': nrm((NA, RK_GATE_LORA, D), RK_GATE_LORA ** -0.5),
        'rk_k_k': near_one((NA, D)),
        'rk_k_a': near_one((NA, D)),
        'rk_r_k': nrm((NA, H, N), 0.1),
        'rk_lnx_g': near_one((NA, D)),
        'rk_lnx_b': nrm((NA, D), 0.02),
        'rk_w_o': nrm((NA, D, D), DN_BETA * D ** -0.5),
        'pool_w': nrm((NB, len(POOL_WINDOWS), POOL_GROUP, POOL_GROUP), DN_BETA * POOL_GROUP ** -0.5),
        'pool_scale': near_one((NB, D)),
        'gdn_w_in': nrm((NC, D, GDN_IN), D ** -0.5),
        'gdn_conv_w': nrm((NC, GDN_CONV, 3 * D), GDN_CONV ** -0.5),
        'gdn_a_log': jnp.log(jax.random.uniform(next(ks), (NC, 2, GDN_HEADS), f32, 1.0, 16.0)),
        'gdn_dt_bias': gdn_dt_bias,
        'gdn_norm_w': near_one((NC, GDN_HEAD)),
        'gdn_w_o': nrm((NC, D, D), DN_BETA * D ** -0.5),
        'ffn_w1': nrm((ND, D, D_FF), D ** -0.5),
        'ffn_w3': nrm((ND, D, D_FF), D ** -0.5),
        'ffn_w2': nrm((ND, D_FF, D), DN_BETA * D_FF ** -0.5),
        'moe_router_w': nrm((NM, D, N_EXPERTS), D ** -0.5),
        'moe_router_b': nrm((NM, N_EXPERTS), 0.01),
        'moe_w1': nrm((NM, N_EXPERTS, D, D_FF_EXPERT), D ** -0.5),
        'moe_w3': nrm((NM, N_EXPERTS, D, D_FF_EXPERT), D ** -0.5),
        'moe_w2': nrm((NM, N_EXPERTS, D_FF_EXPERT, D), DN_BETA * D_FF_EXPERT ** -0.5),
    }

def first_block(x, c, ctx, c_ctx, ada_w, ada_b, ln_g, ln_b,
              rk_mu, rk_w_rkv, rk_w0, rk_w1, rk_w2, rk_a0, rk_a1, rk_a2, rk_g1, rk_g2,
              rk_k_k, rk_k_a, rk_r_k, rk_lnx_g, rk_lnx_b, rk_w_o,
              pool_w, pool_scale,
              gdn_w_in, gdn_conv_w, gdn_a_log, gdn_dt_bias, gdn_norm_w, gdn_w_o,
              ffn_w1, ffn_w3, ffn_w2,
              moe_router_w, moe_router_b, moe_w1, moe_w3, moe_w2):
    b, n, d = x.shape
    n_rows = n // GRID_W
    for i in range(DEPTH):
        want_ctx = i < DEPTH - 1
        mod = jax.nn.silu(c) @ ada_w[i] + ada_b[i]
        mod_c = jax.nn.silu(c_ctx) @ ada_w[i] + ada_b[i]
        sh1, sc1, gt1, sh2, sc2, gt2 = jnp.split(mod[:, None, :], 6, axis=-1)
        csh1, csc1, cgt1, csh2, csc2, cgt2 = jnp.split(mod_c, 6, axis=-1)
        h = x * (1.0 + sc1) + sh1
        hc = ctx * (1.0 + csc1) + csh1
        kind, j = i % N_MIXERS, i // N_MIXERS
        if kind == 0:
            y, yc = rwkv7_mixer(h, hc, n_rows, rk_mu[j], rk_w_rkv[j], rk_w0[j], rk_w1[j], rk_w2[j],
                                rk_a0[j], rk_a1[j], rk_a2[j], rk_g1[j], rk_g2[j], rk_k_k[j], rk_k_a[j],
                                rk_r_k[j], rk_lnx_g[j], rk_lnx_b[j], rk_w_o[j], want_ctx)
        elif kind == 1:
            y = pool_mixer(h.reshape(b, n_rows, GRID_W, d), pool_w[j], pool_scale[j]).reshape(b, n, d)
            yc = pool_mixer(hc, pool_w[j], pool_scale[j]) if want_ctx else None
        else:
            y, yc = gdn_mixer(h, hc, gdn_w_in[j], gdn_conv_w[j], gdn_a_log[j], gdn_dt_bias[j],
                              gdn_norm_w[j], gdn_w_o[j], want_ctx)
        if i % 2 == 0:
            e = i // 2
            channel_mixer = lambda t, e=e: swiglu(t, ffn_w1[e], ffn_w3[e], ffn_w2[e])
        else:
            e = i // 2
            channel_mixer = lambda t, e=e: moe_swiglu(t, moe_router_w[e], moe_router_b[e],
                                                      moe_w1[e], moe_w3[e], moe_w2[e])
        x = layer_norm(DN_ALPHA * x + gt1 * y, ln_g[i, 0], ln_b[i, 0])
        x = layer_norm(DN_ALPHA * x + gt2 * channel_mixer(x * (1.0 + sc2) + sh2), ln_g[i, 1], ln_b[i, 1])
        if want_ctx:
            ctx = layer_norm(DN_ALPHA * ctx + cgt1 * yc, ln_g[i, 0], ln_b[i, 0])
            ctx = layer_norm(DN_ALPHA * ctx + cgt2 * channel_mixer(ctx * (1.0 + csc2) + csh2),
                             ln_g[i, 1], ln_b[i, 1])
    return x


DEPTH_2 = 1

GLA_HEADS = 4
GLA_VAL_WIDTH = D_MODEL // 2
GLA_DV = GLA_VAL_WIDTH // GLA_HEADS
GLA_DK = GLA_DV // 2
GLA_KEY_WIDTH = GLA_HEADS * GLA_DK
GLA_GATE_RANK = 16
GLA_TAU = 16.0
GLA_CHUNK = 64
ATT_WIDTH = D_MODEL - GLA_VAL_WIDTH
ATT_HEAD_DIM = 64
ATT_HEADS = ATT_WIDTH // ATT_HEAD_DIM
ROT_DIM = ATT_HEAD_DIM // 4
ROPE_THETA = 500000.0
DILATED_PATTERNS = ((128, 1), (512, 4), (2048, 16))
MIX_WIDTH = GLA_VAL_WIDTH + ATT_WIDTH
IN_WIDTH = 2 * GLA_KEY_WIDTH + 2 * GLA_VAL_WIDTH + 2 * GLA_GATE_RANK + 3 * ATT_WIDTH
MOE_GROUPS = 4
MOE_EXPERTS_PER_GROUP = 8
MOE_N_EXPERTS = MOE_GROUPS * MOE_EXPERTS_PER_GROUP
MOE_TOP_K = 2
MOE_D_FF = D_MODEL // 2
MOE_BLOCK = 128
EPS = 1e-6
NEG_INF = -1e30


def _rmsnorm(x, w):
    xf = x.astype(jnp.float32)
    y = xf * lax.rsqrt(jnp.mean(xf * xf, axis=-1, keepdims=True) + EPS)
    return (y * w.astype(jnp.float32)).astype(x.dtype)

def _gla_one_direction(q, k, v, log_a):
    B, H, S, dk = q.shape
    dv = v.shape[-1]
    C = GLA_CHUNK
    n = S // C
    q = q.reshape(B, H, n, C, dk)
    k = k.reshape(B, H, n, C, dk)
    v = v.reshape(B, H, n, C, dv)
    b = jnp.cumsum(log_a.reshape(B, H, n, C, dk), axis=-2)
    b_last = b[..., -1:, :]
    q_dec = q * jnp.exp(b)
    k_inv = k * jnp.exp(-b)
    k_end = k * jnp.exp(b_last - b)
    lower = jnp.tril(jnp.ones((C, C), dtype=bool))
    attn = jnp.where(lower, jnp.einsum('bhncd,bhnsd->bhncs', q_dec, k_inv), 0.0)
    o_intra = jnp.einsum('bhncs,bhnsv->bhncv', attn, v)
    chunk_kv = jnp.einsum('bhncd,bhncv->bhndv', k_end, v)
    chunk_decay = jnp.exp(b_last[..., 0, :])

    def step(state, inp):
        kv_n, dec_n = inp
        return state * dec_n[..., None] + kv_n, state

    init = jnp.zeros((B, H, dk, dv), jnp.float32)
    _, states = lax.scan(step, init, (jnp.moveaxis(chunk_kv, 2, 0), jnp.moveaxis(chunk_decay, 2, 0)))
    states = jnp.moveaxis(states, 0, 2)
    o_inter = jnp.einsum('bhncd,bhndv->bhncv', q_dec, states)
    return (o_intra + o_inter).reshape(B, H, S, dv)

def _gla_mixer(q, k, v, g_out, lr_f, lr_b, wf, bf, wb, bb, norm_w):
    B, S, _ = q.shape
    f32 = jnp.float32

    def heads(t, d):
        return t.reshape(B, S, GLA_HEADS, d).transpose(0, 2, 1, 3).astype(f32)

    qh = heads(q, GLA_DK) * (GLA_DK ** -0.5)
    kh = heads(k, GLA_DK)
    vh = heads(v, GLA_DV)
    log_a_f = heads(jax.nn.log_sigmoid(lr_f.astype(f32) @ wf.astype(f32) + bf.astype(f32)), GLA_DK) / GLA_TAU
    log_a_b = heads(jax.nn.log_sigmoid(lr_b.astype(f32) @ wb.astype(f32) + bb.astype(f32)), GLA_DK) / GLA_TAU

    def flip(t):
        return jnp.flip(t, axis=2)

    o = _gla_one_direction(qh, kh, vh, log_a_f) + flip(
        _gla_one_direction(flip(qh), flip(kh), flip(vh), flip(log_a_b)))
    o = o.transpose(0, 2, 1, 3)
    gate = g_out.reshape(B, S, GLA_HEADS, GLA_DV).astype(f32)
    o = _rmsnorm(o, norm_w) * jax.nn.silu(gate)
    return o.reshape(B, S, GLA_VAL_WIDTH).astype(q.dtype)

def _rope_tables(S):
    inv = ROPE_THETA ** (-(jnp.arange(0, ROT_DIM, 2, dtype=jnp.float32) / ROT_DIM))
    ang = jnp.arange(S, dtype=jnp.float32)[:, None] * inv[None, :]
    return jnp.cos(ang), jnp.sin(ang)

def _apply_partial_rope(t, cos, sin):
    half = ROT_DIM // 2
    t1 = t[..., :half]
    t2 = t[..., half:ROT_DIM]
    c = cos[None, :, None, :]
    s = sin[None, :, None, :]
    return jnp.concatenate([t1 * c - t2 * s, t2 * c + t1 * s, t[..., ROT_DIM:]], axis=-1)

def _banded_attention(q, k, v, radius):
    N, L, hd = q.shape
    R = radius
    nb = -(-L // R)
    Lp = nb * R
    q_p = jnp.pad(q, ((0, 0), (0, Lp - L), (0, 0))).reshape(N, nb, R, hd)
    k_p = jnp.pad(k, ((0, 0), (R, Lp - L + R), (0, 0))).reshape(N, nb + 2, R, hd)
    v_p = jnp.pad(v, ((0, 0), (R, Lp - L + R), (0, 0))).reshape(N, nb + 2, R, hd)
    k_win = jnp.concatenate([k_p[:, :-2], k_p[:, 1:-1], k_p[:, 2:]], axis=2)
    v_win = jnp.concatenate([v_p[:, :-2], v_p[:, 1:-1], v_p[:, 2:]], axis=2)
    s = jnp.einsum('nbqd,nbkd->nbqk', q_p, k_win) * (hd ** -0.5)
    qpos = (jnp.arange(nb)[:, None] * R + jnp.arange(R)[None, :])[:, :, None]
    kpos = (jnp.arange(nb)[:, None] * R - R + jnp.arange(3 * R)[None, :])[:, None, :]
    valid = (jnp.abs(qpos - kpos) <= R) & (kpos >= 0) & (kpos < L)
    s = jnp.where(valid, s, NEG_INF)
    m = jnp.max(s, axis=-1, keepdims=True)
    p = jnp.exp(s - m)
    z = jnp.sum(p, axis=-1, keepdims=True)
    o = jnp.einsum('nbqk,nbkd->nbqd', p / z, v_win)
    lse = (m + jnp.log(z))[..., 0]
    return o.reshape(N, Lp, hd)[:, :L], lse.reshape(N, Lp)[:, :L]

def _dilated_attention(q, k, v, window, dilation):
    B, S, H, hd = q.shape
    L = S // dilation

    def to_classes(t):
        return t.reshape(B, L, dilation, H, hd).transpose(0, 2, 3, 1, 4).reshape(B * dilation * H, L, hd)

    o, lse = _banded_attention(to_classes(q), to_classes(k), to_classes(v), window // (2 * dilation))
    o = o.reshape(B, dilation, H, L, hd).transpose(0, 3, 1, 2, 4).reshape(B, S, H, hd)
    lse = lse.reshape(B, dilation, H, L).transpose(0, 3, 1, 2).reshape(B, S, H)
    return o, lse

def _dilated_mixer(q, k, v):
    B, S, _ = q.shape
    cos, sin = _rope_tables(S)

    def heads(t):
        return t.reshape(B, S, ATT_HEADS, ATT_HEAD_DIM).astype(jnp.float32)

    qh = _apply_partial_rope(heads(q), cos, sin)
    kh = _apply_partial_rope(heads(k), cos, sin)
    vh = heads(v)
    outs, lses = [], []
    for window, dilation in DILATED_PATTERNS:
        o, lse = _dilated_attention(qh, kh, vh, window, dilation)
        outs.append(o)
        lses.append(lse)
    w = jax.nn.softmax(jnp.stack(lses, axis=0), axis=0)
    o = jnp.einsum('pbsh,pbshd->bshd', w, jnp.stack(outs, axis=0))
    return o.reshape(B, S, ATT_WIDTH).astype(q.dtype)

def _hier_moe(h, wg, bg, we, be, w_gate, w_up, w_down):
    T, D = h.shape
    f32 = jnp.float32
    hf = h.astype(f32)
    g_logits = hf @ wg.astype(f32) + bg.astype(f32)
    g_prob = jax.nn.softmax(g_logits, axis=-1)
    g_sel = jnp.argmax(g_logits, axis=-1)
    rows = jnp.arange(T)
    g_w = g_prob[rows, g_sel]
    e_logits = jnp.einsum('td,gde->tge', hf, we.astype(f32)) + be.astype(f32)
    e_sel_logits = e_logits[rows, g_sel]
    top_v, top_i = lax.top_k(e_sel_logits, MOE_TOP_K)
    weights = g_w[:, None] * jax.nn.softmax(top_v, axis=-1)
    expert = g_sel[:, None] * MOE_EXPERTS_PER_GROUP + top_i

    A = T * MOE_TOP_K
    e_flat = expert.reshape(-1)
    tok_flat = jnp.repeat(rows, MOE_TOP_K)
    w_flat = weights.reshape(-1)
    order = jnp.argsort(e_flat)
    e_s, tok_s, w_s = e_flat[order], tok_flat[order], w_flat[order]
    counts = jnp.zeros((MOE_N_EXPERTS,), jnp.int32).at[e_flat].add(1)
    padded = ((counts + MOE_BLOCK - 1) // MOE_BLOCK) * MOE_BLOCK
    start = jnp.cumsum(counts) - counts
    pend = jnp.cumsum(padded)
    pstart = pend - padded
    dest = pstart[e_s] + (jnp.arange(A) - start[e_s])
    n_blocks = -(-A // MOE_BLOCK) + MOE_N_EXPERTS
    cap = n_blocks * MOE_BLOCK
    buf_tok = jnp.full((cap,), T, jnp.int32).at[dest].set(tok_s.astype(jnp.int32))
    h_pad = jnp.concatenate([h, jnp.zeros((1, D), h.dtype)], axis=0)
    xb = h_pad[buf_tok].reshape(n_blocks, MOE_BLOCK, D)
    block_expert = jnp.clip(jnp.searchsorted(pend, jnp.arange(n_blocks) * MOE_BLOCK, side='right'),
                            0, MOE_N_EXPERTS - 1)

    def expert_block(args):
        xblk, eid = args
        return (jax.nn.silu(xblk @ w_gate[eid]) * (xblk @ w_up[eid])) @ w_down[eid]

    yb = lax.map(expert_block, (xb, block_expert)).reshape(cap, D)
    y_s = yb[dest] * w_s[:, None].astype(h.dtype)
    return jnp.zeros((T, D), h.dtype).at[tok_s].add(y_s)

def second_inputs(seed: int = 0) -> dict:
    key = jax.random.key(seed)
    ks = jax.random.split(key, 18)

    def nrm(k, shape, scale):
        return jax.random.normal(k, shape, jnp.float32) * scale

    return {
        'x': nrm(ks[0], (BATCH, SEQ, D_MODEL), 1.0),
        'norm1_w': 1.0 + nrm(ks[1], (DEPTH_2, D_MODEL), 0.02),
        'w_in': nrm(ks[2], (DEPTH_2, D_MODEL, IN_WIDTH), D_MODEL ** -0.5),
        'gla_fwd_gate_w': nrm(ks[3], (DEPTH_2, GLA_GATE_RANK, GLA_KEY_WIDTH), GLA_GATE_RANK ** -0.5),
        'gla_fwd_gate_b': nrm(ks[4], (DEPTH_2, GLA_KEY_WIDTH), 0.1),
        'gla_bwd_gate_w': nrm(ks[5], (DEPTH_2, GLA_GATE_RANK, GLA_KEY_WIDTH), GLA_GATE_RANK ** -0.5),
        'gla_bwd_gate_b': nrm(ks[6], (DEPTH_2, GLA_KEY_WIDTH), 0.1),
        'gla_norm_w': 1.0 + nrm(ks[7], (DEPTH_2, GLA_DV), 0.02),
        'w_out': nrm(ks[8], (DEPTH_2, MIX_WIDTH, D_MODEL), MIX_WIDTH ** -0.5),
        'norm2_w': 1.0 + nrm(ks[9], (DEPTH_2, D_MODEL), 0.02),
        'router_group_w': nrm(ks[10], (DEPTH_2, D_MODEL, MOE_GROUPS), D_MODEL ** -0.5),
        'router_group_b': nrm(ks[11], (DEPTH_2, MOE_GROUPS), 0.01),
        'router_expert_w': nrm(ks[12], (DEPTH_2, MOE_GROUPS, D_MODEL, MOE_EXPERTS_PER_GROUP), D_MODEL ** -0.5),
        'router_expert_b': nrm(ks[13], (DEPTH_2, MOE_GROUPS, MOE_EXPERTS_PER_GROUP), 0.01),
        'expert_w_gate': nrm(ks[14], (DEPTH_2, MOE_N_EXPERTS, D_MODEL, MOE_D_FF), D_MODEL ** -0.5),
        'expert_w_up': nrm(ks[15], (DEPTH_2, MOE_N_EXPERTS, D_MODEL, MOE_D_FF), D_MODEL ** -0.5),
        'expert_w_down': nrm(ks[16], (DEPTH_2, MOE_N_EXPERTS, MOE_D_FF, D_MODEL), MOE_D_FF ** -0.5),
        'final_norm_w': 1.0 + nrm(ks[17], (D_MODEL,), 0.02),
    }

def second_block(x, norm1_w, w_in, gla_fwd_gate_w, gla_fwd_gate_b, gla_bwd_gate_w, gla_bwd_gate_b,
              gla_norm_w, w_out, norm2_w, router_group_w, router_group_b, router_expert_w,
              router_expert_b, expert_w_gate, expert_w_up, expert_w_down, final_norm_w):
    B, S, D = x.shape
    sizes = [GLA_KEY_WIDTH, GLA_KEY_WIDTH, GLA_VAL_WIDTH, GLA_VAL_WIDTH,
             GLA_GATE_RANK, GLA_GATE_RANK, ATT_WIDTH, ATT_WIDTH]
    split_at = [int(c) for c in np.cumsum(sizes)]
    h = x
    for l in range(DEPTH_2):
        u = _rmsnorm(h, norm1_w[l])
        proj = u @ w_in[l]
        gq, gk, gv, gg, glf, glb, aq, ak, av = jnp.split(proj, split_at, axis=-1)
        gla_out = _gla_mixer(gq, gk, gv, gg, glf, glb, gla_fwd_gate_w[l], gla_fwd_gate_b[l],
                             gla_bwd_gate_w[l], gla_bwd_gate_b[l], gla_norm_w[l])
        att_out = _dilated_mixer(aq, ak, av)
        mixed = jnp.concatenate([gla_out, att_out], axis=-1)
        h = h + mixed @ w_out[l]
        u = _rmsnorm(h, norm2_w[l])
        moe = _hier_moe(u.reshape(B * S, D), router_group_w[l], router_group_b[l],
                        router_expert_w[l], router_expert_b[l], expert_w_gate[l],
                        expert_w_up[l], expert_w_down[l])
        h = h + moe.reshape(B, S, D)
    return _rmsnorm(h, final_norm_w)


def setup_inputs(seed=0):
    out = dict(first_inputs(seed))
    for name, value in second_inputs(seed + 1).items():
        if name != "x":
            out[name + "_2"] = value
    return out


def reference(
    x, c, ctx, c_ctx, ada_w, ada_b, ln_g, ln_b, rk_mu, rk_w_rkv, rk_w0, rk_w1, rk_w2, rk_a0,
    rk_a1, rk_a2, rk_g1, rk_g2, rk_k_k, rk_k_a, rk_r_k, rk_lnx_g, rk_lnx_b, rk_w_o, pool_w,
    pool_scale, gdn_w_in, gdn_conv_w, gdn_a_log, gdn_dt_bias, gdn_norm_w, gdn_w_o, ffn_w1,
    ffn_w3, ffn_w2, moe_router_w, moe_router_b, moe_w1, moe_w3, moe_w2, norm1_w_2, w_in_2,
    gla_fwd_gate_w_2, gla_fwd_gate_b_2, gla_bwd_gate_w_2, gla_bwd_gate_b_2, gla_norm_w_2,
    w_out_2, norm2_w_2, router_group_w_2, router_group_b_2, router_expert_w_2,
    router_expert_b_2, expert_w_gate_2, expert_w_up_2, expert_w_down_2, final_norm_w_2,
):
    x = first_block(
        x, c, ctx, c_ctx, ada_w, ada_b, ln_g, ln_b, rk_mu, rk_w_rkv, rk_w0, rk_w1, rk_w2, rk_a0,
        rk_a1, rk_a2, rk_g1, rk_g2, rk_k_k, rk_k_a, rk_r_k, rk_lnx_g, rk_lnx_b, rk_w_o, pool_w,
        pool_scale, gdn_w_in, gdn_conv_w, gdn_a_log, gdn_dt_bias, gdn_norm_w, gdn_w_o, ffn_w1,
        ffn_w3, ffn_w2, moe_router_w, moe_router_b, moe_w1, moe_w3, moe_w2,
    )
    return second_block(
        x, norm1_w_2, w_in_2, gla_fwd_gate_w_2, gla_fwd_gate_b_2, gla_bwd_gate_w_2,
        gla_bwd_gate_b_2, gla_norm_w_2, w_out_2, norm2_w_2, router_group_w_2, router_group_b_2,
        router_expert_w_2, router_expert_b_2, expert_w_gate_2, expert_w_up_2, expert_w_down_2,
        final_norm_w_2,
    )


_drawn_inputs = setup_inputs


def setup_inputs(seed=0):
    import zlib

    import numpy as np

    out = dict(_drawn_inputs(seed))
    spreads = {}
    factors = {'ctx': 2.813,
     'c_ctx': 2.87,
     'rk_lnx_b': 4.004,
     'moe_router_b': 3.148,
     'gla_norm_w_2': 9.849,
     'router_group_b_2': 12.626,
     'router_expert_b_2': 13.763,
     'final_norm_w_2': 8.029,
     'rk_k_k': 3.644,
     'norm2_w_2': 3.794}
    for name, (base, spread) in spreads.items():
        noise = np.random.default_rng([zlib.crc32(name.encode()), seed]).standard_normal(out[name].shape)
        drawn = base * np.exp(spread * noise) if base else spread * noise
        out[name] = jnp.asarray(drawn.astype(out[name].dtype))
    for name, factor in factors.items():
        out[name] = (out[name] * factor).astype(out[name].dtype)
    return out
```

```python
import math
from contextlib import ExitStack

import numpy as np

import concourse.bass as bass
from concourse import mybir

F32 = mybir.dt.float32
I32 = mybir.dt.int32
U32 = mybir.dt.uint32
ALU = mybir.AluOpType
ACT = mybir.ActivationFunctionType
AX = mybir.AxisListType

P = 128
D = 1024
KC = D // P
SEQ = 512
CTX = 256
TOK = CTX + SEQ
NT = SEQ // P
GRID_W = 64
ROWS = SEQ // GRID_W
DEPTH = 2
DN_ALPHA = (2 * DEPTH) ** 0.25
LN_EPS = 1e-5
RMS_EPS = 1e-6

RK_HEAD = 64
RK_LORA = 64
RK_DECAY_SCALE = math.exp(-0.5)
RK_GN_EPS = 64e-5
CHUNK = 64
HG = 4

D_FF = 2816
POOL_WINDOWS = (2, 4, 8, 16)

GLA_HEADS = 4
GLA_DK = 64
GLA_DV = 128
GLA_KEY = GLA_HEADS * GLA_DK
GLA_RANK = 16
GLA_TAU = 16.0
ATT_HEADS = 8
ATT_HEAD = 64
ROT_DIM = ATT_HEAD // 4
ROPE_THETA = 500000.0
DILATED = ((128, 1), (512, 4), (2048, 16))
MASKED = -1e30

SQUARES = ["ident", "ones", "headones", "le", "lt", "ge", "gt", "rope", "earlier", "biasrows"]
SQUARES += [f"off{b}_{d}" for d in range(2) for b in (1, 2, 4, 8, 16, 32)]
SQ = {name: n for n, name in enumerate(SQUARES)}


def square_constants():
    s, t = np.meshgrid(np.arange(P), np.arange(P), indexing="ij")
    same = s // CHUNK == t // CHUNK
    c = {
        "ident": s == t, "ones": s >= 0, "headones": s // 64 == t // 64,
        "le": same & (s <= t), "lt": same & (s < t), "ge": same & (s >= t), "gt": same & (s > t),
        "earlier": s < t, "biasrows": s % 64 == 0,
    }
    half = ROT_DIM // 2
    sm, tm = s % ATT_HEAD, t % ATT_HEAD
    same_head = s // ATT_HEAD == t // ATT_HEAD
    c["rope"] = (same_head & (tm >= half) & (tm < ROT_DIM) & (sm == tm - half)).astype(np.float32) \
        - (same_head & (tm < half) & (sm == tm + half)).astype(np.float32)
    for d in range(2):
        for b in (1, 2, 4, 8, 16, 32):
            pair = (s // (2 * b) == t // (2 * b)) & (s // b != t // b)
            c[f"off{b}_{d}"] = pair & ((s < t) if d == 0 else (s > t))
    return np.concatenate([np.asarray(c[n], np.float32) for n in SQUARES], axis=1)


def rope_tables():
    inv = ROPE_THETA ** (-(np.arange(0, ROT_DIM, 2, dtype=np.float32) / ROT_DIM))
    ang = (np.arange(SEQ, dtype=np.float32)[:, None] * inv[None, :].astype(np.float32)).astype(np.float32)
    cos, sin = np.ones((P, SEQ), np.float32), np.zeros((P, SEQ), np.float32)
    for p in range(P):
        if p % ATT_HEAD < ROT_DIM:
            cos[p] = np.cos(ang[:, p % (ROT_DIM // 2)])
            sin[p] = np.sin(ang[:, p % (ROT_DIM // 2)])
    return np.concatenate([cos, sin], axis=1)


def pattern_logs():
    i, j = np.meshgrid(np.arange(SEQ), np.arange(SEQ), indexing="ij")
    n = sum(((i - j) % d == 0) & (abs(i - j) // d <= w // (2 * d)) for w, d in DILATED)
    logs = np.where(n > 0, np.log(np.maximum(n, 1)), MASKED).astype(np.float32)
    return logs.reshape(NT, P, SEQ).transpose(1, 0, 2).reshape(P, NT * SEQ)


def pool_counts():
    out = []
    for w in POOL_WINDOWS:
        t = np.arange(GRID_W)
        n = np.clip(t + w // 2, 0, GRID_W) - np.clip(t - w // 2, 0, GRID_W)
        out.append(1.0 / n.astype(np.float32))
    return np.tile(np.concatenate(out).astype(np.float32)[None], (P, 1))


VECTORS = {}


def column(name, chunks):
    VECTORS[name] = (sum(n for _, n in VECTORS.values()), chunks)


for _n, _c in [("c", KC), ("c_ctx", KC), ("ada_b0", 6 * KC), ("ada_b1", 6 * KC)] + \
        [(f"ln_{x}{i}{j}", KC) for x in "gb" for i in range(2) for j in range(2)] + \
        [(f"mu{m}", KC) for m in range(6)] + \
        [("a0_0", KC), ("a0_1", KC), ("k_k", KC), ("k_a", KC), ("r_k", KC), ("lnx_g", KC), ("lnx_b", KC),
         ("pool_scale", KC), ("norm1", KC), ("norm2", KC), ("final_norm", KC), ("gla_norm", 1),
         ]:
    column(_n, _c)
NVEC = sum(n for _, n in VECTORS.values())

ROWVECS = {"w0": (0, 2 * D), "gate_b": (2 * D, 2 * GLA_KEY)}
ROWLEN = 2 * D + 2 * GLA_KEY
ROUTER_ROW = {"moe_b": (0, 8), "group_b": (8, 4), "expert_b": (12, 32)}


class Signal:

    HEAD = 128

    def __init__(self, sem, head=HEAD):
        self.sem, self.base = sem, head

    def at(self, n):
        return self.base + n


class Kit:
    pass


def build(nc, t, out):
    with ExitStack() as top:
        k = Kit()
        k.nc, k.t, k.out = nc, t, out

        def sb(name, shape, dt=F32, stack=top):
            return stack.enter_context(nc.sbuf_tensor(name, shape, dt))

        k.sb = sb
        sem = lambda name: Signal(top.enter_context(nc.semaphore(name)))
        dma_sem = lambda name: Signal(top.enter_context(nc.semaphore(name)), 0)
        k.ps = top.enter_context(nc.psum_tensor("ps", [P, 8, 512], F32))
        k.prod_a, k.prod_v, k.free_a, k.free_v = sem("prod_a"), sem("prod_v"), sem("free_a"), sem("free_v")
        k.a_for_t, k.v_for_t, k.a_for_v, k.v_for_a = sem("a_for_t"), sem("v_for_t"), sem("a_for_v"), sem("v_for_a")
        k.v_for_p, k.p_for_t, k.p_for_v = sem("v_for_p"), sem("p_for_t"), sem("p_for_v")
        k.used = sem("used")
        k.prep_t, k.prep_a, k.prep_v = sem("prep_t"), sem("prep_a"), sem("prep_v")
        k.passed, k.sp_passed = sem("passed"), sem("sp_passed")
        k.named = {"prod_a": k.prod_a, "prod_v": k.prod_v, "free_a": k.free_a, "free_v": k.free_v,
                   "a_for_t": k.a_for_t, "v_for_t": k.v_for_t, "p_for_t": k.p_for_t, "a_for_v": k.a_for_v,
                   "p_for_v": k.p_for_v, "v_for_a": k.v_for_a, "v_for_p": k.v_for_p, "used": k.used,
                   "passed": k.passed, "sp_passed": k.sp_passed, "prep_t": k.prep_t, "prep_a": k.prep_a, "prep_v": k.prep_v}
        k.landed = [dma_sem(f"landed{n}") for n in range(6)]
        k.loaded = [dma_sem(f"loaded{n}") for n in range(8)]
        k.gathered = [dma_sem(f"gathered{n}") for n in range(2)]
        k.scattered, k.slots_back = dma_sem("scattered"), dma_sem("slots_back")
        k.stored = [sem(f"stored{n}") for n in range(2)]

        k.sq = sb("sq", [P, len(SQUARES), P])
        k.vec = sb("vec", [P, NVEC])
        k.mod = sb("mod", [P, 2, 6 * KC, 2])
        k.x = sb("x", [P, KC, SEQ])
        k.square = lambda name: k.sq[:, SQ[name], :]
        k.v = lambda name: k.vec[:, VECTORS[name][0]:VECTORS[name][0] + VECTORS[name][1]]
        k.eps = sb("eps", [P, 4])

        def scratch(name, shape, dt=F32):
            return nc.dram_tensor(name, shape, dt, kind="Internal").ap()

        k.r_d, k.k_d, k.kk_d = (scratch(n, [P, KC, TOK]) for n in ("r_d", "k_d", "kk_d"))
        k.v_d = scratch("v_d", [TOK, D])
        k.hid_d = scratch("hid_d", [3, P, TOK])

        stage_load(k)
        stage_modulation(k)
        stage_rwkv_features(k)
        with ExitStack() as s:
            y = sb("y", [P, KC, SEQ], stack=s)
            stage_rwkv_scan(k, y)
            stage_rwkv_out(k, y)
            stage_project_residual(k, t["rk_w_o"], y, k.mod[:, 0, 2 * KC:3 * KC, 0])
        stage_layer_norm(k, 0, 0)
        stage_ffn(k)
        stage_layer_norm(k, 0, 1)
        stage_pool(k)
        stage_layer_norm(k, 1, 0)
        stage_first_moe(k)
        stage_layer_norm(k, 1, 1)
        stage_second_mixer(k)
        stage_second_moe(k)
        stage_output(k)


def chunkwise(vec, tokens):
    return vec.unsqueeze(2).to_broadcast([P, vec.shape[1], tokens])


def stage_load(k):
    with k.nc.Block() as block:
        @block.sync
        def _(sp):
            sp.dma_start(k.sq[:, :, :].rearrange("p a b -> p (a b)"), k.t["squares"]).then_inc(k.loaded[0].sem, 16)
            sp.dma_start(k.vec[:, :], k.t["vectors"]).then_inc(k.loaded[1].sem, 16)
            for s in [*k.named.values(), *k.stored]:
                sp.sem_inc(s.sem, Signal.HEAD)
            for n in range(2):
                sp.wait_ge(k.loaded[n].sem, k.loaded[n].at(16))

        @block.vector
        def _(dve):
            for n, eps in enumerate((RK_GN_EPS, LN_EPS, RMS_EPS, 1.0)):
                dve.memset(k.eps[:, n:n + 1], eps)
    for n in range(2):
        k.loaded[n].base += 16


def stage_modulation(k):
    per_layer = 6 * D // 512
    pieces = DEPTH * per_layer
    ring = 4
    with ExitStack() as s:
        wb = k.sb("wb_ada", [P, ring, KC, 512], stack=s)
        c2 = k.sb("c2", [P, KC, 2], stack=s)
        th = k.sb("th", [P, KC, 2], stack=s)
        rows = k.sb("mod_rows", [2, pieces * 512], stack=s)
        with k.nc.Block() as block:
            @block.sync
            def _(sp):
                src = k.t["ada_w"].rearrange("l (c p) n -> l p c n", p=P)
                for layer in range(DEPTH):
                    with sp.Fori(0, per_layer // ring) as i:
                        for j in range(ring):
                            sp.wait_ge(k.prod_v.sem, i * ring + k.prod_v.at(layer * per_layer + j + 1 - ring))
                            sp.dma_start(wb[:, j, :, :],
                                         src[layer, :, :, bass.ds(i * (512 * ring) + j * 512, 512)]).then_inc(
                                k.landed[j].sem, 16)

            @block.scalar
            def _(act):
                for z, name in enumerate(("c", "c_ctx")):
                    act.activation(th[:, :, z], k.v(name), ACT.Tanh, scale=0.5)
                act.drain().then_inc(k.a_for_v.sem, 1)

            @block.vector
            def _(dve):
                dve.wait_ge(k.a_for_v.sem, k.a_for_v.at(1))
                for z, name in enumerate(("c", "c_ctx")):
                    dve.scalar_tensor_tensor(c2[:, :, z], th[:, :, z], 1.0, k.v(name), ALU.add, ALU.mult)
                dve.drain()
                dve.tensor_scalar(c2[:, :, :], c2[:, :, :], 0.5, None, ALU.mult).then_inc(k.v_for_t.sem, 1)
                with dve.Fori(0, pieces // ring) as i:
                    for j in range(ring):
                        dve.wait_ge(k.prod_v.sem, i * ring + k.prod_v.at(j + 1))
                        dve.tensor_copy(rows[:, bass.ds(i * (512 * ring) + j * 512, 512)], k.ps[0:2, j, :]).then_inc(
                            k.free_v.sem, 1)
                dve.wait_ge(k.prod_v.sem, k.prod_v.at(pieces + 1))
                for layer in range(DEPTH):
                    dve.tensor_tensor(
                        k.mod[:, layer, :, :],
                        k.ps[:, 4, layer * 12 * KC:(layer + 1) * 12 * KC].rearrange("p (o z) -> p o z", z=2),
                        k.v(f"ada_b{layer}").unsqueeze(2).to_broadcast([P, 6 * KC, 2]), ALU.add)
                dve.drain()
                for layer in range(DEPTH):
                    for part in (1, 4):
                        m = k.mod[:, layer, part * KC:(part + 1) * KC, :]
                        dve.tensor_scalar(m, m, 1.0, None, ALU.add)

            @block.tensor
            def _(pe):
                pe.wait_ge(k.v_for_t.sem, k.v_for_t.at(1))
                with pe.Fori(0, pieces // ring) as i:
                    for j in range(ring):
                        pe.wait_ge(k.landed[j].sem, i * 16 + k.landed[j].at(16))
                        pe.wait_ge(k.free_v.sem, i * ring + k.free_v.at(j + 1 - ring))
                        for c in range(KC):
                            mm = pe.matmul(k.ps[0:2, j, :], c2[:, c, :], wb[:, j, c, :], start=c == 0, stop=c == KC - 1)
                        mm.then_inc(k.prod_v.sem, 1)
                pe.wait_ge(k.free_v.sem, k.free_v.at(pieces))
                for o in range(pieces * 4):
                    mm = pe.transpose(k.ps[:, 4, 2 * o:2 * o + 2], rows[:, o * P:(o + 1) * P], k.square("ident")[0:2, 0:2])
                mm.then_inc(k.prod_v.sem, 1)
    k.prod_v.base += pieces + 1
    k.free_v.base += pieces
    k.a_for_v.base += 1
    k.v_for_t.base += 1
    for j in range(ring):
        k.landed[j].base += 16 * pieces // ring


def stage_rwkv_features(k):
    nc, t = k.nc, k.t
    half = TOK // 2
    with ExitStack() as s:
        h = k.sb("h", [P, KC, TOK], stack=s)
        xx = k.sb("xx", [P, KC, TOK], stack=s)
        with nc.Block() as block:
            @block.sync
            def _(sp):
                sp.dma_start(h[:, :, :], t["xT"]).then_inc(k.loaded[0].sem, 16)

            @block.vector
            def _(dve):
                dve.wait_ge(k.loaded[0].sem, k.loaded[0].at(16))
                for z, (lo, hi) in enumerate(((CTX, TOK), (0, CTX))):
                    for c in range(KC):
                        dve.tensor_scalar(h[:, c, lo:hi], h[:, c, lo:hi], k.mod[:, 0, KC + c, z:z + 1],
                                          k.mod[:, 0, c, z:z + 1], ALU.mult, ALU.add)
                dve.drain()

                def minus(dst, shifted, own):
                    if shifted is None:
                        dve.tensor_scalar(dst, own, -1.0, None, ALU.mult)
                    else:
                        dve.tensor_tensor(dst, shifted, own, ALU.subtract)

                a, b = slice(0, KC // 2), slice(KC // 2, KC)
                minus(xx[:, a, 1:CTX], h[:, a, 0:CTX - 1], h[:, a, 1:CTX])
                minus(xx[:, a, 0:1], None, h[:, a, 0:1])
                minus(xx[:, b, 0:CTX - 1], h[:, b, 1:CTX], h[:, b, 0:CTX - 1])
                minus(xx[:, b, CTX - 1:CTX], None, h[:, b, CTX - 1:CTX])
                for c in range(KC):
                    grid = lambda m: m[:, c, CTX:TOK].rearrange("p (r w) -> p r w", w=GRID_W)
                    d, g = grid(xx), grid(h)
                    W, R = GRID_W, ROWS
                    if c < KC // 4:
                        minus(d[:, :, 1:W], g[:, :, 0:W - 1], g[:, :, 1:W])
                        minus(d[:, :, 0:1], None, g[:, :, 0:1])
                    elif c < KC // 2:
                        minus(d[:, :, 0:W - 1], g[:, :, 1:W], g[:, :, 0:W - 1])
                        minus(d[:, :, W - 1:W], None, g[:, :, W - 1:W])
                    elif c < 3 * KC // 4:
                        minus(d[:, 1:R, :], g[:, 0:R - 1, :], g[:, 1:R, :])
                        minus(d[:, 0:1, :], None, g[:, 0:1, :])
                    else:
                        minus(d[:, 0:R - 1, :], g[:, 1:R, :], g[:, 0:R - 1, :])
                        minus(d[:, R - 1:R, :], None, g[:, R - 1:R, :])
        k.loaded[0].base += 16

        mix = k.sb("mix", [P, 2, KC, TOK], stack=s)
        wb = k.sb("wb_rkv", [P, 2, KC, 512], stack=s)
        wl = k.sb("wl", [P, 2, KC, P], stack=s)
        vst = k.sb("rkv_out", [P, 2, D], stack=s)
        st = vst[:, :, 0:TOK]
        RH, WH, KH, VH, AH, GH = range(6)
        order = [RH, KH, VH, WH, AH, GH]
        weight_of = {RH: 0, KH: 1, VH: 2}
        groups = {RH: KC, KH: KC, VH: TOK // P, WH: 1, AH: 1, GH: 1}
        first = {}
        for m in order:
            first[m] = sum(groups[q] for q in order[:order.index(m)])
        total = sum(groups.values())
        hid = {WH: 0, AH: 1, GH: 2}
        with nc.Block() as block:
            @block.sync
            def _(sp):
                n = 0
                for m in (RH, KH, VH):
                    src = t["rk_w_rkv"][0, weight_of[m]].rearrange("(c p) n -> p c n", p=P)
                    for j in range(2):
                        if n >= 2:
                            sp.wait_ge(k.prod_a.sem, k.prod_a.at(first[m]))
                        sp.dma_start(wb[:, j, :, :], src[:, :, j * 512:(j + 1) * 512]).then_inc(k.landed[j].sem, 16)
                        n += 1
                for n, (m, name) in enumerate(((WH, "rk_w1"), (AH, "rk_a1"), (GH, "rk_g1"))):
                    slot = n % 2
                    if n == 2:
                        sp.wait_ge(k.prod_a.sem, k.prod_a.at(first[AH]))
                    if m == GH:
                        sp.dma_start(wl[:, slot, :, :], t[name][0].rearrange("(c p) n -> p c n", p=P)).then_inc(
                            k.landed[2 + n].sem, 16)
                    else:
                        for z in range(2):
                            sp.dma_start(wl[:, slot, :, z * RK_LORA:(z + 1) * RK_LORA],
                                         t[name][0, z].rearrange("(c p) n -> p c n", p=P)).then_inc(
                                k.landed[2 + n].sem, 16)

            @block.vector
            def _(dve):
                for n, m in enumerate(order):
                    if n >= 2:
                        dve.wait_ge(k.prod_a.sem, k.prod_a.at(first[order[n - 1]]))
                    for c in range(KC):
                        ins = dve.scalar_tensor_tensor(mix[:, n % 2, c, :], xx[:, c, :], k.v(f"mu{m}")[:, c:c + 1],
                                                       h[:, c, :], ALU.mult, ALU.add)
                    dve.drain().then_inc(k.v_for_t.sem, 1)

            @block.tensor
            def _(pe):
                for n, m in enumerate(order):
                    pe.wait_ge(k.v_for_t.sem, k.v_for_t.at(n + 1))
                    x = mix[:, n % 2, :, :]
                    if m in weight_of:
                        for j in range(2):
                            pe.wait_ge(k.landed[j].sem, k.landed[j].at(16 * (weight_of[m] + 1)))
                    else:
                        q = 2 + hid[m]
                        pe.wait_ge(k.landed[q].sem, k.landed[q].at(16 if m == GH else 32))
                    for g in range(groups[m]):
                        number = first[m] + g
                        pe.wait_ge(k.free_a.sem, k.free_a.at(number - 3))
                        for part in range(2):
                            bank = number % 4 * 2 + part
                            for c in range(KC):
                                if m == VH:
                                    lhs, rhs = x[:, c, g * P:(g + 1) * P], wb[:, part, c, :]
                                    o = k.ps[:, bank, :]
                                else:
                                    w = wl[:, hid[m] % 2, c, :] if m in hid else wb[:, g // 4, c, g % 4 * P:g % 4 * P + P]
                                    lhs, rhs = w, x[:, c, part * half:(part + 1) * half]
                                    o = k.ps[:, bank, 0:half]
                                mm = pe.matmul(o, lhs, rhs, start=c == 0, stop=c == KC - 1)
                        mm.then_inc(k.prod_a.sem, 1)

            @block.scalar
            def _(act):
                for m in order:
                    for g in range(groups[m]):
                        number = first[m] + g
                        act.wait_ge(k.prod_a.sem, k.prod_a.at(number + 1))
                        if m != VH:
                            banks = k.ps[:, number % 4 * 2:number % 4 * 2 + 2, 0:half]
                            slot = st[:, number % 2, :]
                        else:
                            banks = k.ps[:, number % 4 * 2:number % 4 * 2 + 2, :]
                            slot = vst[:, number % 2, :]
                        if number >= 2:
                            q = k.stored[number % 2]
                            act.wait_ge(q.sem, q.at(16 * (number // 2)))
                        f = {WH: ACT.Tanh, GH: ACT.Tanh}.get(m, ACT.Copy)
                        act.activation(slot.rearrange("p (a b) -> p a b", a=2), banks, f,
                                       scale=0.5 if m == GH else 1.0)
                        act.drain().then_inc(k.free_a.sem, 1)
                        if m == VH:
                            dst = k.v_d[g * P:(g + 1) * P, :]
                        elif m in hid:
                            dst = k.hid_d[hid[m]]
                        else:
                            dst = (k.r_d if m == RH else k.k_d)[:, g, :]
                        act.dma_start(dst, slot).then_inc(k.stored[number % 2].sem, 16)
                for q in range(2):
                    act.wait_ge(k.stored[q].sem, k.stored[q].at(16 * ((total + 1 - q) // 2)))
        k.prod_a.base += total
        k.free_a.base += total
        k.v_for_t.base += len(order)
        for j in range(2):
            k.landed[j].base += 48
            k.landed[2 + j].base += 32
            k.stored[j].base += 16 * ((total + 1 - j) // 2)
        k.landed[4].base += 16

    with ExitStack() as s:
        kk = k.sb("kk", [P, KC, TOK], stack=s)
        sqr = k.sb("kk_sq", [P, KC, TOK], stack=s)
        with nc.Block() as block:
            @block.sync
            def _(sp):
                sp.dma_start(kk[:, :, :], k.k_d).then_inc(k.loaded[0].sem, 16)
                sp.wait_ge(k.v_for_a.sem, k.v_for_a.at(2))
                sp.dma_start(k.kk_d, kk[:, :, :]).then_inc(k.stored[0].sem, 16)
                sp.wait_ge(k.stored[0].sem, k.stored[0].at(16))

            @block.vector
            def _(dve):
                dve.wait_ge(k.loaded[0].sem, k.loaded[0].at(16))
                dve.tensor_tensor(kk[:, :, :], kk[:, :, :], chunkwise(k.v("k_k"), TOK), ALU.mult)
                dve.drain().then_inc(k.v_for_a.sem, 1)
                for c in range(KC):
                    dve.wait_ge(k.a_for_v.sem, k.a_for_v.at(c + 1))
                    dve.tensor_scalar(sqr[:, c, :], sqr[:, c, :], 1e-12, None, ALU.max)
                    dve.drain()
                    dve.reciprocal(sqr[:, c, :], sqr[:, c, :])
                    dve.drain()
                    dve.tensor_tensor(kk[:, c, :], kk[:, c, :], sqr[:, c, :], ALU.mult)
                dve.drain().then_inc(k.v_for_a.sem, 1)

            @block.scalar
            def _(act):
                act.wait_ge(k.v_for_a.sem, k.v_for_a.at(1))
                act.activation(sqr[:, :, :], kk[:, :, :], ACT.Square)
                act.drain().then_inc(k.a_for_t.sem, 1)
                for c in range(KC):
                    act.wait_ge(k.prod_a.sem, k.prod_a.at(c + 1))
                    act.activation(sqr[:, c, :].rearrange("p (a b) -> p a b", a=2),
                                   k.ps[:, c % 4 * 2:c % 4 * 2 + 2, 0:half], ACT.Sqrt)
                    act.drain().then_inc(k.a_for_v.sem, 1)

            @block.tensor
            def _(pe):
                pe.wait_ge(k.a_for_t.sem, k.a_for_t.at(1))
                for c in range(KC):
                    pe.wait_ge(k.a_for_v.sem, k.a_for_v.at(c - 3))
                    for part in range(2):
                        mm = pe.matmul(k.ps[:, c % 4 * 2 + part, 0:half], k.square("headones"),
                                       sqr[:, c, part * half:(part + 1) * half], start=True, stop=True)
                    mm.then_inc(k.prod_a.sem, 1)
    k.loaded[0].base += 16
    k.stored[0].base += 16
    k.v_for_a.base += 2
    k.a_for_t.base += 1
    k.a_for_v.base += KC
    k.prod_a.base += KC


def stage_rwkv_scan(k, y):
    nc, t = k.nc, k.t
    HP = D // P
    NG = 2 * HP // HG
    LEVELS = (2, 4, 8, 16, 32)
    BEFORE = {0: ("le", "lt"), 1: ("ge", "gt")}
    with ExitStack() as s:
        def sb(name, shape):
            return k.sb(name, shape, stack=s)

        w2, a2, w0 = sb("w2", [P, D]), sb("a2", [P, D]), sb("w0", [P, D])
        a0h, kah, kar = sb("a0h", [P, 2, KC]), sb("kah", [P, KC]), sb("kar", [P, KC])
        rkk = sb("rkk", [P, 3, KC, P])
        V = sb("V", [P, 2, D])
        hid = sb("hid", [P, 2, 2, P])
        lw = sb("lw", [P, D])
        spare = [k.x[:, 2 * n:2 * n + 2, :].rearrange("p a (c n) -> p (a c) n", n=P) for n in range(4)]
        rate, e_ex, e_in, e_inv = ([sb(name, [P, KC, P])[:, :, :], spare[n]]
                                   for n, name in enumerate(("rate", "e_ex", "e_in", "e_inv")))
        tmp = sb("tmp", [P, KC, P])
        pend = sb("pend", [P, 2, KC, 2])
        tok = sb("tok", [P, 3, D])
        AT, BT, QT, GT, T, TT, X = (sb(n, [P, 2 * HP, P]) for n in ("AT", "BT", "QT", "GT", "T", "TT", "X"))
        bv, ub, tkt = sb("bv", [P, D]), sb("ub", [P, D]), sb("tkt", [P, HP, P])
        N = sb("N", [P, 2, 3, HP * 64])
        kappa, rr, beta, kt = e_ex, e_in, rate, e_inv

        with nc.Block() as block:
            @block.sync
            def _(sp):
                sp.dma_start(w2[:, :], t["rk_w2"][0].rearrange("z r d -> (z r) d")).then_inc(k.loaded[0].sem, 16)
                sp.dma_start(a2[:, :], t["rk_a2"][0].rearrange("z r d -> (z r) d")).then_inc(k.loaded[1].sem, 16)
                sp.wait_ge(k.v_for_t.sem, k.v_for_t.at(1))
                for z in range(2):
                    sp.dma_start(w0[z * 64:z * 64 + 1, :], t["rows"][0:1, z * D:(z + 1) * D]).then_inc(
                        k.loaded[2].sem, 16)
                for n in range(3):
                    sp.wait_ge(k.loaded[n].sem, k.loaded[n].at(16 if n < 2 else 32))

            @block.vector
            def _(dve):
                dve.memset(w0[:, :], 0.0).then_inc(k.v_for_t.sem, 1)
                dve.memset(N[:, :, :, :], 0.0)
                dve.memset(y[:, :, :], 0.0)
                for d in range(2):
                    dve.tensor_scalar(a0h[:, d, :], k.v(f"a0_{d}"), 0.5, None, ALU.mult)
                dve.tensor_scalar(kah[:, :], k.v("k_a"), 0.5, None, ALU.mult)
                dve.tensor_scalar(kar[:, :], k.v("k_a"), -0.5, 1.0, ALU.mult, ALU.add)
        for n in range(3):
            k.loaded[n].base += 16 if n < 2 else 32
        k.v_for_t.base += 1

        PREP = {"prep_t": 2, "prep_a": 3, "prep_v": 3}

        def first_row(i, d, tok0, count):
            return i * (P if d == 0 else -P) + (tok0 if d == 0 else tok0 + (count - 1) * P)

        def two(m):
            return m.rearrange("p (a c) n -> p a (c n)", a=2)

        def load_tile(sp, d, at0, w):
            sp.wait_ge(k.prep_v.sem, w("prep_v", 0))
            sp.sem_inc(k.sp_passed.sem, 1)
            for n, src in enumerate((k.r_d, k.k_d, k.kk_d)):
                sp.dma_start(rkk[:, n, :, :], src[:, :, bass.ds(at0, P)]).then_inc(k.loaded[n].sem, 16)
            sp.dma_start(V[:, d, :], k.v_d[bass.ds(at0, P), :]).then_inc(k.loaded[3 + d].sem, 16)
            sp.dma_start(hid[:, d, :, :], k.hid_d[0:2, :, bass.ds(at0, P)].rearrange("a p n -> p a n")).then_inc(
                k.loaded[5 + d].sem, 16)

        def prep_lora(pe, d, turn):
            lora = slice(d * RK_LORA, (d + 1) * RK_LORA)
            pe.wait_ge(k.loaded[5 + d].sem, turn * 16 + k.loaded[5 + d].at(16))
            for j in range(2):
                cols = slice(j * 512, (j + 1) * 512)
                pe.matmul(k.ps[:, 4 + j, :], hid[lora, d, 0, :], w2[lora, cols], start=True, stop=False)
                pe.matmul(k.ps[:, 4 + j, :], k.square("biasrows")[lora, :], w0[lora, cols], start=False, stop=True)
            for c in range(KC):
                mm = pe.matmul(k.ps[:, 6 + c // 4, c % 4 * P:c % 4 * P + P], a2[lora, c * P:(c + 1) * P],
                               hid[lora, d, 1, :], start=True, stop=True)
            mm.then_inc(k.prep_t.sem, 1)

        def prep_sums(pe, d, w):
            pe.wait_ge(k.prep_v.sem, w("prep_v", 1))
            pe.wait_ge(k.prep_a.sem, w("prep_a", 2))
            for q, mask in zip((4, 6), BEFORE[d]):
                for c in range(KC):
                    mm = pe.matmul(k.ps[:, q + c // 4, c % 4 * P:c % 4 * P + P], lw[:, c * P:(c + 1) * P],
                                   k.square(mask), start=True, stop=True)
            mm.then_inc(k.prep_t.sem, 1)

        def prep_tanh(act, d, w):
            act.wait_ge(k.prep_t.sem, w("prep_t", 1))
            act.activation(lw[:, :].rearrange("p (a b) -> p a b", a=2), k.ps[:, 4:6, :], ACT.Tanh, scale=0.5).then_inc(
                k.prep_a.sem, 1)
            for c in range(KC):
                act.activation(rate[d][:, c, :], k.ps[:, 6 + c // 4, c % 4 * P:c % 4 * P + P], ACT.Tanh,
                               bias=a0h[:, d, c:c + 1], scale=0.5)
            act.drain().then_inc(k.prep_a.sem, 1)

        def prep_exp(act, d, w):
            act.wait_ge(k.prep_t.sem, w("prep_t", 2))
            act.activation(two(e_in[d]), k.ps[:, 4:6, :], ACT.Exp)
            act.activation(two(e_ex[d]), k.ps[:, 6:8, :], ACT.Exp)
            act.activation(two(e_inv[d]), k.ps[:, 4:6, :], ACT.Exp, scale=-1.0)
            act.drain().then_inc(k.prep_a.sem, 1)

        def prep_decay(dve, w):
            dve.wait_ge(k.prep_a.sem, w("prep_a", 1))
            dve.tensor_scalar(lw[:, :], lw[:, :], -0.5 * RK_DECAY_SCALE, -0.5 * RK_DECAY_SCALE,
                              ALU.mult, ALU.add).then_inc(k.prep_v.sem, 1)

        def prep_rates(dve, d, item, w):
            for n in range(3):
                dve.wait_ge(k.loaded[n].sem, item * 16 + k.loaded[n].at(16))
            dve.wait_ge(k.prep_a.sem, w("prep_a", 2))
            kf, kk = rkk[:, 1, :, :], rkk[:, 2, :, :]
            dve.tensor_tensor(tmp[:, :, :], rate[d], chunkwise(kah[:, :], P), ALU.mult)
            dve.drain()
            dve.tensor_tensor(tmp[:, :, :], tmp[:, :, :], chunkwise(kar[:, :], P), ALU.add)
            dve.scalar_tensor_tensor(rate[d], rate[d], 1.0, kk, ALU.add, ALU.mult)
            dve.drain()
            dve.tensor_tensor(tmp[:, :, :], tmp[:, :, :], kf, ALU.mult)
            dve.drain().then_inc(k.prep_v.sem, 1)

        def prep_features(dve, d, w):
            dve.wait_ge(k.prep_a.sem, w("prep_a", 3))
            ends = (63, 127) if d == 0 else (0, 64)
            for c in range(2):
                dve.tensor_copy(pend[:, d, :, c:c + 1], e_in[d][:, :, ends[c]:ends[c] + 1])
            dve.tensor_tensor(kappa[d], e_ex[d], rkk[:, 2, :, :], ALU.mult)
            dve.scalar_tensor_tensor(beta[d], rate[d], 0.5, e_inv[d], ALU.mult, ALU.mult)
            dve.drain()
            dve.tensor_tensor(rr[d], e_in[d], rkk[:, 0, :, :], ALU.mult)
            dve.tensor_tensor(kt[d], e_inv[d], tmp[:, :, :], ALU.mult)
            dve.drain().then_inc(k.prep_v.sem, 1)

        w_first = lambda name, n: k.named[name].at(n)
        with nc.Block() as block:
            @block.sync
            def _(sp):
                load_tile(sp, 0, 0, w_first)

            @block.tensor
            def _(pe):
                prep_lora(pe, 0, 0)
                prep_sums(pe, 0, w_first)

            @block.scalar
            def _(act):
                prep_tanh(act, 0, w_first)
                prep_exp(act, 0, w_first)

            @block.vector
            def _(dve):
                prep_decay(dve, w_first)
                prep_rates(dve, 0, 0, w_first)
                prep_features(dve, 0, w_first)

        def tiles(tok0, count, want_y, final):
            kinds = 4 if want_y else 2
            NB = NG * kinds
            NL = 2 * len(LEVELS) * NG
            LA = NG
            cnt = {
                "prod_a": 1 + LA + 2, "a_for_t": 1 + LA + 2, "v_for_p": NG, "p_for_t": NG,
                "prod_v": NB + NL + 1 + 4 + want_y, "v_for_t": NB + NL + 1 + 4 + want_y,
            }

            def program(engine, body):
                def turn(i, last):
                    for d in range(2):
                        v = lambda name, n: i * (2 * cnt[name]) + k.named[name].at(d * cnt[name] + n)
                        w = lambda name, n: i * (2 * PREP[name]) + k.named[name].at((d + 1) * PREP[name] + n)
                        nxt = None
                        if not (last and d == 1):
                            nxt = (1 - d, first_row(i + d, 1 - d, tok0, count), i + d, i * 2 + (d + 1), w)
                        body(i, d, v, nxt)
                loops = count - 1 if final else count
                with engine.Fori(0, loops) as i:
                    turn(i, False)
                if final:
                    turn(loops, True)

            def heads(g):
                return [2 * (g // 2 * HG + q) + g % 2 for q in range(HG)]

            def slot(h):
                return (h // 2 // HG * 2 + h % 2) * HG + h // 2 % HG

            def half(h):
                return slice(h % 2 * 64, h % 2 * 64 + 64)

            def early(m, b, d):
                return m.rearrange("p (n s b) -> p n s b", s=2, b=b)[:, :, d, :]

            def late(m, b, d):
                return early(m, b, 1 - d)

            with nc.Block() as block:
                @block.sync
                def _(sp):
                    def body(i, d, v, nxt):
                        if nxt:
                            d2, at0, _, _, w = nxt
                            sp.wait_ge(k.v_for_t.sem, v("v_for_t", 0))
                            sp.sem_inc(k.sp_passed.sem, 1)
                            load_tile(sp, d2, at0, w)
                    program(sp, body)

                @block.tensor
                def _(pe):
                    def body(i, d, v, nxt):
                        prepared = i * (2 * PREP["prep_v"]) + k.prep_v.at((d + 1) * PREP["prep_v"])
                        pe.wait_ge(k.prep_v.sem, prepared)
                        pe.wait_ge(k.v_for_t.sem, v("v_for_t", 0))
                        for n, m in enumerate((beta[d], kt[d], kappa[d])):
                            for c in range(KC):
                                mm = pe.transpose(k.ps[:, 2 * n + c // 4, c % 4 * P:c % 4 * P + P], m[:, c, :],
                                                  k.square("ident"))
                        mm.then_inc(k.prod_a.sem, 1)
                        n = 0
                        for g in range(NG):
                            pairs = [(beta[d], kappa[d]), (kt[d], kappa[d]), (beta[d], rr[d]), (kt[d], rr[d])][:kinds]
                            for left, right in pairs:
                                bank = (6 + n) % 8
                                if n == 2:
                                    pe.wait_ge(k.a_for_t.sem, v("a_for_t", 1))
                                if n >= 8:
                                    pe.wait_ge(k.v_for_t.sem, v("v_for_t", n - 7))
                                for q, h in enumerate(heads(g)):
                                    mm = pe.matmul(k.ps[:, bank, q * P:(q + 1) * P], left[half(h), h // 2, :],
                                                   right[half(h), h // 2, :], start=True, stop=True)
                                mm.then_inc(k.prod_v.sem, 1)
                                n += 1

                        pe.wait_ge(k.v_for_t.sem, v("v_for_t", NB))
                        for g in range(NG):
                            pe.wait_ge(k.p_for_t.sem, v("p_for_t", g + 1))
                            for q, h in enumerate(heads(g)):
                                mm = pe.transpose(k.ps[:, g, q * P:(q + 1) * P], TT[:, slot(h), :], k.square("ident"))
                            mm.then_inc(k.prod_a.sem, 1)
                        for l, b in enumerate(LEVELS):
                            l0 = NB + 2 * NG * l
                            for g in range(NG):
                                if l == 0:
                                    pe.wait_ge(k.a_for_t.sem, v("a_for_t", 1 + g + 1))
                                else:
                                    pe.wait_ge(k.v_for_t.sem, v("v_for_t", l0 - NG + g + 1))
                                for q, h in enumerate(heads(g)):
                                    mm = pe.matmul(k.ps[:, g, q * P:(q + 1) * P], AT[:, slot(h), :], T[:, slot(h), :],
                                                   start=True, stop=True)
                                mm.then_inc(k.prod_v.sem, 1)
                            for g in range(NG):
                                pe.wait_ge(k.v_for_t.sem, v("v_for_t", l0 + g + 1))
                                for q, h in enumerate(heads(g)):
                                    if b != LEVELS[-1]:
                                        pe.matmul(k.ps[:, g, q * 64:(q + 1) * 64], TT[:, slot(h), :],
                                                  early(X[:, slot(h), :], b, d), start=True, stop=True)
                                    mm = pe.matmul(k.ps[:, g, 256 + q * 64:256 + (q + 1) * 64], X[:, slot(h), :],
                                                   late(TT[:, slot(h), :], b, d), start=True, stop=True)
                                mm.then_inc(k.prod_v.sem, 1)
                            if nxt and l == 0:
                                prep_lora(pe, nxt[0], nxt[2])
                            if nxt and l == 2:
                                prep_sums(pe, nxt[0], nxt[4])
                        done = NB + NL
                        pe.wait_ge(k.loaded[3 + d].sem, i * 16 + k.loaded[3 + d].at(16))
                        pe.wait_ge(k.v_for_t.sem, v("v_for_t", done))
                        for h in range(2 * HP):
                            mm = pe.matmul(k.ps[:, h // 8, h % 8 * 64:h % 8 * 64 + 64], BT[:, slot(h), :],
                                           V[:, d, h * 64:(h + 1) * 64], start=True, stop=True)
                        mm.then_inc(k.prod_a.sem, 1)
                        for h in range(2 * HP):
                            c = h // 2
                            mm = pe.matmul(k.ps[half(h), 2 + c // 4, c % 4 * P:c % 4 * P + P],
                                           tok[:, 2, h * 64:(h + 1) * 64], TT[:, slot(h), :], start=True, stop=True)
                        mm.then_inc(k.prod_a.sem, 1)
                        pe.wait_ge(k.a_for_t.sem, v("a_for_t", 1 + LA + 1))
                        if nxt:
                            pe.wait_ge(k.prep_a.sem, nxt[4]("prep_a", 3))
                        for h in range(2 * HP):
                            mm = pe.matmul(k.ps[:, 4 + h // 8, h % 8 * 64:h % 8 * 64 + 64], TT[:, slot(h), :],
                                           bv[:, h * 64:(h + 1) * 64], start=True, stop=True)
                        mm.then_inc(k.prod_v.sem, 1)

                        chunk = lambda step: step if d == 0 else 1 - step
                        of_chunk = lambda step: slice(chunk(step) * 64, chunk(step) * 64 + 64)

                        def from_state(step):
                            for h in range(2 * HP):
                                mm = pe.matmul(k.ps[of_chunk(step), 6 + h % 2, h // 2 * 64:h // 2 * 64 + 64],
                                               tkt[half(h), h // 2, of_chunk(step)],
                                               N[half(h), d, step, h // 2 * 64:h // 2 * 64 + 64], start=True, stop=True)
                            mm.then_inc(k.prod_v.sem, 1)

                        def old(bank, m):
                            pe.matmul(k.ps[:, bank, :], k.square("ident"), m, start=True, stop=False)

                        def to_state(step, m, part):
                            r = of_chunk(step)
                            for h in range(2 * HP):
                                cols = slice(h * 64, (h + 1) * 64)
                                mm = pe.matmul(k.ps[half(h), step, h // 2 * 64:h // 2 * 64 + 64], tok[r, part, cols],
                                               m[r, cols], start=False, stop=part == 0 and h >= 2 * HP - 2)
                            return mm

                        def output_of(h):
                            return k.ps[half(h), 2 + h // 2 // 4, h // 2 % 4 * P:h // 2 % 4 * P + P]

                        pe.wait_ge(k.a_for_t.sem, v("a_for_t", 1 + LA + 2))
                        for step in range(2):
                            if step:
                                pe.wait_ge(k.v_for_t.sem, v("v_for_t", done + 3))
                            pe.sem_inc(k.passed.sem, 1)
                            from_state(step)
                            old(step, N[:, d, step, :])
                            to_state(step, V[:, d, :], 1)
                            pe.wait_ge(k.v_for_t.sem, v("v_for_t", done + 2 + 2 * step))
                            pe.sem_inc(k.passed.sem, 1)
                            to_state(step, ub, 0).then_inc(k.prod_v.sem, 1)
                            if want_y and step == 0:
                                for b in range(2):
                                    old(2 + b, y[:, 4 * b:4 * b + 4, bass.ds(first_row(i, d, tok0 - CTX, count), P)])
                        if want_y:
                            for h in range(2 * HP):
                                o = output_of(h)
                                pe.matmul(o, V[:, d, h * 64:(h + 1) * 64], GT[:, slot(h), :], start=False, stop=False)
                                pe.matmul(o, ub[:, h * 64:(h + 1) * 64], QT[:, slot(h), :], start=False, stop=False)
                                for step in range(2):
                                    mm = pe.matmul(o[:, of_chunk(step)], N[half(h), d, step, h // 2 * 64:h // 2 * 64 + 64],
                                                   rr[d][half(h), h // 2, of_chunk(step)], start=False,
                                                   stop=step == 1 and h % 8 >= 6)
                            mm.then_inc(k.prod_v.sem, 1)
                    program(pe, body)

                @block.scalar
                def _(act):
                    def body(i, d, v, nxt):
                        e = 0

                        def taken(dst, src, f=ACT.Copy, scale=1.0):
                            nonlocal e
                            act.wait_ge(k.prod_a.sem, v("prod_a", e + 1))
                            act.activation(dst, src, f, scale=scale).then_inc(k.a_for_t.sem, 1)
                            e += 1

                        act.wait_ge(k.prod_a.sem, v("prod_a", 1))
                        for n in range(3):
                            act.activation(tok[:, n, :].rearrange("p (a b) -> p a b", a=2), k.ps[:, 2 * n:2 * n + 2, :],
                                           ACT.Copy, scale=-1.0 if n == 0 else 1.0)
                        act.drain().then_inc(k.a_for_t.sem, 1)
                        e = 1
                        bank = lambda g: k.ps[:, g, :].rearrange("p (a b) -> p a b", a=HG)
                        for g in range(NG):
                            taken(T[:, g * HG:(g + 1) * HG, :], bank(g))
                        if nxt:
                            prep_tanh(act, nxt[0], nxt[4])
                            prep_exp(act, nxt[0], nxt[4])
                        taken(bv[:, :].rearrange("p (a b) -> p a b", a=2), k.ps[:, 0:2, :])
                        taken(two(tkt[:, :, :]), k.ps[:, 2:4, :])
                    program(act, body)

                @block.gpsimd
                def _(pool):
                    def body(i, d, v, nxt):
                        for g in range(NG):
                            four = slice(g * HG, (g + 1) * HG)
                            pool.wait_ge(k.v_for_p.sem, v("v_for_p", g + 1))
                            pool.tensor_tensor(TT[:, four, :], AT[:, four, :],
                                               k.square(f"off1_{d}").unsqueeze(1).to_broadcast([P, HG, P]), ALU.mult)
                            pool.drain()
                            pool.tensor_tensor(TT[:, four, :], k.square("ident").unsqueeze(1).to_broadcast([P, HG, P]),
                                               TT[:, four, :], ALU.subtract).then_inc(k.p_for_t.sem, 1)
                    program(pool, body)

                @block.vector
                def _(dve):
                    def body(i, d, v, nxt):
                        incl, strict = BEFORE[d]
                        four = lambda m, g: m[:, g * HG:(g + 1) * HG, :]
                        wide = lambda name: k.square(name).unsqueeze(1).to_broadcast([P, HG, P])
                        bank4 = lambda b: k.ps[:, b, :].rearrange("p (a b) -> p a b", a=HG)
                        dve.tensor_copy(N[:, d, 0, :], N[:, d, 2, :])
                        n = 0
                        for g in range(NG):
                            for kind in range(kinds):
                                bank = bank4((6 + n) % 8)
                                dve.wait_ge(k.prod_v.sem, v("prod_v", n + 1))
                                if kind == 0:
                                    dve.tensor_tensor(four(AT, g), bank, wide(strict), ALU.mult)
                                    dve.drain().then_inc(k.v_for_p.sem, 1)
                                elif kind == 1:
                                    dve.tensor_tensor(four(BT, g), bank, wide(strict), ALU.mult)
                                elif kind == 2:
                                    dve.scalar_tensor_tensor(four(QT, g), bank, -1.0, wide(incl), ALU.mult, ALU.mult)
                                else:
                                    dve.tensor_tensor(four(GT, g), bank, wide(incl), ALU.mult)
                                dve.drain().then_inc(k.v_for_t.sem, 1)
                                n += 1
                        for l, b in enumerate(LEVELS):
                            l0 = NB + 2 * NG * l
                            for g in range(NG):
                                dve.wait_ge(k.prod_v.sem, v("prod_v", l0 + g + 1))
                                dve.tensor_tensor(four(X, g), bank4(g), wide(f"off{b}_{1 - d}"), ALU.mult).then_inc(
                                    k.v_for_t.sem, 1)
                            for g in range(NG):
                                dve.wait_ge(k.prod_v.sem, v("prod_v", l0 + NG + g + 1))
                                for m, side, at0 in ((T, d, 0), (TT, 1 - d, 256)):
                                    if m is T and b == LEVELS[-1]:
                                        continue
                                    cols = four(m, g).rearrange("p h (n s b) -> p h n s b", s=2, b=b)[:, :, :, side, :]
                                    change = k.ps[:, g, at0:at0 + 256].rearrange("p (h n b) -> p h n b", h=HG, b=b)
                                    ins = dve.tensor_tensor(cols, cols, change, ALU.subtract)
                                ins.then_inc(k.v_for_t.sem, 1)
                            if nxt and l == 1:
                                prep_decay(dve, nxt[4])
                            if nxt and l == 2:
                                prep_rates(dve, nxt[0], nxt[3], nxt[4])
                        e = NB + NL
                        if nxt:
                            prep_features(dve, nxt[0], nxt[4])
                        dve.wait_ge(k.prod_v.sem, v("prod_v", e + 1))
                        dve.tensor_copy(ub[:, :].rearrange("p (a b) -> p a b", a=2), k.ps[:, 4:6, :])
                        dve.drain().then_inc(k.v_for_t.sem, 1)
                        for step in range(2):
                            c = step if d == 0 else 1 - step
                            rows = slice(c * 64, c * 64 + 64)
                            dve.wait_ge(k.prod_v.sem, v("prod_v", e + 2 + 2 * step))
                            u = ub[rows, :].rearrange("p (c a b) -> p a c b", a=2, b=64)
                            dve.tensor_tensor(u, u, k.ps[rows, 6:8, :].rearrange("p a (c b) -> p a c b", b=64), ALU.add)
                            dve.drain().then_inc(k.v_for_t.sem, 1)
                            dve.wait_ge(k.prod_v.sem, v("prod_v", e + 3 + 2 * step))
                            dve.tensor_tensor(N[:, d, step + 1, :].rearrange("p (a b) -> p a b", a=HP),
                                              k.ps[:, step, :].rearrange("p (a b) -> p a b", a=HP),
                                              pend[:, d, :, c:c + 1].to_broadcast([P, HP, 64]), ALU.mult)
                            dve.drain().then_inc(k.v_for_t.sem, 1)
                        if want_y:
                            dve.wait_ge(k.prod_v.sem, v("prod_v", cnt["prod_v"]))
                            yt = y[:, :, bass.ds(first_row(i, d, tok0 - CTX, count), P)]
                            dve.tensor_copy(yt, k.ps[:, 2:4, :].rearrange("p a (c n) -> p (a c) n", n=P))
                            dve.drain().then_inc(k.v_for_t.sem, 1)
                    program(dve, body)
            for name, n in cnt.items():
                k.named[name].base += 2 * count * n
            for name, n in PREP.items():
                k.named[name].base += 2 * count * n
            for n in range(3):
                k.loaded[n].base += 32 * count
            for n in range(3, 7):
                k.loaded[n].base += 16 * count

        tiles(0, CTX // P, False, False)
        tiles(CTX, NT, True, True)


def stage_rwkv_out(k, y):
    nc, t = k.nc, k.t
    with ExitStack() as s:
        def sb(name, shape):
            return k.sb(name, shape, stack=s)

        r, kf, v = sb("o_r", [P, KC, SEQ]), sb("o_k", [P, KC, SEQ]), sb("o_v", [P, NT, D])
        a2, g2, hid = sb("o_a2", [P, D]), sb("o_g2", [P, D]), sb("o_hid", [P, 2, SEQ])
        a0h, kah, kar = sb("o_a0h", [P, 2, KC]), sb("o_kah", [P, KC]), sb("o_kar", [P, KC])
        rate = sb("o_rate", [P, 2, 2, SEQ])
        vt, cen, sqr, rstd = (sb(n, [P, 2, SEQ]) for n in ("o_vt", "o_cen", "o_sqr", "o_rstd"))
        lat = slice(CTX, TOK)
        with nc.Block() as block:
            @block.sync
            def _(sp):
                sp.dma_start(k.x[:, :, :], t["xT"][:, :, lat]).then_inc(k.loaded[6].sem, 16)
                sp.dma_start(r[:, :, :], k.r_d[:, :, lat]).then_inc(k.loaded[0].sem, 16)
                sp.dma_start(kf[:, :, :], k.k_d[:, :, lat]).then_inc(k.loaded[1].sem, 16)
                sp.dma_start(v[:, :, :], k.v_d[lat, :].rearrange("(t p) d -> p t d", p=P)).then_inc(k.loaded[2].sem, 16)
                sp.dma_start(a2[:, :], t["rk_a2"][0].rearrange("z r d -> (z r) d")).then_inc(k.loaded[3].sem, 16)
                sp.dma_start(g2[:, :], t["rk_g2"][0]).then_inc(k.loaded[4].sem, 16)
                sp.dma_start(hid[:, :, :], k.hid_d[1:3, :, lat].rearrange("a p n -> p a n")).then_inc(
                    k.loaded[5].sem, 16)
                sp.wait_ge(k.loaded[6].sem, k.loaded[6].at(16))

            @block.vector
            def _(dve):
                for d in range(2):
                    dve.tensor_scalar(a0h[:, d, :], k.v(f"a0_{d}"), 0.5, None, ALU.mult)
                dve.tensor_scalar(kah[:, :], k.v("k_a"), 0.5, None, ALU.mult)
                dve.tensor_scalar(kar[:, :], k.v("k_a"), -1.0, 2.0, ALU.mult, ALU.add)
                dve.wait_ge(k.loaded[5].sem, k.loaded[5].at(16))
                dve.tensor_scalar(hid[:, 1, :], hid[:, 1, :], 0.5, 0.5, ALU.mult, ALU.add)
                dve.drain().then_inc(k.v_for_t.sem, 1)
                for n in (0, 1):
                    dve.wait_ge(k.loaded[n].sem, k.loaded[n].at(16))
                for c in range(KC):
                    j = c % 2
                    e = 4 * c
                    dve.wait_ge(k.a_for_v.sem, k.a_for_v.at(3 * c + 1))
                    dve.tensor_tensor(rate[:, j, 0, :], rate[:, j, 0, :], rate[:, j, 1, :], ALU.add)
                    dve.tensor_tensor(r[:, c, :], r[:, c, :], kf[:, c, :], ALU.mult)
                    dve.drain()
                    dve.tensor_scalar(rate[:, j, 0, :], rate[:, j, 0, :], kah[:, c:c + 1], kar[:, c:c + 1],
                                      ALU.mult, ALU.add)
                    dve.tensor_scalar(r[:, c, :], r[:, c, :], k.v("r_k")[:, c:c + 1], None, ALU.mult)
                    dve.drain()
                    dve.tensor_tensor(r[:, c, :], r[:, c, :], rate[:, j, 0, :], ALU.mult)
                    dve.wait_ge(k.prod_v.sem, k.prod_v.at(3 * c + 1))
                    dve.scalar_tensor_tensor(cen[:, j, :], k.ps[:, 0, :], -1.0 / RK_HEAD, y[:, c, :], ALU.mult, ALU.add)
                    dve.drain().then_inc(k.v_for_t.sem, 1)
                    dve.wait_ge(k.a_for_v.sem, k.a_for_v.at(3 * c + 2))
                    dve.reciprocal(rstd[:, j, :], rstd[:, j, :])
                    dve.drain()
                    dve.tensor_tensor(cen[:, j, :], cen[:, j, :], rstd[:, j, :], ALU.mult)
                    dve.drain()
                    dve.tensor_scalar(cen[:, j, :], cen[:, j, :], k.v("lnx_g")[:, c:c + 1], k.v("lnx_b")[:, c:c + 1],
                                      ALU.mult, ALU.add)
                    dve.wait_ge(k.prod_v.sem, k.prod_v.at(3 * c + 2))
                    dve.wait_ge(k.a_for_v.sem, k.a_for_v.at(3 * c + 3))
                    dve.tensor_tensor(vt[:, j, :], vt[:, j, :], k.ps[:, 2, :], ALU.mult)
                    dve.drain()
                    dve.tensor_tensor(cen[:, j, :], cen[:, j, :], vt[:, j, :], ALU.add)
                    dve.drain()
                    dve.wait_ge(k.prod_v.sem, k.prod_v.at(3 * c + 3))
                    dve.tensor_tensor(y[:, c, :], cen[:, j, :], k.ps[:, 3, :], ALU.mult)
                    dve.drain().then_inc(k.v_for_t.sem, 1)

            @block.scalar
            def _(act):
                for c in range(KC):
                    j = c % 2
                    act.wait_ge(k.prod_a.sem, k.prod_a.at(3 * c + 1))
                    if c >= 2:
                        act.wait_ge(k.v_for_t.sem, k.v_for_t.at(1 + 2 * (c - 1)))
                    for d in range(2):
                        act.activation(rate[:, j, d, :], k.ps[:, 4 + d, :], ACT.Tanh, bias=a0h[:, d, c:c + 1], scale=0.5)
                    act.drain().then_inc(k.a_for_v.sem, 1)
                    act.wait_ge(k.v_for_t.sem, k.v_for_t.at(1 + 2 * c + 1))
                    act.activation(sqr[:, j, :], cen[:, j, :], ACT.Square)
                    act.drain().then_inc(k.a_for_t.sem, 1)
                    act.wait_ge(k.prod_a.sem, k.prod_a.at(3 * c + 2))
                    act.activation(rstd[:, j, :], k.ps[:, 1, :], ACT.Sqrt, scale=1.0 / RK_HEAD, bias=k.eps[:, 0:1])
                    act.drain().then_inc(k.a_for_v.sem, 1)
                    act.wait_ge(k.prod_a.sem, k.prod_a.at(3 * c + 3))
                    act.activation(vt[:, j, :], k.ps[:, 6, :], ACT.Copy)
                    act.drain().then_inc(k.a_for_v.sem, 1)

            @block.tensor
            def _(pe):
                pe.wait_ge(k.v_for_t.sem, k.v_for_t.at(1))
                for n in (2, 3, 4):
                    pe.wait_ge(k.loaded[n].sem, k.loaded[n].at(16))
                for c in range(KC):
                    j = c % 2
                    cols = slice(c * P, (c + 1) * P)
                    pe.wait_ge(k.v_for_t.sem, k.v_for_t.at(1 + 2 * c))
                    for d in range(2):
                        lora = slice(d * RK_LORA, (d + 1) * RK_LORA)
                        mm = pe.matmul(k.ps[:, 4 + d, :], a2[lora, cols], hid[lora, 0, :], start=True, stop=True)
                    mm.then_inc(k.prod_a.sem, 1)
                    pe.matmul(k.ps[:, 0, :], k.square("headones"), y[:, c, :], start=True, stop=True).then_inc(
                        k.prod_v.sem, 1)
                    pe.wait_ge(k.a_for_t.sem, k.a_for_t.at(c + 1))
                    pe.matmul(k.ps[:, 1, :], k.square("headones"), sqr[:, j, :], start=True, stop=True).then_inc(
                        k.prod_a.sem, 1)
                    for q in range(NT):
                        mm = pe.transpose(k.ps[:, 6, q * P:(q + 1) * P], v[:, q, cols], k.square("ident"))
                    mm.then_inc(k.prod_a.sem, 1)
                    pe.matmul(k.ps[:, 2, :], k.square("headones"), r[:, c, :], start=True, stop=True).then_inc(
                        k.prod_v.sem, 1)
                    pe.matmul(k.ps[:, 3, :], g2[:, cols], hid[:, 1, :], start=True, stop=True).then_inc(
                        k.prod_v.sem, 1)
    for n in range(7):
        k.loaded[n].base += 16
    k.prod_a.base += 3 * KC
    k.prod_v.base += 3 * KC
    k.a_for_v.base += 3 * KC
    k.a_for_t.base += KC
    k.v_for_t.base += 1 + 2 * KC


def stage_scale_residual(k):
    with k.nc.Block() as block:
        @block.vector
        def _(dve):
            dve.tensor_scalar(k.x[:, :, :], k.x[:, :, :], DN_ALPHA, None, ALU.mult)


def stage_project_residual(k, w, z, gate, alpha=DN_ALPHA):
    nc = k.nc
    with ExitStack() as s:
        wb = k.sb(f"wb_{w.tensor.name}", [P, 2, KC, 512], stack=s)
        with nc.Block() as block:
            @block.sync
            def _(sp):
                src = w[0].rearrange("(c p) n -> p c n", p=P)
                for j in range(2):
                    sp.dma_start(wb[:, j, :, :], src[:, :, j * 512:(j + 1) * 512]).then_inc(k.landed[j].sem, 16)

            @block.tensor
            def _(pe):
                for o in range(KC):
                    if o % 4 == 0:
                        pe.wait_ge(k.landed[o // 4].sem, k.landed[o // 4].at(16))
                    for c in range(KC):
                        mm = pe.matmul(k.ps[:, o, :], wb[:, o // 4, c, o % 4 * P:o % 4 * P + P], z[:, c, :],
                                       start=c == 0, stop=c == KC - 1)
                    mm.then_inc(k.prod_v.sem, 1)

            @block.vector
            def _(dve):
                if alpha != 1.0:
                    dve.tensor_scalar(k.x[:, :, :], k.x[:, :, :], alpha, None, ALU.mult)
                    dve.drain()
                for o in range(KC):
                    dve.wait_ge(k.prod_v.sem, k.prod_v.at(o + 1))
                    x = k.x[:, o, :]
                    if gate is None:
                        dve.tensor_tensor(x, k.ps[:, o, :], x, ALU.add)
                    else:
                        dve.scalar_tensor_tensor(x, k.ps[:, o, :], gate[:, o:o + 1], x, ALU.mult, ALU.add)
    k.prod_v.base += KC
    for j in range(2):
        k.landed[j].base += 16


def stage_layer_norm(k, i, j):
    g, b = k.v(f"ln_g{i}{j}"), k.v(f"ln_b{i}{j}")
    with ExitStack() as s:
        sqr = k.sb(f"ln_sq{i}{j}", [P, KC, SEQ], stack=s)
        mean, rstd = k.sb(f"ln_m{i}{j}", [P, SEQ], stack=s), k.sb(f"ln_r{i}{j}", [P, SEQ], stack=s)
        with k.nc.Block() as block:
            @block.tensor
            def _(pe):
                for c in range(KC):
                    mm = pe.matmul(k.ps[:, 0, :], k.square("ones"), k.x[:, c, :], start=c == 0, stop=c == KC - 1)
                mm.then_inc(k.prod_v.sem, 1)
                for c in range(KC):
                    pe.wait_ge(k.a_for_t.sem, k.a_for_t.at(c + 1))
                    mm = pe.matmul(k.ps[:, 1, :], k.square("ones"), sqr[:, c, :], start=c == 0, stop=c == KC - 1)
                mm.then_inc(k.prod_a.sem, 1)

            @block.vector
            def _(dve):
                dve.wait_ge(k.prod_v.sem, k.prod_v.at(1))
                dve.tensor_scalar(mean[:, :], k.ps[:, 0, :], 1.0 / D, None, ALU.mult)
                dve.drain()
                for c in range(KC):
                    dve.tensor_tensor(k.x[:, c, :], k.x[:, c, :], mean[:, :], ALU.subtract).then_inc(k.v_for_a.sem, 1)
                dve.wait_ge(k.a_for_v.sem, k.a_for_v.at(1))
                dve.reciprocal(rstd[:, :], rstd[:, :])
                dve.drain()
                for c in range(KC):
                    dve.tensor_tensor(k.x[:, c, :], k.x[:, c, :], rstd[:, :], ALU.mult).then_inc(k.v_for_a.sem, 1)

            @block.scalar
            def _(act):
                for c in range(KC):
                    act.wait_ge(k.v_for_a.sem, k.v_for_a.at(c + 1))
                    act.activation(sqr[:, c, :], k.x[:, c, :], ACT.Square).then_inc(k.a_for_t.sem, 1)
                act.wait_ge(k.prod_a.sem, k.prod_a.at(1))
                act.activation(rstd[:, :], k.ps[:, 1, :], ACT.Sqrt, scale=1.0 / D, bias=k.eps[:, 1:2])
                act.drain().then_inc(k.a_for_v.sem, 1)
                for c in range(KC):
                    act.wait_ge(k.v_for_a.sem, k.v_for_a.at(KC + c + 1))
                    act.activation(k.x[:, c, :], k.x[:, c, :], ACT.Identity, scale=g[:, c:c + 1], bias=b[:, c:c + 1])
    k.prod_v.base += 1
    k.prod_a.base += 1
    k.v_for_a.base += 2 * KC
    k.a_for_t.base += KC
    k.a_for_v.base += 1


def stage_modulate(k, dst, layer, part):
    with k.nc.Block() as block:
        @block.vector
        def _(dve):
            for c in range(KC):
                dve.tensor_scalar(dst[:, c, :], k.x[:, c, :], k.mod[:, layer, (part + 1) * KC + c, 0:1],
                                  k.mod[:, layer, part * KC + c, 0:1], ALU.mult, ALU.add)


def stage_ffn(k):
    nc, t = k.nc, k.t
    width = 2 * P
    pieces = D_FF // width
    FC = D_FF // P
    with ExitStack() as s:
        g = k.sb("ffn_g", [P, FC, SEQ], stack=s)
        with ExitStack() as s1:
            h = k.sb("ffn_h", [P, KC, SEQ], stack=s1)
            wb = k.sb("ffn_wb", [P, 2, 2, KC, width], stack=s1)
            th = k.sb("ffn_th", [P, 2, SEQ], stack=s1)
            stage_modulate(k, h, 0, 3)
            with nc.Block() as block:
                w13 = [t[n][0].rearrange("(c p) n -> p c n", p=P) for n in ("ffn_w1", "ffn_w3")]

                @block.sync
                def _(sp):
                    def piece(i, j):
                        sp.wait_ge(k.prod_a.sem, i * 4 + k.prod_a.at(2 * (j - 1)))
                        for q in range(2):
                            sp.dma_start(wb[:, j, q, :, :], w13[q][:, :, bass.ds(i * (2 * width) + j * width, width)])\
                                .then_inc(k.landed[2 * j + q].sem, 16)
                    with sp.Fori(0, pieces // 2) as i:
                        piece(i, 0)
                        piece(i, 1)
                    piece(pieces // 2, 0)

                @block.tensor
                def _(pe):
                    def piece(i, j):
                        for q in range(2):
                            pe.wait_ge(k.landed[2 * j + q].sem, i * 16 + k.landed[2 * j + q].at(16))
                        for o in range(2):
                            e = 2 * j + o
                            bank = 2 * (e % 4)
                            pe.wait_ge(k.free_v.sem, i * 4 + k.free_v.at(e - 3))
                            for q in range(2):
                                for c in range(KC):
                                    mm = pe.matmul(k.ps[:, bank + q, :], wb[:, j, q, c, o * P:(o + 1) * P], h[:, c, :],
                                                   start=c == 0, stop=c == KC - 1)
                            mm.then_inc(k.prod_a.sem, 1)
                    with pe.Fori(0, pieces // 2) as i:
                        piece(i, 0)
                        piece(i, 1)
                    piece(pieces // 2, 0)

                @block.scalar
                def _(act):
                    def chunk(i, e):
                        act.wait_ge(k.prod_a.sem, i * 4 + k.prod_a.at(e + 1))
                        act.wait_ge(k.free_v.sem, i * 4 + k.free_v.at(e - 1))
                        act.activation(th[:, e % 2, :], k.ps[:, 2 * (e % 4), :], ACT.Tanh, scale=0.5).then_inc(
                            k.a_for_v.sem, 1)
                    with act.Fori(0, pieces // 2) as i:
                        for e in range(4):
                            chunk(i, e)
                    for e in range(2):
                        chunk(pieces // 2, e)

                @block.vector
                def _(dve):
                    def chunk(i, e):
                        dst = g[:, bass.ds(i * 4 + e, 1), :].rearrange("p a n -> p (a n)")
                        bank = 2 * (e % 4)
                        dve.wait_ge(k.a_for_v.sem, i * 4 + k.a_for_v.at(e + 1))
                        dve.scalar_tensor_tensor(th[:, e % 2, :], th[:, e % 2, :], 1.0, k.ps[:, bank, :], ALU.add, ALU.mult)
                        dve.drain()
                        dve.scalar_tensor_tensor(dst, th[:, e % 2, :], 0.5, k.ps[:, bank + 1, :], ALU.mult, ALU.mult)\
                            .then_inc(k.free_v.sem, 1)
                    with dve.Fori(0, pieces // 2) as i:
                        for e in range(4):
                            chunk(i, e)
                    for e in range(2):
                        chunk(pieces // 2, e)
            k.prod_a.base += FC
            k.free_v.base += FC
            k.a_for_v.base += FC
            for j in range(2):
                for q in range(2):
                    k.landed[2 * j + q].base += 16 * ((pieces + 1 - j) // 2)
        wd = k.sb("ffn_wd", [P, 4, FC, P], stack=s)
        with nc.Block() as block:
            src = t["ffn_w2"][0].rearrange("(c p) n -> p c n", p=P)

            @block.sync
            def _(sp):
                with sp.Fori(0, KC // 4) as i:
                    for j in range(4):
                        sp.wait_ge(k.prod_v.sem, i * 4 + k.prod_v.at(j - 3))
                        sp.dma_start(wd[:, j, :, :], src[:, :, bass.ds(i * (4 * P) + j * P, P)]).then_inc(
                            k.landed[j].sem, 16)

            @block.tensor
            def _(pe):
                with pe.Fori(0, KC // 4) as i:
                    for j in range(4):
                        pe.wait_ge(k.landed[j].sem, i * 16 + k.landed[j].at(16))
                        pe.wait_ge(k.free_v.sem, i * 4 + k.free_v.at(j - 3))
                        for c in range(FC):
                            mm = pe.matmul(k.ps[:, j, :], wd[:, j, c, :], g[:, c, :], start=c == 0, stop=c == FC - 1)
                        mm.then_inc(k.prod_v.sem, 1)

            @block.vector
            def _(dve):
                dve.tensor_scalar(k.x[:, :, :], k.x[:, :, :], DN_ALPHA, None, ALU.mult)
                dve.drain()
                gate = k.mod[:, 0, 5 * KC:6 * KC, 0]
                with dve.Fori(0, KC // 4) as i:
                    for j in range(4):
                        o = i * 4 + j
                        x = k.x[:, bass.ds(o, 1), :].rearrange("p a n -> p (a n)")
                        dve.wait_ge(k.prod_v.sem, i * 4 + k.prod_v.at(j + 1))
                        dve.scalar_tensor_tensor(x, k.ps[:, j, :], gate[:, bass.ds(o, 1)], x, ALU.mult, ALU.add)\
                            .then_inc(k.free_v.sem, 1)
        k.prod_v.base += KC
        k.free_v.base += KC
        for j in range(4):
            k.landed[j].base += 16 * KC // 4


def stage_pool(k):
    nc, t = k.nc, k.t
    PAD = max(POOL_WINDOWS) // 2
    W = GRID_W + 2 * PAD
    GC = KC // len(POOL_WINDOWS)
    with ExitStack() as s:
        def sb(name, shape):
            return k.sb(name, shape, stack=s)

        h = sb("pl_h", [P, KC, SEQ])
        inv = sb("pl_inv", [P, len(POOL_WINDOWS), GRID_W])
        wp = sb("pl_w", [P, len(POOL_WINDOWS), GC, GC * P])
        gate = sb("pl_gate", [P, KC])
        pad = [sb(f"pl_{n}", [P, GC * ROWS, W]) for n in range(3)]
        stage_modulate(k, h, 1, 0)
        with nc.Block() as block:
            @block.sync
            def _(sp):
                sp.dma_start(inv[:, :, :].rearrange("p a b -> p (a b)"), t["pool_counts"]).then_inc(k.loaded[0].sem, 16)
                for g in range(len(POOL_WINDOWS)):
                    sp.dma_start(wp[:, g, :, :], t["pool_w"][0, g].rearrange("(c p) n -> p c n", p=P)).then_inc(
                        k.loaded[1].sem, 16)

            @block.vector
            def _(dve):
                dve.tensor_tensor(gate[:, :], k.mod[:, 1, 2 * KC:3 * KC, 0], k.v("pool_scale"), ALU.mult)
                dve.tensor_scalar(k.x[:, :, :], k.x[:, :, :], DN_ALPHA, None, ALU.mult)
                dve.memset(pad[0][:, :, :], 0.0)
                dve.wait_ge(k.loaded[0].sem, k.loaded[0].at(16))
                dve.drain()
                for g, window in enumerate(POOL_WINDOWS):
                    own = h[:, g * GC:(g + 1) * GC, :].rearrange("p c (r w) -> p (c r) w", w=GRID_W)
                    dve.tensor_copy(pad[0][:, :, PAD:PAD + GRID_W], own)
                    dve.drain()
                    src, size, lo, hi, n = pad[0], 1, 0, W, 1
                    while size < window:
                        dst = pad[n]
                        if size == 1:
                            lo += 1
                            dve.tensor_tensor(dst[:, :, lo:hi], src[:, :, lo - 1:hi - 1], src[:, :, lo:hi], ALU.add)
                        else:
                            q = size // 2
                            lo, hi = lo + q, hi - q
                            dve.tensor_tensor(dst[:, :, lo:hi], src[:, :, lo - q:hi - q], src[:, :, lo + q:hi + q],
                                              ALU.add)
                        dve.drain()
                        src, size, n = dst, 2 * size, 3 - n
                    mean = pad[n][:, :, PAD:PAD + GRID_W]
                    dve.tensor_tensor(mean, src[:, :, PAD:PAD + GRID_W],
                                      inv[:, g:g + 1, :].to_broadcast([P, GC * ROWS, GRID_W]), ALU.mult)
                    dve.drain()
                    dve.tensor_tensor(own, mean, own, ALU.subtract)
                    dve.drain().then_inc(k.v_for_t.sem, 1)
                for o in range(KC):
                    dve.wait_ge(k.prod_v.sem, k.prod_v.at(o + 1))
                    dve.scalar_tensor_tensor(k.x[:, o, :], k.ps[:, o, :], gate[:, o:o + 1], k.x[:, o, :],
                                             ALU.mult, ALU.add)

            @block.tensor
            def _(pe):
                pe.wait_ge(k.loaded[1].sem, k.loaded[1].at(16 * len(POOL_WINDOWS)))
                for g in range(len(POOL_WINDOWS)):
                    pe.wait_ge(k.v_for_t.sem, k.v_for_t.at(g + 1))
                    for o in range(GC):
                        for c in range(GC):
                            mm = pe.matmul(k.ps[:, g * GC + o, :], wp[:, g, c, o * P:(o + 1) * P], h[:, g * GC + c, :],
                                           start=c == 0, stop=c == GC - 1)
                        mm.then_inc(k.prod_v.sem, 1)
    k.loaded[0].base += 16
    k.loaded[1].base += 16 * len(POOL_WINDOWS)
    k.v_for_t.base += len(POOL_WINDOWS)
    k.prod_v.base += KC


class Moe:

    def __init__(self, name, experts, width, weights, layer, router, first_logit):
        self.name, self.E, self.F, self.weights, self.layer = name, experts, width, weights, layer
        self.router, self.first_logit = router, first_logit
        self.blocks = experts + (2 * SEQ - experts) // P
        self.slabs = [min(512, width - n) for n in range(0, width, 512)]
        self.chunks = width // P
        assert self.blocks % 2 == 1 and self.blocks > 3 and width % P == 0
        assert self.pieces * 2 % RING == 0

    @property
    def pieces(self):
        return 3 * len(self.slabs)


RING = 6


def stage_moe(k, m, h, gate, alpha):
    nc, t = k.nc, k.t
    E, NB = m.E, m.blocks
    S = len(m.slabs)
    GT_GROUPS = [min(4, m.chunks - n) for n in range(0, m.chunks, 4)]
    NG = len(GT_GROUPS)
    name = m.name

    def scratch(n, shape, dt=F32):
        return nc.dram_tensor(f"{name}_{n}", shape, dt, kind="Internal").ap()

    rows_d, slots_d, out_d = scratch("rows", [SEQ, D]), scratch("slots", [NB * P, 1], I32), scratch("out", [NB * P, D])
    with ExitStack() as keep:
        def sb(n, shape, dt=F32, stack=keep):
            return k.sb(f"{name}_{n}", shape, dt, stack=stack)

        dest = sb("dest", [P, NT * 2], I32)
        weight = sb("weight", [P, NT, 2])
        expert_of = sb("expert_of", [1, NB], I32)
        in_use = sb("in_use", [1, 1], I32)
        slot_token = sb("slot_token", [P, NB], I32)

        with ExitStack() as s:
            row = sb("row", [P, 2, D], stack=s)
            NLOG = m.router[-1][1] + m.router[-1][2]
            wr = sb("wr", [P, KC, NLOG], stack=s)
            bias = sb("bias", [P, NLOG], stack=s)
            iota = sb("iota", [P, 40], stack=s)
            tokid = sb("tokid", [P, NT], I32, stack=s)
            zero = sb("zero", [P, NB], I32, stack=s)
            log = sb("log", [P, NT, NLOG], stack=s)
            gl = sb("gl", [P, NT, 8], stack=s)
            lg = sb("lg", [P, NT, 8], stack=s)
            part = sb("part", [P, NT, 8], stack=s)
            top = sb("top", [P, NT, 8], stack=s)
            idx = sb("idx", [P, NT, 8], U32, stack=s)
            gidx = sb("gidx", [P, NT], stack=s)
            gsum = sb("gsum", [P, NT], stack=s)
            goh = sb("goh", [P, NT, 4], stack=s)
            ex = sb("ex", [P, NT, 2], stack=s)
            e1 = sb("e1", [P, NT], stack=s)
            oh = sb("oh", [P, NT * 2, E], stack=s)
            both = sb("both", [P, NT, E], stack=s)
            pos = sb("pos", [P, NT, E], stack=s)
            destf = sb("destf", [P, NT * 2], stack=s)
            cnt = sb("cnt", [E, P], stack=s)
            nb, nb2 = sb("nb", [E, P], stack=s), sb("nb2", [E, P], stack=s)
            ind = sb("ind", [E, NB + 1], stack=s)
            start = sb("start", [P, E], stack=s)
            grouped = m.first_logit > 0
            with nc.Block() as block:
                @block.sync
                def _(sp):
                    for src, lo, n in m.router:
                        if len(src.shape) == 3:
                            for g in range(src.shape[0]):
                                sp.dma_start(wr[:, :, lo + g * 8:lo + g * 8 + 8],
                                             src[g].rearrange("(c p) e -> p c e", p=P)).then_inc(k.loaded[0].sem, 16)
                        else:
                            sp.dma_start(wr[:, :, lo:lo + n], src.rearrange("(c p) e -> p c e", p=P)).then_inc(
                                k.loaded[0].sem, 16)
                    sp.dma_start(bias[:, :], m_bias(m, t).to_broadcast([P, NLOG])).then_inc(k.loaded[1].sem, 16)
                    sp.dma_start(iota[:, :], t["iotas"]).then_inc(k.loaded[2].sem, 16)
                    sp.dma_start(tokid[:, :], t["token_ids"]).then_inc(k.loaded[3].sem, 16)
                    sp.wait_ge(k.v_for_p.sem, k.v_for_p.at(1))
                    sp.dma_start(slots_d.rearrange("(p b) a -> p (b a)", p=P), zero[:, :]).then_inc(k.loaded[4].sem, 16)
                    for q in range(NT):
                        sp.wait_ge(k.a_for_v.sem, k.a_for_v.at(q + 1))
                        sp.dma_start(rows_d[q * P:(q + 1) * P, :], row[:, q % 2, :]).then_inc(k.stored[q % 2].sem, 16)
                    for j in range(2):
                        sp.wait_ge(k.stored[j].sem, k.stored[j].at(32))

                nrouter = sum(src.shape[0] if len(src.shape) == 3 else 1 for src, _, _ in m.router)

                @block.tensor
                def _(pe):
                    pe.wait_ge(k.loaded[0].sem, k.loaded[0].at(16 * nrouter))
                    for q in range(NT):
                        for c in range(KC):
                            mm = pe.matmul(k.ps[:, 0, q * NLOG:(q + 1) * NLOG], h[:, c, q * P:(q + 1) * P], wr[:, c, :],
                                           start=c == 0, stop=c == KC - 1)
                    mm.then_inc(k.prod_v.sem, 1)
                    for q in range(NT):
                        pe.wait_ge(k.a_for_v.sem, k.a_for_v.at(q - 1))
                        for c in range(KC):
                            mm = pe.transpose(k.ps[:, 4 + q % 2 * 2 + c // 4, c % 4 * P:c % 4 * P + P],
                                              h[:, c, q * P:(q + 1) * P], k.square("ident"))
                        mm.then_inc(k.prod_a.sem, 1)
                    pe.wait_ge(k.v_for_t.sem, k.v_for_t.at(1))
                    for q in range(NT):
                        for q2 in range(q + 1):
                            pe.matmul(k.ps[:, 1, q * E:(q + 1) * E], k.square("ones" if q2 < q else "earlier"),
                                      both[:, q2, :], start=q2 == 0, stop=q2 == q)
                    for q in range(NT):
                        mm = pe.matmul(k.ps[0:E, 2, 0:P], both[:, q, :], k.square("ones"), start=q == 0, stop=q == NT - 1)
                    mm.then_inc(k.prod_v.sem, 1)
                    pe.wait_ge(k.v_for_t.sem, k.v_for_t.at(2))
                    pe.matmul(k.ps[:, 3, 0:E], nb[:, :], k.square("earlier")[0:E, 0:E], start=True, stop=True)
                    pe.matmul(k.ps[0:E, 2, P:P + NB], k.square("le")[0:E, 0:E], nb[:, 0:NB], start=True, stop=True).then_inc(
                        k.prod_v.sem, 1)
                    pe.wait_ge(k.v_for_t.sem, k.v_for_t.at(3))
                    pe.matmul(k.ps[0:1, 2, 256:256 + NB + 1], k.square("ones")[0:E, 0:1], ind[:, :], start=True,
                              stop=True).then_inc(k.prod_v.sem, 1)

                @block.scalar
                def _(act):
                    for q in range(NT):
                        act.wait_ge(k.prod_a.sem, k.prod_a.at(q + 1))
                        if q >= 2:
                            act.wait_ge(k.stored[q % 2].sem, k.stored[q % 2].at(16))
                        act.activation(row[:, q % 2, :].rearrange("p (a b) -> p a b", a=2),
                                       k.ps[:, 4 + q % 2 * 2:6 + q % 2 * 2, :], ACT.Copy)
                        act.drain().then_inc(k.a_for_v.sem, 1)
                    act.wait_ge(k.v_for_a.sem, k.v_for_a.at(1))
                    act.activation(e1[:, :], e1[:, :], ACT.Exp)
                    if grouped:
                        act.activation(gl[:, :, 0:4], gl[:, :, 0:4], ACT.Exp)
                    act.drain().then_inc(k.a_for_v.sem, 1)

                @block.vector
                def _(dve):
                    dve.memset(zero[:, :], 0)
                    dve.memset(gl[:, :, :], -3e38)
                    dve.drain().then_inc(k.v_for_p.sem, 1)
                    for n in (1, 2):
                        dve.wait_ge(k.loaded[n].sem, k.loaded[n].at(16))
                    dve.wait_ge(k.prod_v.sem, k.prod_v.at(1))
                    dve.tensor_tensor(log[:, :, :], k.ps[:, 0, 0:NT * NLOG].rearrange("p (q e) -> p q e", q=NT),
                                      bias[:, :].unsqueeze(1).to_broadcast([P, NT, NLOG]), ALU.add)
                    dve.drain()
                    if grouped:
                        dve.tensor_copy(gl[:, :, 0:4], log[:, :, 0:4])
                        dve.drain()
                        for q in range(NT):
                            dve.max(top[:, q, :], gl[:, q, :])
                        dve.drain()
                        for q in range(NT):
                            dve.max_index(idx[:, q, :], top[:, q, :], gl[:, q, :])
                        dve.drain()
                        dve.tensor_copy(gidx[:, :].unsqueeze(2), idx[:, :, 0:1])
                        dve.tensor_tensor(gl[:, :, 0:4], gl[:, :, 0:4], top[:, :, 0:1].to_broadcast([P, NT, 4]),
                                          ALU.subtract)
                        dve.drain()
                        dve.tensor_tensor(goh[:, :, :], iota[:, 0:4].unsqueeze(1).to_broadcast([P, NT, 4]),
                                          gidx[:, :].unsqueeze(2).to_broadcast([P, NT, 4]), ALU.is_equal)
                        dve.drain()
                        for g in range(4):
                            src = log[:, :, 4 + 8 * g:12 + 8 * g]
                            o = lg if g == 0 else part
                            dve.tensor_tensor(o[:, :, :], src, goh[:, :, g:g + 1].to_broadcast([P, NT, 8]), ALU.mult)
                            dve.drain()
                            if g > 0:
                                dve.tensor_tensor(lg[:, :, :], lg[:, :, :], part[:, :, :], ALU.add)
                                dve.drain()
                    else:
                        dve.tensor_copy(lg[:, :, :], log[:, :, :])
                        dve.drain()
                    for q in range(NT):
                        dve.max(top[:, q, :], lg[:, q, :])
                    dve.drain()
                    for q in range(NT):
                        dve.max_index(idx[:, q, :], top[:, q, :], lg[:, q, :])
                    dve.tensor_tensor(e1[:, :].unsqueeze(2), top[:, :, 1:2], top[:, :, 0:1], ALU.subtract)
                    dve.drain().then_inc(k.v_for_a.sem, 1)
                    dve.tensor_copy(ex[:, :, :], idx[:, :, 0:2])
                    dve.drain()
                    if grouped:
                        dve.tensor_scalar(gidx[:, :], gidx[:, :], 8.0, None, ALU.mult)
                        dve.drain()
                        dve.tensor_tensor(ex[:, :, :], ex[:, :, :], gidx[:, :].unsqueeze(2).to_broadcast([P, NT, 2]),
                                          ALU.add)
                        dve.drain()
                    dve.tensor_tensor(oh[:, :, :], iota[:, 0:E].unsqueeze(1).to_broadcast([P, NT * 2, E]),
                                      ex[:, :, :].rearrange("p q j -> p (q j)").unsqueeze(2).to_broadcast(
                                          [P, NT * 2, E]), ALU.is_equal)
                    dve.drain()
                    o4 = oh[:, :, :].rearrange("p (q j) e -> p q j e", j=2)
                    dve.tensor_tensor(both[:, :, :], o4[:, :, 0, :], o4[:, :, 1, :], ALU.add)
                    dve.drain().then_inc(k.v_for_t.sem, 1)
                    dve.wait_ge(k.a_for_v.sem, k.a_for_v.at(NT + 1))
                    w0, w1 = weight[:, :, 0], weight[:, :, 1]
                    dve.tensor_scalar(w0, e1[:, :], 1.0, None, ALU.add)
                    dve.drain()
                    dve.reciprocal(w0, w0)
                    dve.drain()
                    if grouped:
                        dve.tensor_reduce(gsum[:, :], gl[:, :, 0:4], AX.X, ALU.add)
                        dve.drain()
                        dve.reciprocal(gsum[:, :], gsum[:, :])
                        dve.drain()
                        dve.tensor_tensor(w0, w0, gsum[:, :], ALU.mult)
                        dve.drain()
                    dve.tensor_tensor(w1, w0, e1[:, :], ALU.mult)
                    dve.wait_ge(k.prod_v.sem, k.prod_v.at(2))
                    dve.tensor_copy(cnt[:, :], k.ps[0:E, 2, 0:P])
                    dve.tensor_scalar(nb[:, :], k.ps[0:E, 2, 0:P], 0.0, None, ALU.is_gt)
                    dve.tensor_copy(pos[:, :, :], k.ps[:, 1, 0:NT * E].rearrange("p (q e) -> p q e", q=NT))
                    dve.drain()
                    for j in range(1, NT):
                        dve.tensor_scalar(nb2[:, :], cnt[:, :], float(P * j), None, ALU.is_gt)
                        dve.drain()
                        dve.tensor_tensor(nb[:, :], nb[:, :], nb2[:, :], ALU.add)
                        dve.drain()
                    dve.drain().then_inc(k.v_for_t.sem, 1)
                    dve.wait_ge(k.prod_v.sem, k.prod_v.at(3))
                    dve.tensor_scalar(start[:, :], k.ps[:, 3, 0:E], float(P), None, ALU.mult)
                    dve.tensor_copy(ind[:, NB:NB + 1], nb[:, 0:1])
                    dve.tensor_tensor(ind[:, 0:NB], iota[0:E, 0:NB], k.ps[0:E, 2, P:P + NB], ALU.is_ge)
                    dve.drain().then_inc(k.v_for_t.sem, 1)
                    dve.tensor_tensor(pos[:, :, :], pos[:, :, :], start[:, :].unsqueeze(1).to_broadcast([P, NT, E]),
                                      ALU.add)
                    dve.drain()
                    for j in range(2):
                        dve.tensor_tensor(o4[:, :, j, :], o4[:, :, j, :], pos[:, :, :], ALU.mult)
                    dve.drain()
                    dve.tensor_reduce(destf[:, :], oh[:, :, :], AX.X, ALU.add)
                    dve.drain()
                    dve.tensor_copy(dest[:, :], destf[:, :])
                    dve.wait_ge(k.prod_v.sem, k.prod_v.at(4))
                    dve.tensor_copy(in_use[:, :], k.ps[0:1, 2, 256 + NB:256 + NB + 1])
                    dve.tensor_scalar(expert_of[:, :], k.ps[0:1, 2, 256:256 + NB], float(E - 1), None, ALU.min)
                    dve.drain().then_inc(k.v_for_p.sem, 1)

                @block.gpsimd
                def _(pool):
                    pool.wait_ge(k.loaded[3].sem, k.loaded[3].at(16))
                    pool.wait_ge(k.loaded[4].sem, k.loaded[4].at(16))
                    pool.wait_ge(k.v_for_p.sem, k.v_for_p.at(2))
                    for q in range(NT):
                        for j in range(2):
                            pool.indirect_dma_start(
                                out=slots_d, out_offset=bass.IndirectOffsetOnAxis(
                                    ap=dest[:, 2 * q + j:2 * q + j + 1], axis=0),
                                in_=tokid[:, q:q + 1], in_offset=None).then_inc(k.scattered.sem, 16)
                    pool.wait_ge(k.scattered.sem, k.scattered.at(16 * 2 * NT))
                    pool.dma_start(slot_token[:, :], slots_d.rearrange("(b p) a -> p (b a)", p=P),
                                   allow_slow_non_contiguous=True).then_inc(k.slots_back.sem, 16)
                    pool.wait_ge(k.slots_back.sem, k.slots_back.at(16))
            k.loaded[0].base += 16 * nrouter
            for n in (1, 2, 3, 4):
                k.loaded[n].base += 16
            k.slots_back.base += 16
            k.scattered.base += 32 * NT
            k.prod_v.base += 4
            k.prod_a.base += NT
            k.a_for_v.base += NT + 1
            k.v_for_a.base += 1
            k.v_for_t.base += 3
            k.v_for_p.base += 2
            for j in range(2):
                k.stored[j].base += 32

        with ExitStack() as s:
            wb = sb("wb", [P, RING, 4096], stack=s)
            xg, xt = sb("xg", [P, 2, D], stack=s), sb("xt", [P, KC, P], stack=s)
            index = sb("index", [P, 2], I32, stack=s)
            th = sb("th", [P, 2, 512], stack=s)
            act_, actT = sb("act", [P, 2, m.F], stack=s), sb("actT", [P, m.chunks, P], stack=s)
            yb = sb("yb", [P, 2, D], stack=s)
            w1, w3, w2 = m.weights
            A, V = NG + 1, S + 1
            half_blocks = NB // 2
            turned_banks = S % 2 * 2

            def all_steps(engine, both, own, neither, end, no_end):
                count = engine.value_load(in_use[0:1, 0:1], min_val=1, max_val=NB)

                def step(i, j, last):
                    with engine.If(i * 2 + (j + 1) < count):
                        both(i, j, last)
                    with engine.Else():
                        with engine.If(i * 2 + j < count):
                            own(i, j, last)
                        with engine.Else():
                            neither(i, j, last)
                        engine.nop()

                with engine.Fori(0, half_blocks - 1) as i:
                    step(i, 0, False)
                    step(i, 1, False)
                step(half_blocks - 1, 0, False)
                step(half_blocks - 1, 1, True)
                with engine.If(count > NB - 1):
                    end()
                with engine.Else():
                    no_end()
                engine.nop()

            def count_on(engine, *signals):
                engine.drain()
                for signal, n in signals:
                    if n:
                        engine.sem_inc(signal.sem, n)

            def up(j, n, q):
                return 2 * n + q + (0 if j < 0 else 2 * S + j * m.pieces)

            def down(j, n, end):
                return 2 * S + j * m.pieces + (0 if end else 2 * S) + n

            with nc.Block() as block:
                @block.sync
                def _(sp):
                    def expert(i, j):
                        return sp.value_load(expert_of[0:1, bass.ds(i * 2 + j, 1)], min_val=0, max_val=E - 1)

                    def load(i, number, columns, rows, src):
                        slot = number % RING
                        sp.wait_ge(k.used.sem, i * (2 * m.pieces) + k.used.at(number + 1 - RING))
                        sp.dma_start(wb[:, slot, 0:rows * columns].rearrange("p (c n) -> p c n", c=rows), src).then_inc(
                            k.landed[slot].sem, 16)

                    def load_up(i, j, e):
                        for n, width in enumerate(m.slabs):
                            for q, w in enumerate((w1, w3)):
                                load(i, up(j, n, q), width, KC, w[bass.ds(e, 1), :, n * 512:n * 512 + width].rearrange(
                                    "a (c p) n -> p (a c) n", p=P))

                    def load_down(i, j, e, end):
                        for n, rows in enumerate(GT_GROUPS):
                            load(i, down(j, n, end), D, rows, w2[bass.ds(e, 1), n * 512:n * 512 + rows * P, :].rearrange(
                                "a (c p) n -> p (a c) n", p=P))

                    def leave_out(i, numbers):
                        for number in numbers:
                            slot = number % RING
                            sp.wait_ge(k.used.sem, i * (2 * m.pieces) + k.used.at(number + 1 - RING))
                            sp.sem_inc(k.landed[slot].sem, 16)

                    def ups(j):
                        return [up(j, n, q) for n in range(S) for q in range(2)]

                    def downs(j, end):
                        return [down(j, n, end) for n in range(NG)]

                    load_up(0, -1, expert(0, 0))

                    def both(i, j, last):
                        load_up(i, j, expert(i, j + 1))
                        load_down(i, j, expert(i, j), False)

                    def own(i, j, last):
                        leave_out(i, ups(j))
                        load_down(i, j, expert(i, j), False)

                    all_steps(sp, both, own,
                              lambda i, j, last: leave_out(i, ups(j) + downs(j, False)),
                              lambda: load_down(half_blocks, 0, expert(half_blocks, 0), True),
                              lambda: leave_out(half_blocks, downs(0, True)))

                per_turn = 2 * m.pieces // RING

                @block.gpsimd
                def _(pool):
                    def body(i, j):
                        pool.wait_ge(k.prod_v.sem, i * 2 + k.prod_v.at(j - 1))
                        pool.tensor_copy(index[:, j:j + 1], slot_token[:, bass.ds(i * 2 + j, 1)])
                        pool.drain()
                        pool.indirect_dma_start(
                            out=xg[:, j, :], out_offset=None, in_=rows_d,
                            in_offset=bass.IndirectOffsetOnAxis(ap=index[:, j:j + 1], axis=0)).then_inc(
                            k.gathered[j].sem, 16)

                    with pool.Fori(0, half_blocks) as i:
                        body(i, 0)
                        body(i, 1)
                    body(half_blocks, 0)

                @block.tensor
                def _(pe):
                    def turn(i, j):
                        pe.wait_ge(k.gathered[j].sem, i * 16 + k.gathered[j].at(16))
                        for c in range(KC):
                            mm = pe.transpose(k.ps[:, turned_banks + c // 4, c % 4 * P:c % 4 * P + P],
                                              xg[:, j, c * P:(c + 1) * P], k.square("ident"))
                        mm.then_inc(k.prod_v.sem, 1)

                    def piece(i, number):
                        slot = number % RING
                        pe.wait_ge(k.landed[slot].sem, i * (16 * per_turn) + k.landed[slot].at(16 * (number // RING + 1)))
                        return slot

                    def hidden(i, j, n, width):
                        if n >= 2:
                            pe.wait_ge(k.v_for_t.sem, i * (2 * V) + k.v_for_t.at(1 + (j + 1) * V + n - 1))
                        for q in range(2):
                            slot = piece(i, up(j, n, q))
                            for c in range(KC):
                                mm = pe.matmul(k.ps[:, n % 2 * 2 + q, 0:width], xt[:, c, :],
                                               wb[:, slot, c * width:(c + 1) * width], start=c == 0, stop=c == KC - 1)
                            mm.then_inc(k.used.sem, 1)

                    def turn_activations(i, j, n, rows):
                        if n >= 2:
                            pe.wait_ge(k.a_for_t.sem, i * (2 * A) + k.a_for_t.at(j * A + n - 1))
                        for q in range(rows):
                            c = 4 * n + q
                            mm = pe.transpose(k.ps[:, 4 + n % 2, q * P:(q + 1) * P], act_[:, j, c * P:(c + 1) * P],
                                              k.square("ident"))
                        mm.then_inc(k.prod_a.sem, 1)

                    def output(i, j, end):
                        pe.wait_ge(k.a_for_t.sem, i * (2 * A) + k.a_for_t.at(j * A))
                        for n, rows in enumerate(GT_GROUPS):
                            pe.wait_ge(k.a_for_t.sem, i * (2 * A) + k.a_for_t.at(j * A + n + 1))
                            slot = piece(i, down(j, n, end))
                            for q in range(rows):
                                c = 4 * n + q
                                for o in range(2):
                                    mm = pe.matmul(k.ps[:, 6 + o, :], actT[:, c, :],
                                                   wb[:, slot, q * D + o * 512:q * D + (o + 1) * 512],
                                                   start=c == 0, stop=c == m.chunks - 1)
                            mm.then_inc(k.used.sem, 1)

                    turn(0, 0)
                    pe.wait_ge(k.v_for_t.sem, k.v_for_t.at(1))
                    for n, width in enumerate(m.slabs):
                        hidden(0, -1, n, width)
                    if S > 1:
                        pe.wait_ge(k.v_for_t.sem, k.v_for_t.at(S))
                    turn(0, 1)

                    def both(i, j, last):
                        pe.wait_ge(k.v_for_t.sem, i * (2 * V) + k.v_for_t.at(1 + (j + 1) * V))
                        for n, width in enumerate(m.slabs):
                            hidden(i, j, n, width)
                            turn_activations(i, j, n, GT_GROUPS[n])
                        if not last:
                            if S > 1:
                                pe.wait_ge(k.v_for_t.sem, i * (2 * V) + k.v_for_t.at(1 + (j + 1) * V + S - 1))
                            turn(i + 1, j)
                        output(i, j, False)

                    def finish(i, j, end):
                        for n, rows in enumerate(GT_GROUPS):
                            turn_activations(i, j, n, rows)
                        output(i, j, end)

                    def own(i, j, last):
                        count_on(pe, (k.used, 2 * S), (k.prod_v, 0 if last else 1))
                        pe.wait_ge(k.v_for_t.sem, i * (2 * V) + k.v_for_t.at(1 + (j + 1) * V))
                        finish(i, j, False)

                    def end():
                        pe.wait_ge(k.v_for_t.sem, k.v_for_t.at(NB * V))
                        finish(half_blocks, 0, True)

                    all_steps(pe, both, own,
                              lambda i, j, last: count_on(pe, (k.used, m.pieces), (k.prod_a, NG),
                                                          (k.prod_v, 0 if last else 1)),
                              end, lambda: count_on(pe, (k.used, NG), (k.prod_a, NG)))

                @block.scalar
                def _(act):
                    def used(i, number):
                        return i * (2 * m.pieces) + k.used.at(number + 1)

                    def tanh(i, j, n, width):
                        act.wait_ge(k.used.sem, used(i, up(j, n, 0)))
                        if n >= 2:
                            act.wait_ge(k.v_for_t.sem, i * (2 * V) + k.v_for_t.at(1 + (j + 1) * V + n - 1))
                        act.activation(th[:, n % 2, 0:width], k.ps[:, n % 2 * 2, 0:width], ACT.Tanh,
                                       scale=0.5).then_inc(k.a_for_v.sem, 1)

                    def turned(i, j, n, rows):
                        act.wait_ge(k.prod_a.sem, i * (2 * NG) + k.prod_a.at(j * NG + n + 1))
                        act.activation(actT[:, 4 * n:4 * n + rows, :],
                                       k.ps[:, 4 + n % 2, 0:rows * P].rearrange("p (a b) -> p a b", b=P),
                                       ACT.Copy).then_inc(k.a_for_t.sem, 1)

                    def store(i, j):
                        act.dma_start(out_d[bass.ds(i * (2 * P) + j * P, P), :], yb[:, j, :]).then_inc(
                            k.stored[j].sem, 16)

                    def output(i, j, end):
                        act.wait_ge(k.used.sem, used(i, down(j, NG - 1, end)))
                        act.wait_ge(k.stored[j].sem, i * 16 + k.stored[j].at(0))
                        act.activation(yb[:, j, :].rearrange("p (a b) -> p a b", a=2), k.ps[:, 6:8, :], ACT.Copy)
                        act.drain().then_inc(k.a_for_t.sem, 1)
                        store(i, j)

                    for n, width in enumerate(m.slabs):
                        tanh(0, -1, n, width)

                    def both(i, j, last):
                        for n, width in enumerate(m.slabs):
                            tanh(i, j, n, width)
                            turned(i, j, n, GT_GROUPS[n])
                        output(i, j, False)

                    def finish(i, j, end):
                        for n, rows in enumerate(GT_GROUPS):
                            turned(i, j, n, rows)
                        output(i, j, end)

                    def own(i, j, last):
                        count_on(act, (k.a_for_v, S))
                        finish(i, j, False)

                    def neither(i, j, tanhs):
                        store(i, j)
                        count_on(act, (k.a_for_v, tanhs), (k.a_for_t, A))

                    all_steps(act, both, own, lambda i, j, last: neither(i, j, S),
                              lambda: finish(half_blocks, 0, True), lambda: neither(half_blocks, 0, 0))
                    act.wait_ge(k.stored[0].sem, k.stored[0].at(16 * (half_blocks + 1)))
                    act.wait_ge(k.stored[1].sem, k.stored[1].at(16 * half_blocks))

                @block.vector
                def _(dve):
                    def turned(n):
                        dve.wait_ge(k.prod_v.sem, n)
                        dve.tensor_copy(xt[:, :, :].rearrange("p (a c) n -> p a (c n)", a=2),
                                        k.ps[:, turned_banks:turned_banks + 2, :]).then_inc(k.v_for_t.sem, 1)

                    def activations(i, j):
                        for n, width in enumerate(m.slabs):
                            dve.wait_ge(k.a_for_v.sem, i * (2 * S) + k.a_for_v.at((j + 1) * S + n + 1))
                            dve.scalar_tensor_tensor(th[:, n % 2, 0:width], th[:, n % 2, 0:width], 1.0,
                                                     k.ps[:, n % 2 * 2, 0:width], ALU.add, ALU.mult)
                            dve.drain()
                            dve.wait_ge(k.used.sem, i * (2 * m.pieces) + k.used.at(up(j, n, 1) + 1))
                            dve.scalar_tensor_tensor(act_[:, (j + 1) % 2, n * 512:n * 512 + width], th[:, n % 2, 0:width],
                                                     0.5, k.ps[:, n % 2 * 2 + 1, 0:width], ALU.mult,
                                                     ALU.mult).then_inc(k.v_for_t.sem, 1)

                    turned(k.prod_v.at(1))
                    activations(0, -1)
                    turned(k.prod_v.at(2))

                    def both(i, j, last):
                        activations(i, j)
                        if not last:
                            turned(i * 2 + k.prod_v.at(j + 3))

                    def left_out(i, j, last):
                        count_on(dve, (k.v_for_t, S if last else V))

                    all_steps(dve, both, left_out, left_out, dve.nop, dve.nop)
            k.used.base += NB * m.pieces
            k.prod_v.base += NB
            k.prod_a.base += NB * NG
            k.a_for_v.base += NB * S
            k.v_for_t.base += NB * V
            k.a_for_t.base += NB * (NG + 1)
            total = NB * m.pieces
            for q in range(RING):
                k.landed[q].base += 16 * ((total - q + RING - 1) // RING)
            for j in range(2):
                k.stored[j].base += 16 * (half_blocks + 1 - j)
                k.gathered[j].base += 16 * (half_blocks + 1 - j)

        with ExitStack() as s:
            yg = sb("yg", [P, 2, 2, D], stack=s)
            with nc.Block() as block:
                @block.gpsimd
                def _(pool):
                    for q in range(NT):
                        pool.wait_ge(k.prod_v.sem, k.prod_v.at(q - 1))
                        for j in range(2):
                            pool.indirect_dma_start(
                                out=yg[:, q % 2, j, :], out_offset=None, in_=out_d,
                                in_offset=bass.IndirectOffsetOnAxis(ap=dest[:, 2 * q + j:2 * q + j + 1], axis=0)
                            ).then_inc(k.gathered[q % 2].sem, 16)

                @block.vector
                def _(dve):
                    def add(q):
                        dve.wait_ge(k.prod_v.sem, k.prod_v.at(q + 1))
                        for c in range(KC):
                            x = k.x[:, c, q * P:(q + 1) * P]
                            src = k.ps[:, q % 2 * 2 + c // 4, c % 4 * P:c % 4 * P + P]
                            if gate is None:
                                dve.tensor_tensor(x, src, x, ALU.add)
                            else:
                                dve.scalar_tensor_tensor(x, src, gate[:, c:c + 1], x, ALU.mult, ALU.add)
                        dve.drain().then_inc(k.free_v.sem, 1)

                    if alpha != 1.0:
                        dve.tensor_scalar(k.x[:, :, :], k.x[:, :, :], alpha, None, ALU.mult)
                        dve.drain()
                    for q in range(NT):
                        a, b = yg[:, q % 2, 0, :], yg[:, q % 2, 1, :]
                        dve.wait_ge(k.gathered[q % 2].sem, k.gathered[q % 2].at(32 * (q // 2 + 1)))
                        dve.tensor_scalar(a, a, weight[:, q, 0:1], None, ALU.mult)
                        dve.drain()
                        dve.scalar_tensor_tensor(a, b, weight[:, q, 1:2], a, ALU.mult, ALU.add)
                        dve.drain().then_inc(k.v_for_t.sem, 1)
                        if q:
                            add(q - 1)
                    add(NT - 1)

                @block.tensor
                def _(pe):
                    for q in range(NT):
                        pe.wait_ge(k.v_for_t.sem, k.v_for_t.at(q + 1))
                        pe.wait_ge(k.free_v.sem, k.free_v.at(q - 1))
                        for c in range(KC):
                            mm = pe.transpose(k.ps[:, q % 2 * 2 + c // 4, c % 4 * P:c % 4 * P + P],
                                              yg[:, q % 2, 0, c * P:(c + 1) * P], k.square("ident"))
                        mm.then_inc(k.prod_v.sem, 1)
            k.prod_v.base += NT
            k.free_v.base += NT
            k.v_for_t.base += NT
            for j in range(2):
                k.gathered[j].base += 16 * NT


def m_bias(m, t):
    lo = {"moe": 0, "hier": 8}[m.name]
    n = m.router[-1][1] + m.router[-1][2]
    return t["router_rows"][0:1, lo:lo + n]


def stage_first_moe(k):
    m = Moe("moe", 8, 1408, [k.t[n][0] for n in ("moe_w1", "moe_w3", "moe_w2")], 1,
            [(k.t["moe_router_w"][0], 0, 8)], 0)
    with ExitStack() as s:
        h = k.sb("moe_h", [P, KC, SEQ], stack=s)
        stage_modulate(k, h, 1, 3)
        stage_moe(k, m, h, k.mod[:, 1, 5 * KC:6 * KC, 0], DN_ALPHA)


def stage_rms_norm(k, dst, weight):
    name = dst.name
    with ExitStack() as s:
        sqr, rstd = k.sb(f"rms_sq_{name}", [P, KC, SEQ], stack=s), k.sb(f"rms_r_{name}", [P, SEQ], stack=s)
        with k.nc.Block() as block:
            @block.scalar
            def _(act):
                for c in range(KC):
                    act.activation(sqr[:, c, :], k.x[:, c, :], ACT.Square).then_inc(k.a_for_t.sem, 1)
                act.wait_ge(k.prod_a.sem, k.prod_a.at(1))
                act.activation(rstd[:, :], k.ps[:, 0, :], ACT.Sqrt, scale=1.0 / D, bias=k.eps[:, 2:3]).then_inc(
                    k.a_for_v.sem, 1)

            @block.tensor
            def _(pe):
                for c in range(KC):
                    pe.wait_ge(k.a_for_t.sem, k.a_for_t.at(c + 1))
                    mm = pe.matmul(k.ps[:, 0, :], k.square("ones"), sqr[:, c, :], start=c == 0, stop=c == KC - 1)
                mm.then_inc(k.prod_a.sem, 1)

            @block.vector
            def _(dve):
                dve.wait_ge(k.a_for_v.sem, k.a_for_v.at(1))
                dve.reciprocal(rstd[:, :], rstd[:, :])
                dve.drain()
                for c in range(KC):
                    dve.scalar_tensor_tensor(dst[:, c, :], k.x[:, c, :], weight[:, c:c + 1], rstd[:, :],
                                             ALU.mult, ALU.mult)
    k.a_for_t.base += KC
    k.prod_a.base += 1
    k.a_for_v.base += 1


def stage_in_projection(k, fm, tm, lr):
    nc, t = k.nc, k.t
    att = 2 * GLA_KEY + 2 * GLA_HEADS * GLA_DV + 2 * GLA_RANK
    pieces = [("fm", 0, 0), ("tm", 0, 512), ("fm", 1, 1024), ("fm", 2, att), ("fm", 3, att + 512), ("tm", 1, att + 1024)]
    with ExitStack() as s:
        u = k.sb("in_u", [P, KC, SEQ], stack=s)
        wb = k.sb("in_wb", [P, 3, KC, 512], stack=s)
        wl = k.sb("in_wl", [P, KC, 2 * GLA_RANK], stack=s)
        stage_rms_norm(k, u, k.v("norm1"))
        with nc.Block() as block:
            @block.sync
            def _(sp):
                src = t["w_in_2"][0].rearrange("(c p) n -> p c n", p=P)
                sp.dma_start(wl[:, :, :], src[:, :, att - 2 * GLA_RANK:att]).then_inc(k.loaded[0].sem, 16)
                for n, (_, _, col) in enumerate(pieces):
                    if n >= 3:
                        sp.wait_ge(k.prod_a.sem, k.prod_a.at(4 * (n - 2)))
                    sp.dma_start(wb[:, n % 3, :, :], src[:, :, col:col + 512]).then_inc(k.landed[n % 3].sem, 16)

            @block.tensor
            def _(pe):
                for n, (kind, _, _) in enumerate(pieces):
                    pe.wait_ge(k.landed[n % 3].sem, k.landed[n % 3].at(16 * (n // 3 + 1)))
                    for g in range(4):
                        e = 4 * n + g
                        pe.wait_ge(k.a_for_t.sem, k.a_for_t.at(e - 5))
                        for c in range(KC):
                            own, tokens = wb[:, n % 3, c, :], u[:, c, :]
                            piece = slice(g * P, (g + 1) * P)
                            mm = pe.matmul(k.ps[:, e % 6, :], own[:, piece] if kind == "fm" else tokens[:, piece],
                                           tokens if kind == "fm" else own, start=c == 0, stop=c == KC - 1)
                        mm.then_inc(k.prod_a.sem, 1)
                pe.wait_ge(k.loaded[0].sem, k.loaded[0].at(16))
                for d in range(2):
                    for c in range(KC):
                        mm = pe.matmul(k.ps[32 * d:32 * d + GLA_RANK, 6, :], wl[:, c, d * GLA_RANK:(d + 1) * GLA_RANK],
                                       u[:, c, :], start=c == 0, stop=c == KC - 1)
                mm.then_inc(k.prod_v.sem, 1)

            @block.scalar
            def _(act):
                for n, (kind, q, _) in enumerate(pieces):
                    for g in range(4):
                        e = 4 * n + g
                        act.wait_ge(k.prod_a.sem, k.prod_a.at(e + 1))
                        act.activation((fm[q] if kind == "fm" else tm[q])[:, g, :], k.ps[:, e % 6, :], ACT.Copy)\
                            .then_inc(k.a_for_t.sem, 1)

            @block.vector
            def _(dve):
                dve.memset(lr[:, :], 1.0)
                dve.drain()
                dve.wait_ge(k.prod_v.sem, k.prod_v.at(1))
                for d in range(2):
                    dve.tensor_copy(lr[32 * d:32 * d + GLA_RANK, :], k.ps[32 * d:32 * d + GLA_RANK, 6, :])
    k.loaded[0].base += 16
    for n in range(3):
        k.landed[n].base += 32
    k.prod_a.base += 4 * len(pieces)
    k.a_for_t.base += 4 * len(pieces)
    k.prod_v.base += 1


def stage_linear_attention(k, qk, gg, v, lr, mixed):
    nc, t = k.nc, k.t
    KK = GLA_KEY // P
    BEFORE = {0: ("le", "gt"), 1: ("ge", "lt")}
    with ExitStack() as s:
        def sb(name, shape):
            return k.sb(name, shape, stack=s)

        wg = sb("gl_wg", [64, GLA_KEY])
        la, az, mz = (sb(n, [P, NT, 2 * GLA_KEY]) for n in ("gl_la", "gl_az", "gl_mz"))
        eb, ei, ea = (sb(n, [P, KK, P]) for n in ("gl_eb", "gl_ei", "gl_ea"))
        dec = sb("gl_dec", [P, KK, 2])
        vt = sb("gl_vt", [P, GLA_HEADS * GLA_DV])
        lat = sb("gl_lat", [P, 2 * GLA_KEY])
        kend = sb("gl_kend", [P, GLA_KEY])
        att = sb("gl_att", [P, GLA_HEADS, P])
        S = sb("gl_S", [P, 2, 3, KK * GLA_DV])
        o = mixed[:, 0:GLA_HEADS, :]
        K1 = GLA_RANK + 1
        with nc.Block() as block:
            @block.sync
            def _(sp):
                for d, n in enumerate(("gla_fwd_gate_w_2", "gla_bwd_gate_w_2")):
                    sp.dma_start(wg[32 * d:32 * d + GLA_RANK, :], t[n][0]).then_inc(k.loaded[0].sem, 16)
                    sp.dma_start(wg[32 * d + GLA_RANK:32 * d + K1, :],
                                 t["rows"][0:1, 2 * D + d * GLA_KEY:2 * D + (d + 1) * GLA_KEY]).then_inc(
                        k.loaded[0].sem, 16)

            @block.tensor
            def _(pe):
                pe.wait_ge(k.loaded[0].sem, k.loaded[0].at(64))
                for q in range(NT):
                    for d in range(2):
                        rows = slice(32 * d, 32 * d + K1)
                        mm = pe.matmul(k.ps[:, 2 * q + d, 0:GLA_KEY], lr[rows, q * P:(q + 1) * P], wg[rows, :],
                                       start=True, stop=True)
                mm.then_inc(k.prod_v.sem, 1)

            @block.vector
            def _(dve):
                dve.memset(S[:, :, :, :], 0.0)
                dve.memset(o, 0.0)
                dve.wait_ge(k.prod_v.sem, k.prod_v.at(1))
                z = k.ps[:, :, 0:GLA_KEY]
                flat = lambda m: m[:, :, :].rearrange("p q (d n) -> p (q d) n", d=2)
                dve.tensor_scalar(flat(mz), z, 0.0, None, ALU.min)
                dve.tensor_scalar(flat(az), z, 0.0, None, ALU.max)
                dve.drain()
                dve.tensor_tensor(az[:, :, :], az[:, :, :], mz[:, :, :], ALU.subtract)
                dve.drain().then_inc(k.v_for_a.sem, 1)
                dve.wait_ge(k.a_for_v.sem, k.a_for_v.at(1))
                dve.tensor_tensor(la[:, :, :], mz[:, :, :], la[:, :, :], ALU.subtract)
                dve.drain()
                dve.tensor_scalar(la[:, :, :], la[:, :, :], 1.0 / GLA_TAU, None, ALU.mult)

            @block.scalar
            def _(act):
                act.wait_ge(k.v_for_a.sem, k.v_for_a.at(1))
                act.activation(az[:, :, :], az[:, :, :], ACT.Exp, scale=-1.0)
                act.drain()
                act.activation(la[:, :, :], az[:, :, :], ACT.Ln, bias=k.eps[:, 3:4])
                act.drain().then_inc(k.a_for_v.sem, 1)
        k.loaded[0].base += 64
        k.prod_v.base += 1
        k.v_for_a.base += 1
        k.a_for_v.base += 1

        cnt = {"prod_a": 2, "a_for_v": 1, "a_for_t": 1, "prod_v": 4, "v_for_t": 5, "p_for_t": 2}

        def program(engine, body):
            with engine.Fori(0, NT) as i:
                for d in range(2):
                    first = 0 if d == 0 else SEQ - P
                    body(d, i * (1 if d == 0 else -1) + (0 if d == 0 else NT - 1), i * (P if d == 0 else -P) + first,
                         lambda name, n, d=d: i * (2 * cnt[name]) + k.named[name].at(d * cnt[name] + n))

        def half(h):
            return slice(h % 2 * 64, h % 2 * 64 + 64)

        with nc.Block() as block:
            @block.gpsimd
            def _(pool):
                def body(d, q, at0, at):
                    pool.wait_ge(k.v_for_t.sem, at("v_for_t", 0))
                    for dst, src in ((lat, la), (vt, v)):
                        pool.tensor_copy(dst[:, :], src[:, bass.ds(q, 1), :].rearrange("p a n -> p (a n)")).then_inc(
                            k.p_for_t.sem, 1)
                program(pool, body)

            @block.tensor
            def _(pe):
                def body(d, q, at0, v):
                    incl, after = (k.square(n) for n in BEFORE[d])
                    pe.wait_ge(k.v_for_t.sem, v("v_for_t", 0))
                    pe.wait_ge(k.p_for_t.sem, v("p_for_t", 1))
                    for j, mask in enumerate((incl, after)):
                        for c in range(KK):
                            n = d * GLA_KEY + c * P
                            mm = pe.matmul(k.ps[:, 0, (2 * j + c) * P:(2 * j + c + 1) * P], lat[:, n:n + P], mask,
                                           start=True, stop=True)
                    mm.then_inc(k.prod_a.sem, 1)
                    pe.wait_ge(k.v_for_t.sem, v("v_for_t", 1))
                    for c in range(KK):
                        mm = pe.transpose(k.ps[:, 1, c * P:(c + 1) * P], ea[:, c, :], k.square("ident"))
                    mm.then_inc(k.prod_a.sem, 1)
                    for h in range(GLA_HEADS):
                        mm = pe.matmul(k.ps[:, 2 + h % 2, h // 2 * P:(h // 2 + 1) * P], ei[half(h), h // 2, :],
                                       eb[half(h), h // 2, :], start=True, stop=True)
                    mm.then_inc(k.prod_v.sem, 1)
                    pe.wait_ge(k.p_for_t.sem, v("p_for_t", 2))
                    pe.wait_ge(k.a_for_t.sem, v("a_for_t", 1))
                    pe.sem_inc(k.passed.sem, 1)
                    for step in range(2):
                        c = step if d == 0 else 1 - step
                        rows = slice(c * 64, c * 64 + 64)
                        for h in range(GLA_HEADS):
                            mm = pe.matmul(k.ps[half(h), 4 + step, h // 2 * P:(h // 2 + 1) * P],
                                           kend[rows, h * 64:(h + 1) * 64], vt[rows, h * P:(h + 1) * P],
                                           start=True, stop=True)
                        mm.then_inc(k.prod_v.sem, 1)
                    pe.wait_ge(k.v_for_t.sem, v("v_for_t", 4))
                    for h in range(GLA_HEADS):
                        bank, col = 6 + h % 2, h // 2 * P
                        pe.matmul(k.ps[:, bank, col:col + P], vt[:, h * P:(h + 1) * P], att[:, h, :],
                                  start=True, stop=False)
                        for step in range(2):
                            c = step if d == 0 else 1 - step
                            mm = pe.matmul(k.ps[:, bank, col + c * 64:col + c * 64 + 64],
                                           S[half(h), d, step, h // 2 * P:(h // 2 + 1) * P],
                                           eb[half(h), h // 2, c * 64:c * 64 + 64], start=False, stop=step == 1)
                    mm.then_inc(k.prod_v.sem, 1)
                program(pe, body)

            @block.scalar
            def _(act):
                def body(d, q, at0, v):
                    act.wait_ge(k.prod_a.sem, v("prod_a", 1))
                    sums = k.ps[:, 0, :].rearrange("p (j c n) -> p j c n", j=2, c=KK)
                    act.activation(eb[:, :, :], sums[:, 0, :, :], ACT.Exp)
                    act.activation(ei[:, :, :], sums[:, 0, :, :], ACT.Exp, scale=-1.0)
                    act.activation(ea[:, :, :], sums[:, 1, :, :], ACT.Exp)
                    act.drain().then_inc(k.a_for_v.sem, 1)
                    act.wait_ge(k.prod_a.sem, v("prod_a", 2))
                    act.activation(kend[:, :], k.ps[:, 1, 0:GLA_KEY], ACT.Copy).then_inc(k.a_for_t.sem, 1)
                program(act, body)

            @block.vector
            def _(dve):
                def body(d, q, at0, v):
                    dve.wait_ge(k.a_for_v.sem, v("a_for_v", 1))
                    dve.tensor_copy(S[:, d, 0, :], S[:, d, 2, :])
                    ends = (63, 127) if d == 0 else (0, 64)
                    for c in range(2):
                        dve.tensor_copy(dec[:, :, c:c + 1], eb[:, :, ends[c]:ends[c] + 1])
                    dve.drain()
                    qt, kt = qk[:, 0:KK, bass.ds(at0, P)], qk[:, KK:2 * KK, bass.ds(at0, P)]
                    dve.tensor_scalar(eb[:, :, :], eb[:, :, :], GLA_DK ** -0.5, None, ALU.mult)
                    dve.tensor_tensor(ei[:, :, :], ei[:, :, :], kt, ALU.mult)
                    dve.tensor_tensor(ea[:, :, :], ea[:, :, :], kt, ALU.mult)
                    dve.drain()
                    dve.tensor_tensor(eb[:, :, :], eb[:, :, :], qt, ALU.mult)
                    dve.drain().then_inc(k.v_for_t.sem, 1)
                    dve.wait_ge(k.prod_v.sem, v("prod_v", 1))
                    incl = k.square(BEFORE[d][0]).unsqueeze(1).to_broadcast([P, 2, P])
                    a4 = att[:, :, :].rearrange("p (c j) n -> p j c n", j=2)
                    for j in range(2):
                        dve.tensor_tensor(a4[:, j, :, :], k.ps[:, 2 + j, 0:2 * P].rearrange("p (c n) -> p c n", c=2),
                                          incl, ALU.mult)
                    dve.drain().then_inc(k.v_for_t.sem, 1)
                    for step in range(2):
                        c = step if d == 0 else 1 - step
                        now = S[:, d, step, :].rearrange("p (c n) -> p c n", c=KK)
                        nxt = S[:, d, step + 1, :].rearrange("p (c n) -> p c n", c=KK)
                        dve.wait_ge(k.prod_v.sem, v("prod_v", 2 + step))
                        dve.tensor_tensor(nxt, now, dec[:, :, c:c + 1].to_broadcast([P, KK, GLA_DV]), ALU.mult)
                        dve.drain()
                        dve.tensor_tensor(nxt, nxt, k.ps[:, 4 + step, 0:KK * P].rearrange("p (c n) -> p c n", c=KK), ALU.add)
                        dve.drain().then_inc(k.v_for_t.sem, 1)
                    dve.wait_ge(k.prod_v.sem, v("prod_v", 4))
                    o4 = mixed[:, 0:GLA_HEADS, bass.ds(at0, P)].rearrange("p (c j) n -> p j c n", j=2)
                    dve.tensor_tensor(o4, o4, k.ps[:, 6:8, 0:2 * P].rearrange("p j (c n) -> p j c n", c=2), ALU.add)
                    dve.drain().then_inc(k.v_for_t.sem, 1)
                program(dve, body)
        for name, n in cnt.items():
            k.named[name].base += 2 * NT * n

        with nc.Block() as block:
            @block.scalar
            def _(act):
                sqr = la
                act.activation(sqr[:, :, :], o, ACT.Square).then_inc(k.a_for_t.sem, 1)
                act.activation(az[:, :, :], gg, ACT.Tanh, scale=0.5)
                act.wait_ge(k.prod_a.sem, k.prod_a.at(1))
                act.activation(mz[:, :, :], k.ps[:, 0:GLA_HEADS, :], ACT.Sqrt, scale=1.0 / GLA_DV, bias=k.eps[:, 2:3])
                act.drain().then_inc(k.a_for_v.sem, 1)

            @block.tensor
            def _(pe):
                pe.wait_ge(k.a_for_t.sem, k.a_for_t.at(1))
                for h in range(GLA_HEADS):
                    mm = pe.matmul(k.ps[:, h, :], k.square("ones"), la[:, h, :], start=True, stop=True)
                mm.then_inc(k.prod_a.sem, 1)

            @block.vector
            def _(dve):
                dve.wait_ge(k.a_for_v.sem, k.a_for_v.at(1))
                dve.reciprocal(mz[:, :, :], mz[:, :, :])
                dve.scalar_tensor_tensor(az[:, :, :], az[:, :, :], 1.0, gg, ALU.add, ALU.mult)
                dve.drain()
                dve.scalar_tensor_tensor(o, o, k.v("gla_norm"), mz[:, :, :], ALU.mult, ALU.mult)
                dve.drain()
                dve.scalar_tensor_tensor(o, az[:, :, :], 0.5, o, ALU.mult, ALU.mult)
        k.a_for_t.base += 1
        k.prod_a.base += 1
        k.a_for_v.base += 1


def stage_attention(k, q_, k_, v, mixed):
    nc, t = k.nc, k.t
    HC = ATT_HEADS // 2
    with ExitStack() as s:
        def sb(name, shape):
            return k.sb(name, shape, stack=s)

        rope = sb("at_rope", [P, 2, SEQ])
        logs = sb("at_logs", [P, NT, SEQ])
        tmp = sb("at_tmp", [P, 2, SEQ])
        with nc.Block() as block:
            @block.sync
            def _(sp):
                sp.dma_start(rope[:, :, :].rearrange("p a n -> p (a n)"), t["rope"]).then_inc(k.loaded[0].sem, 16)
                sp.dma_start(logs[:, :, :].rearrange("p a n -> p (a n)"), t["pattern_logs"]).then_inc(
                    k.loaded[1].sem, 16)
                sp.wait_ge(k.loaded[1].sem, k.loaded[1].at(16))

            @block.tensor
            def _(pe):
                for n in range(2 * HC):
                    src = (q_, k_)[n // HC][:, n % HC, :]
                    mm = pe.matmul(k.ps[:, n, :], k.square("rope"), src, start=True, stop=True)
                    mm.then_inc(k.prod_v.sem, 1)

            @block.vector
            def _(dve):
                dve.wait_ge(k.loaded[0].sem, k.loaded[0].at(16))
                for n in range(2 * HC):
                    x = (q_, k_)[n // HC][:, n % HC, :]
                    dve.wait_ge(k.prod_v.sem, k.prod_v.at(n + 1))
                    dve.tensor_tensor(tmp[:, n % 2, :], k.ps[:, n, :], rope[:, 1, :], ALU.mult)
                    dve.tensor_tensor(x, x, rope[:, 0, :], ALU.mult)
                    dve.drain()
                    dve.tensor_tensor(x, x, tmp[:, n % 2, :], ALU.add)
        for n in range(2):
            k.loaded[n].base += 16
        k.prod_v.base += 2 * HC

        own = sb("at_own", [P, 2, SEQ])
        vh = sb("at_vh", [P, NT, P])
        sc, pr = sb("at_sc", [P, 2, SEQ]), sb("at_pr", [P, 2, SEQ])
        pt = sb("at_pt", [P, 2, NT, P])
        mx, z, rz = sb("at_mx", [P, 2, 1]), sb("at_z", [P, 2, 1]), sb("at_rz", [P, 2, 1])
        U = 2 * NT
        with nc.Block() as block:
            @block.gpsimd
            def _(pool):
                with pool.Fori(0, HC) as i:
                    pool.wait_ge(k.free_v.sem, i * 1 + k.free_v.at(0))
                    pool.tensor_copy(own[:, 0, :], q_[:, bass.ds(i, 1), :].rearrange("p a n -> p (a n)"))
                    pool.tensor_copy(own[:, 1, :], k_[:, bass.ds(i, 1), :].rearrange("p a n -> p (a n)"))
                    pool.tensor_copy(vh[:, :, :], v[:, :, bass.ds(i * P, P)])
                    pool.drain().then_inc(k.p_for_t.sem, 1)

            @block.tensor
            def _(pe):
                with pe.Fori(0, HC) as i:
                    pe.wait_ge(k.p_for_t.sem, i + k.p_for_t.at(1))

                    def scores(n):
                        h, q = n // NT, n % NT
                        rows = slice(h * 64, h * 64 + 64)
                        pe.wait_ge(k.v_for_a.sem, i * U + k.v_for_a.at(n - 1))
                        pe.matmul(k.ps[:, n % 2, :], own[rows, 0, q * P:(q + 1) * P], own[rows, 1, :],
                                  start=True, stop=True).then_inc(k.prod_v.sem, 1)

                    def values(n):
                        h, q = n // NT, n % NT
                        pe.wait_ge(k.v_for_t.sem, i * U + k.v_for_t.at(n + 1))
                        pe.wait_ge(k.a_for_t.sem, i * U + k.a_for_t.at(n - 1))
                        for j in range(NT):
                            mm = pe.transpose(k.ps[:, 2 + n % 2, j * P:(j + 1) * P], pr[:, n % 2, j * P:(j + 1) * P],
                                              k.square("ident"))
                        mm.then_inc(k.prod_a.sem, 1)
                        pe.wait_ge(k.a_for_t.sem, i * U + k.a_for_t.at(n + 1))
                        if n == 0:
                            pe.wait_ge(k.free_v.sem, i + k.free_v.at(0))
                        for j in range(NT):
                            mm = pe.matmul(k.ps[h * 64:h * 64 + 64, 4 + h, q * P:(q + 1) * P],
                                           vh[:, j, h * 64:h * 64 + 64], pt[:, n % 2, j, :], start=j == 0, stop=j == NT - 1)
                        if n == U - 1:
                            mm.then_inc(k.used.sem, 1)

                    scores(0)
                    for n in range(U):
                        if n + 1 < U:
                            scores(n + 1)
                        values(n)

            @block.vector
            def _(dve):
                with dve.Fori(0, HC) as i:
                    def softmax(n):
                        j = n % 2
                        dve.wait_ge(k.prod_v.sem, i * U + k.prod_v.at(n + 1))
                        dve.wait_ge(k.a_for_v.sem, i * U + k.a_for_v.at(n - 1))
                        dve.scalar_tensor_tensor(sc[:, j, :], k.ps[:, j, :], ATT_HEAD ** -0.5, logs[:, n % NT, :],
                                                 ALU.mult, ALU.add)
                        dve.drain()
                        dve.tensor_reduce(mx[:, j, :], sc[:, j, :], AX.X, ALU.max)
                        dve.drain()
                        dve.tensor_scalar(mx[:, j, :], mx[:, j, :], -1.0, None, ALU.mult)
                        dve.drain().then_inc(k.v_for_a.sem, 1)

                    def normalise(n):
                        j = n % 2
                        dve.wait_ge(k.a_for_v.sem, i * U + k.a_for_v.at(n + 1))
                        dve.reciprocal(rz[:, j, :], z[:, j, :])
                        dve.drain()
                        dve.tensor_scalar(pr[:, j, :], pr[:, j, :], rz[:, j, :], None, ALU.mult).then_inc(
                            k.v_for_t.sem, 1)

                    softmax(0)
                    for n in range(U):
                        if n + 1 < U:
                            softmax(n + 1)
                        normalise(n)
                    dve.wait_ge(k.used.sem, i + k.used.at(1))
                    for h in range(2):
                        rows = slice(h * 64, h * 64 + 64)
                        dve.tensor_copy(mixed[rows, bass.ds(i + GLA_HEADS, 1), :].rearrange("p a n -> p (a n)"),
                                        k.ps[rows, 4 + h, :])
                    dve.drain().then_inc(k.free_v.sem, 1)

            @block.scalar
            def _(act):
                with act.Fori(0, HC) as i:
                    def turned(n):
                        act.wait_ge(k.prod_a.sem, i * U + k.prod_a.at(n + 1))
                        act.activation(pt[:, n % 2, :, :].rearrange("p j n -> p (j n)"), k.ps[:, 2 + n % 2, :],
                                       ACT.Copy).then_inc(k.a_for_t.sem, 1)

                    for n in range(U):
                        act.wait_ge(k.v_for_a.sem, i * U + k.v_for_a.at(n + 1))
                        act.wait_ge(k.prod_a.sem, i * U + k.prod_a.at(n - 1))
                        act.activation(pr[:, n % 2, :], sc[:, n % 2, :], ACT.Exp, bias=mx[:, n % 2, :],
                                       accum_out=z[:, n % 2, :])
                        act.drain().then_inc(k.a_for_v.sem, 1)
                        if n:
                            turned(n - 1)
                    turned(U - 1)
        for name, n in (("prod_v", U), ("prod_a", U), ("v_for_a", U), ("v_for_t", U), ("a_for_t", U), ("a_for_v", U),
                        ("free_v", 1), ("used", 1), ("p_for_t", 1)):
            k.named[name].base += HC * n


def stage_second_mixer(k):
    with ExitStack() as s:
        mixed = k.sb("mixed", [P, KC, SEQ], stack=s)
        with ExitStack() as s1:
            fm = [k.sb(f"fm{n}", [P, 4, SEQ], stack=s1) for n in range(4)]
            tm = [k.sb(f"tm{n}", [P, NT, 512], stack=s1) for n in range(2)]
            lr = k.sb("lr", [64, SEQ], stack=s1)
            stage_in_projection(k, fm, tm, lr)
            stage_linear_attention(k, fm[0][:, :, :], fm[1][:, :, :], tm[0], lr, mixed)
            stage_attention(k, fm[2], fm[3], tm[1], mixed)
        stage_project_residual(k, k.t["w_out_2"], mixed, None, alpha=1.0)


def stage_second_moe(k):
    t = k.t
    m = Moe("hier", 32, 512, [t[n][0] for n in ("expert_w_gate_2", "expert_w_up_2", "expert_w_down_2")], 1,
            [(t["router_group_w_2"][0], 0, 4), (t["router_expert_w_2"][0], 4, 32)], 4)
    with ExitStack() as s:
        h = k.sb("hier_h", [P, KC, SEQ], stack=s)
        stage_rms_norm(k, h, k.v("norm2"))
        stage_moe(k, m, h, None, 1.0)


def stage_output(k):
    with ExitStack() as s:
        y = k.sb("out_y", [P, KC, SEQ], stack=s)
        stage_rms_norm(k, y, k.v("final_norm"))
        with k.nc.Block() as block:
            @block.sync
            def _(sp):
                sp.dma_start(k.out, y[:, :, :]).then_inc(k.stored[0].sem, 16)
                sp.wait_ge(k.stored[0].sem, k.stored[0].at(16))
        k.stored[0].base += 16


WEIGHTS = ["ada_w", "rk_w_rkv", "rk_w1", "rk_w2", "rk_a1", "rk_a2", "rk_g1", "rk_g2", "rk_w_o", "pool_w",
           "ffn_w1", "ffn_w3", "ffn_w2", "moe_router_w", "moe_w1", "moe_w3", "moe_w2", "w_in_2", "w_out_2",
           "router_group_w_2", "router_expert_w_2", "expert_w_gate_2", "expert_w_up_2", "expert_w_down_2",
           "gla_fwd_gate_w_2", "gla_bwd_gate_w_2"]


def lay_out(inputs):
    a = {n: np.ascontiguousarray(inputs[n]) for n in WEIGHTS}
    both = np.concatenate([np.asarray(inputs["ctx"])[0], np.asarray(inputs["x"])[0]], axis=0)
    a["xT"] = np.ascontiguousarray(both.T.reshape(KC, P, TOK).transpose(1, 0, 2))
    columns = {
        "c": inputs["c"], "c_ctx": inputs["c_ctx"], "k_k": inputs["rk_k_k"], "k_a": inputs["rk_k_a"],
        "r_k": inputs["rk_r_k"], "lnx_g": inputs["rk_lnx_g"], "lnx_b": inputs["rk_lnx_b"],
        "pool_scale": inputs["pool_scale"], "norm1": inputs["norm1_w_2"], "norm2": inputs["norm2_w_2"],
        "final_norm": inputs["final_norm_w_2"], "gla_norm": inputs["gla_norm_w_2"],
    }
    for i in range(2):
        columns[f"ada_b{i}"] = inputs["ada_b"][i]
        columns[f"a0_{i}"] = inputs["rk_a0"][0, i]
        for j in range(2):
            columns[f"ln_g{i}{j}"] = inputs["ln_g"][i, j]
            columns[f"ln_b{i}{j}"] = inputs["ln_b"][i, j]
    for m in range(6):
        columns[f"mu{m}"] = inputs["rk_mu"][0, m]
    a["vectors"] = np.ascontiguousarray(
        np.concatenate([np.asarray(columns[n]).reshape(-1, P).T for n in VECTORS], axis=1))
    a["rows"] = np.concatenate([np.asarray(inputs[n]).reshape(1, -1) for n in
                                ("rk_w0", "gla_fwd_gate_b_2", "gla_bwd_gate_b_2")], axis=1)
    a["router_rows"] = np.concatenate([np.asarray(inputs[n]).reshape(1, -1) for n in
                                       ("moe_router_b", "router_group_b_2", "router_expert_b_2")], axis=1)
    a["squares"] = square_constants()
    a["rope"] = rope_tables()
    a["pattern_logs"] = pattern_logs()
    a["pool_counts"] = pool_counts()
    a["iotas"] = np.tile(np.arange(40, dtype=np.float32)[None], (P, 1))
    a["token_ids"] = np.ascontiguousarray(np.arange(SEQ, dtype=np.int32).reshape(NT, P).T)
    return a


def kernel(**inputs):
    import concourse.bacc as bacc
    from concourse.bass_utils import run_bass_kernel_spmd

    nc = bacc.Bacc("TRN2", target_bir_lowering=False, num_devices=1)
    arrays = {f"in_{n}": a for n, a in lay_out(inputs).items()}
    t = {n[3:]: nc.dram_tensor(n, a.shape, mybir.dt.from_np(a.dtype), kind="ExternalInput").ap()
         for n, a in arrays.items()}
    out = nc.dram_tensor("outT", (P, KC, SEQ), F32, kind="ExternalOutput").ap()
    build(nc, t, out)
    r = run_bass_kernel_spmd(nc, [arrays], core_ids=[0])
    got = r.results[0]["outT"]
    return np.ascontiguousarray(got.transpose(1, 0, 2).reshape(D, SEQ).T)[None]
```

```python
import math
from contextlib import ExitStack

import numpy as np

import concourse.bass as bass
from concourse import mybir

F32 = mybir.dt.float32
I32 = mybir.dt.int32
U32 = mybir.dt.uint32
ALU = mybir.AluOpType
ACT = mybir.ActivationFunctionType
AX = mybir.AxisListType

P = 128
D = 1024
KC = D // P
SEQ = 512
CTX = 256
TOK = CTX + SEQ
NT = SEQ // P
GRID_W = 64
ROWS = SEQ // GRID_W
DEPTH = 2
DN_ALPHA = (2 * DEPTH) ** 0.25
LN_EPS = 1e-5
RMS_EPS = 1e-6

RK_HEAD = 64
RK_LORA = 64
RK_DECAY_SCALE = math.exp(-0.5)
RK_GN_EPS = 64e-5
CHUNK = 64
HG = 4

D_FF = 2816
POOL_WINDOWS = (2, 4, 8, 16)

GLA_HEADS = 4
GLA_DK = 64
GLA_DV = 128
GLA_KEY = GLA_HEADS * GLA_DK
GLA_RANK = 16
GLA_TAU = 16.0
ATT_HEADS = 8
ATT_HEAD = 64
ROT_DIM = ATT_HEAD // 4
ROPE_THETA = 500000.0
DILATED = ((128, 1), (512, 4), (2048, 16))
MASKED = -1e30

SQUARES = ["ident", "ones", "headones", "le", "lt", "ge", "gt", "rope", "earlier", "biasrows", "head_of"]
SQUARES += [f"off{b}_{d}" for d in range(2) for b in (1, 2, 4, 8, 16, 32)]
SQ = {name: n for n, name in enumerate(SQUARES)}


def square_constants():
    s, t = np.meshgrid(np.arange(P), np.arange(P), indexing="ij")
    same = s // CHUNK == t // CHUNK
    c = {
        "ident": s == t, "ones": s >= 0, "headones": s // 64 == t // 64,
        "le": same & (s <= t), "lt": same & (s < t), "ge": same & (s >= t), "gt": same & (s > t),
        "earlier": s < t, "biasrows": s % 64 == 0,
    }
    c["head_of"] = t % 16 == 2 * (t // 16) + s // RK_HEAD
    half = ROT_DIM // 2
    sm, tm = s % ATT_HEAD, t % ATT_HEAD
    same_head = s // ATT_HEAD == t // ATT_HEAD
    c["rope"] = (same_head & (tm >= half) & (tm < ROT_DIM) & (sm == tm - half)).astype(np.float32) \
        - (same_head & (tm < half) & (sm == tm + half)).astype(np.float32)
    for d in range(2):
        for b in (1, 2, 4, 8, 16, 32):
            pair = (s // (2 * b) == t // (2 * b)) & (s // b != t // b)
            c[f"off{b}_{d}"] = pair & ((s < t) if d == 0 else (s > t))
    return np.concatenate([np.asarray(c[n], np.float32) for n in SQUARES], axis=1)


def head_rows():
    return (np.arange(D)[None] // RK_HEAD == np.arange(D // RK_HEAD)[:, None]).astype(np.float32)


def rope_tables():
    inv = ROPE_THETA ** (-(np.arange(0, ROT_DIM, 2, dtype=np.float32) / ROT_DIM))
    ang = (np.arange(SEQ, dtype=np.float32)[:, None] * inv[None, :].astype(np.float32)).astype(np.float32)
    cos, sin = np.ones((P, SEQ), np.float32), np.zeros((P, SEQ), np.float32)
    for p in range(P):
        if p % ATT_HEAD < ROT_DIM:
            cos[p] = np.cos(ang[:, p % (ROT_DIM // 2)])
            sin[p] = np.sin(ang[:, p % (ROT_DIM // 2)])
    return np.concatenate([cos, sin], axis=1)


def pattern_logs():
    i, j = np.meshgrid(np.arange(SEQ), np.arange(SEQ), indexing="ij")
    n = sum(((i - j) % d == 0) & (abs(i - j) // d <= w // (2 * d)) for w, d in DILATED)
    logs = np.where(n > 0, np.log(np.maximum(n, 1)), MASKED).astype(np.float32)
    return logs.reshape(NT, P, SEQ).transpose(1, 0, 2).reshape(P, NT * SEQ)


def pool_counts():
    out = []
    for w in POOL_WINDOWS:
        t = np.arange(GRID_W)
        n = np.clip(t + w // 2, 0, GRID_W) - np.clip(t - w // 2, 0, GRID_W)
        out.append(1.0 / n.astype(np.float32))
    return np.tile(np.concatenate(out).astype(np.float32)[None], (P, 1))


VECTORS = {}


def column(name, chunks):
    VECTORS[name] = (sum(n for _, n in VECTORS.values()), chunks)


for _n, _c in [("c", KC), ("c_ctx", KC), ("ada_b0", 6 * KC), ("ada_b1", 6 * KC)] + \
        [(f"ln_{x}{i}{j}", KC) for x in "gb" for i in range(2) for j in range(2)] + \
        [(f"mu{m}", KC) for m in range(6)] + \
        [("a0_0", KC), ("a0_1", KC), ("k_k", KC), ("k_a", KC), ("r_k", KC), ("lnx_g", KC), ("lnx_b", KC),
         ("pool_scale", KC), ("norm1", KC), ("norm2", KC), ("final_norm", KC), ("gla_norm", 1),
         ]:
    column(_n, _c)
NVEC = sum(n for _, n in VECTORS.values())

ROWVECS = {"w0": (0, 2 * D), "gate_b": (2 * D, 2 * GLA_KEY)}
ROWLEN = 2 * D + 2 * GLA_KEY
ROUTER_ROW = {"moe_b": (0, 8), "group_b": (8, 4), "expert_b": (12, 32)}


class Signal:

    HEAD = 128

    def __init__(self, sem, head=HEAD):
        self.sem, self.base = sem, head

    def at(self, n):
        return self.base + n


class Kit:
    pass


def build(nc, t, out):
    with ExitStack() as top:
        k = Kit()
        k.nc, k.t, k.out = nc, t, out

        def sb(name, shape, dt=F32, stack=top):
            return stack.enter_context(nc.sbuf_tensor(name, shape, dt))

        k.sb = sb
        sem = lambda name: Signal(top.enter_context(nc.semaphore(name)))
        dma_sem = lambda name: Signal(top.enter_context(nc.semaphore(name)), 0)
        k.ps = top.enter_context(nc.psum_tensor("ps", [P, 8, 512], F32))
        k.prod_a, k.prod_v, k.free_a, k.free_v = sem("prod_a"), sem("prod_v"), sem("free_a"), sem("free_v")
        k.a_for_t, k.v_for_t, k.a_for_v, k.v_for_a = sem("a_for_t"), sem("v_for_t"), sem("a_for_v"), sem("v_for_a")
        k.v_for_p, k.p_for_t, k.p_for_v = sem("v_for_p"), sem("p_for_t"), sem("p_for_v")
        k.used, k.normed = sem("used"), sem("normed")
        k.prep_t, k.prep_a, k.prep_v = sem("prep_t"), sem("prep_a"), sem("prep_v")
        k.passed, k.sp_passed = sem("passed"), sem("sp_passed")
        k.named = {"prod_a": k.prod_a, "prod_v": k.prod_v, "free_a": k.free_a, "free_v": k.free_v,
                   "a_for_t": k.a_for_t, "v_for_t": k.v_for_t, "p_for_t": k.p_for_t, "a_for_v": k.a_for_v,
                   "p_for_v": k.p_for_v, "v_for_a": k.v_for_a, "v_for_p": k.v_for_p, "used": k.used, "normed": k.normed,
                   "passed": k.passed, "sp_passed": k.sp_passed, "prep_t": k.prep_t, "prep_a": k.prep_a, "prep_v": k.prep_v}
        k.landed = [dma_sem(f"landed{n}") for n in range(6)]
        k.loaded = [dma_sem(f"loaded{n}") for n in range(8)]
        k.gathered = [dma_sem(f"gathered{n}") for n in range(2)]
        k.scattered, k.slots_back = dma_sem("scattered"), dma_sem("slots_back")
        k.stored = [sem(f"stored{n}") for n in range(2)]

        k.sq = sb("sq", [P, len(SQUARES), P])
        k.vec = sb("vec", [P, NVEC])
        k.mod = sb("mod", [P, 2, 6 * KC, 2])
        k.x = sb("x", [P, KC, SEQ])
        k.square = lambda name: k.sq[:, SQ[name], :]
        k.v = lambda name: k.vec[:, VECTORS[name][0]:VECTORS[name][0] + VECTORS[name][1]]
        k.eps = sb("eps", [P, 4])

        def scratch(name, shape, dt=F32):
            return nc.dram_tensor(name, shape, dt, kind="Internal").ap()

        k.r_d, k.k_d, k.kk_d = (scratch(n, [P, KC, TOK]) for n in ("r_d", "k_d", "kk_d"))
        k.v_d = scratch("v_d", [TOK, D])
        k.hid_d = scratch("hid_d", [3, P, TOK])

        stage_load(k)
        with ExitStack() as s:
            h = sb("h", [P, KC, TOK], stack=s)
            stage_modulation(k, h)
            stage_rwkv_features(k, h)
        stage_key_directions(k)
        with ExitStack() as s:
            y = sb("y", [P, KC, SEQ], stack=s)
            stage_rwkv_scan(k, y)
            wb = sb("wb_rk_w_o", [P, 2, KC, 512], stack=s)
            stage_rwkv_out(k, y, wb, t["rk_w_o"])
            stage_project_residual(k, wb, y, k.mod[:, 0, 2 * KC:3 * KC, 0])
        stage_layer_norm(k, 0, 0)
        stage_ffn(k)
        stage_layer_norm(k, 0, 1)
        stage_pool(k)
        stage_layer_norm(k, 1, 0)
        stage_first_moe(k)
        stage_layer_norm(k, 1, 1)
        stage_second_mixer(k)
        stage_second_moe(k)
        stage_output(k)


def chunkwise(vec, tokens):
    return vec.unsqueeze(2).to_broadcast([P, vec.shape[1], tokens])


def stage_load(k):
    with k.nc.Block() as block:
        @block.sync
        def _(sp):
            sp.dma_start(k.sq[:, :, :].rearrange("p a b -> p (a b)"), k.t["squares"]).then_inc(k.loaded[0].sem, 16)
            sp.dma_start(k.vec[:, :], k.t["vectors"]).then_inc(k.loaded[1].sem, 16)
            for s in [*k.named.values(), *k.stored]:
                sp.sem_inc(s.sem, Signal.HEAD)
            for n in range(2):
                sp.wait_ge(k.loaded[n].sem, k.loaded[n].at(16))

        @block.vector
        def _(dve):
            for n, eps in enumerate((RK_GN_EPS, LN_EPS, RMS_EPS, 1.0)):
                dve.memset(k.eps[:, n:n + 1], eps)
    for n in range(2):
        k.loaded[n].base += 16


def stage_modulation(k, h):
    per_layer = 6 * D // 512
    pieces = DEPTH * per_layer
    ring = 4
    with ExitStack() as s:
        wb = k.sb("wb_ada", [P, ring, KC, 512], stack=s)
        c2 = k.sb("c2", [P, KC, 2], stack=s)
        th = k.sb("th", [P, KC, 2], stack=s)
        rows = k.sb("mod_rows", [2, pieces * 512], stack=s)
        with k.nc.Block() as block:
            @block.sync
            def _(sp):
                src = k.t["ada_w"].rearrange("l (c p) n -> l p c n", p=P)
                for layer in range(DEPTH):
                    with sp.Fori(0, per_layer // ring) as i:
                        for j in range(ring):
                            sp.wait_ge(k.prod_v.sem, i * ring + k.prod_v.at(layer * per_layer + j + 1 - ring))
                            sp.dma_start(wb[:, j, :, :],
                                         src[layer, :, :, bass.ds(i * (512 * ring) + j * 512, 512)]).then_inc(
                                k.landed[j].sem, 16)
                sp.dma_start(h[:, :, :], k.t["xT"]).then_inc(k.loaded[0].sem, 16)
                sp.wait_ge(k.loaded[0].sem, k.loaded[0].at(16))

            @block.scalar
            def _(act):
                for z, name in enumerate(("c", "c_ctx")):
                    act.activation(th[:, :, z], k.v(name), ACT.Tanh, scale=0.5)
                act.drain().then_inc(k.a_for_v.sem, 1)

            @block.vector
            def _(dve):
                dve.wait_ge(k.a_for_v.sem, k.a_for_v.at(1))
                for z, name in enumerate(("c", "c_ctx")):
                    dve.scalar_tensor_tensor(c2[:, :, z], th[:, :, z], 1.0, k.v(name), ALU.add, ALU.mult)
                dve.drain()
                dve.tensor_scalar(c2[:, :, :], c2[:, :, :], 0.5, None, ALU.mult).then_inc(k.v_for_t.sem, 1)
                with dve.Fori(0, pieces // ring) as i:
                    for j in range(ring):
                        dve.wait_ge(k.prod_v.sem, i * ring + k.prod_v.at(j + 1))
                        dve.tensor_copy(rows[:, bass.ds(i * (512 * ring) + j * 512, 512)], k.ps[0:2, j, :]).then_inc(
                            k.free_v.sem, 1)
                dve.wait_ge(k.prod_v.sem, k.prod_v.at(pieces + 1))
                for layer in range(DEPTH):
                    dve.tensor_tensor(
                        k.mod[:, layer, :, :],
                        k.ps[:, 4, layer * 12 * KC:(layer + 1) * 12 * KC].rearrange("p (o z) -> p o z", z=2),
                        k.v(f"ada_b{layer}").unsqueeze(2).to_broadcast([P, 6 * KC, 2]), ALU.add)
                dve.drain()
                for layer in range(DEPTH):
                    for part in (1, 4):
                        m = k.mod[:, layer, part * KC:(part + 1) * KC, :]
                        dve.tensor_scalar(m, m, 1.0, None, ALU.add)

            @block.tensor
            def _(pe):
                pe.wait_ge(k.v_for_t.sem, k.v_for_t.at(1))
                with pe.Fori(0, pieces // ring) as i:
                    for j in range(ring):
                        pe.wait_ge(k.landed[j].sem, i * 16 + k.landed[j].at(16))
                        pe.wait_ge(k.free_v.sem, i * ring + k.free_v.at(j + 1 - ring))
                        for c in range(KC):
                            mm = pe.matmul(k.ps[0:2, j, :], c2[:, c, :], wb[:, j, c, :], start=c == 0, stop=c == KC - 1)
                        mm.then_inc(k.prod_v.sem, 1)
                pe.wait_ge(k.free_v.sem, k.free_v.at(pieces))
                for o in range(pieces * 4):
                    mm = pe.transpose(k.ps[:, 4, 2 * o:2 * o + 2], rows[:, o * P:(o + 1) * P], k.square("ident")[0:2, 0:2])
                mm.then_inc(k.prod_v.sem, 1)
    k.prod_v.base += pieces + 1
    k.free_v.base += pieces
    k.a_for_v.base += 1
    k.v_for_t.base += 1
    k.loaded[0].base += 16
    for j in range(ring):
        k.landed[j].base += 16 * pieces // ring


def stage_rwkv_features(k, h):
    nc, t = k.nc, k.t
    half = TOK // 2
    with ExitStack() as s:
        xx = k.sb("xx", [P, KC, TOK], stack=s)
        mix = k.sb("mix", [P, 2, KC, TOK], stack=s)
        zero = k.sb("zero", [P, CTX], stack=s)
        wb2 = k.sb("wb_rkv", [P, 2, KC, 512], stack=s)
        slots = [wb2[:, 0, :, :], wb2[:, 1, :, :], k.x[:, :, :]]
        wl = k.sb("wl", [P, 2, KC, P], stack=s)
        vst = k.sb("rkv_out", [P, 2, D], stack=s)
        st = vst[:, :, 0:TOK]
        RH, WH, KH, VH, AH, GH = range(6)
        order = [RH, KH, VH, WH, AH, GH]
        weight_of = {RH: 0, KH: 1, VH: 2}
        groups = {RH: KC, KH: KC, VH: TOK // P, WH: 1, AH: 1, GH: 1}
        first = {}
        for m in order:
            first[m] = sum(groups[q] for q in order[:order.index(m)])
        total = sum(groups.values())
        hid = {WH: 0, AH: 1, GH: 2}
        with nc.Block() as block:
            @block.sync
            def _(sp):
                for n, m in enumerate((RH, RH, KH, KH, VH, VH)):
                    if n >= 3:
                        used = first[RH if n < 5 else KH] + (8 if n == 4 else 4)
                        sp.wait_ge(k.prod_a.sem, k.prod_a.at(used))
                    src = t["rk_w_rkv"][0, weight_of[m]].rearrange("(c p) n -> p c n", p=P)
                    sp.dma_start(slots[n % 3], src[:, :, n % 2 * 512:(n % 2 + 1) * 512]).then_inc(k.landed[n % 3].sem, 16)
                for n, (m, name) in enumerate(((WH, "rk_w1"), (AH, "rk_a1"), (GH, "rk_g1"))):
                    slot = n % 2
                    if n == 2:
                        sp.wait_ge(k.prod_a.sem, k.prod_a.at(first[AH]))
                    if m == GH:
                        sp.dma_start(wl[:, slot, :, :], t[name][0].rearrange("(c p) n -> p c n", p=P)).then_inc(
                            k.landed[3 + n].sem, 16)
                    else:
                        for z in range(2):
                            sp.dma_start(wl[:, slot, :, z * RK_LORA:(z + 1) * RK_LORA],
                                         t[name][0, z].rearrange("(c p) n -> p c n", p=P)).then_inc(
                                k.landed[3 + n].sem, 16)

            @block.vector
            def _(dve):
                dve.memset(zero[:, :], 0.0)
                dve.drain().then_inc(k.v_for_a.sem, 1)
                for z, (lo, hi) in enumerate(((CTX, TOK), (0, CTX))):
                    for c in range(KC):
                        dve.tensor_scalar(h[:, c, lo:hi], h[:, c, lo:hi], k.mod[:, 0, KC + c, z:z + 1],
                                          k.mod[:, 0, c, z:z + 1], ALU.mult, ALU.add)
                dve.drain()

                def minus(dst, shifted, own):
                    if shifted is None:
                        dve.tensor_scalar(dst, own, -1.0, None, ALU.mult)
                    else:
                        dve.tensor_tensor(dst, shifted, own, ALU.subtract)

                a, b = slice(0, KC // 2), slice(KC // 2, KC)
                minus(xx[:, a, 1:CTX], h[:, a, 0:CTX - 1], h[:, a, 1:CTX])
                minus(xx[:, a, 0:1], None, h[:, a, 0:1])
                minus(xx[:, b, 0:CTX - 1], h[:, b, 1:CTX], h[:, b, 0:CTX - 1])
                minus(xx[:, b, CTX - 1:CTX], None, h[:, b, CTX - 1:CTX])
                for c in range(KC):
                    grid = lambda m: m[:, c, CTX:TOK].rearrange("p (r w) -> p r w", w=GRID_W)
                    d, g = grid(xx), grid(h)
                    W, R = GRID_W, ROWS
                    if c < KC // 4:
                        minus(d[:, :, 1:W], g[:, :, 0:W - 1], g[:, :, 1:W])
                        minus(d[:, :, 0:1], None, g[:, :, 0:1])
                    elif c < KC // 2:
                        minus(d[:, :, 0:W - 1], g[:, :, 1:W], g[:, :, 0:W - 1])
                        minus(d[:, :, W - 1:W], None, g[:, :, W - 1:W])
                    elif c < 3 * KC // 4:
                        minus(d[:, 1:R, :], g[:, 0:R - 1, :], g[:, 1:R, :])
                        minus(d[:, 0:1, :], None, g[:, 0:1, :])
                    else:
                        minus(d[:, 0:R - 1, :], g[:, 1:R, :], g[:, 0:R - 1, :])
                        minus(d[:, R - 1:R, :], None, g[:, R - 1:R, :])
                dve.drain()
                for n, m in enumerate(order):
                    if n >= 2:
                        dve.wait_ge(k.prod_a.sem, k.prod_a.at(first[order[n - 1]]))
                    own = slice(CTX if m == RH else 0, TOK)
                    for c in range(KC):
                        dve.scalar_tensor_tensor(mix[:, n % 2, c, own], xx[:, c, own], k.v(f"mu{m}")[:, c:c + 1],
                                                 h[:, c, own], ALU.mult, ALU.add)
                    dve.drain().then_inc(k.v_for_t.sem, 1)

            @block.tensor
            def _(pe):
                for n, m in enumerate(order):
                    pe.wait_ge(k.v_for_t.sem, k.v_for_t.at(n + 1))
                    x = mix[:, n % 2, :, :]
                    if m in weight_of:
                        halves = [2 * weight_of[m], 2 * weight_of[m] + 1]
                        for n in halves:
                            pe.wait_ge(k.landed[n % 3].sem, k.landed[n % 3].at(16 * (n // 3 + 1)))
                    else:
                        q = 3 + hid[m]
                        pe.wait_ge(k.landed[q].sem, k.landed[q].at(16 if m == GH else 32))
                    for g in range(groups[m]):
                        number = first[m] + g
                        pe.wait_ge(k.free_a.sem, k.free_a.at(number - 3))
                        for part in range(1 if m == RH else 2):
                            bank = number % 4 * 2 + part
                            for c in range(KC):
                                if m == VH:
                                    lhs, rhs = x[:, c, g * P:(g + 1) * P], slots[halves[part] % 3][:, c, :]
                                    o = k.ps[:, bank, :]
                                elif m == RH:
                                    lhs = slots[halves[g // 4] % 3][:, c, g % 4 * P:g % 4 * P + P]
                                    rhs, o = x[:, c, CTX:TOK], k.ps[:, bank, :]
                                else:
                                    lhs = wl[:, hid[m] % 2, c, :] if m in hid else \
                                        slots[halves[g // 4] % 3][:, c, g % 4 * P:g % 4 * P + P]
                                    rhs = x[:, c, part * half:(part + 1) * half]
                                    o = k.ps[:, bank, 0:half]
                                mm = pe.matmul(o, lhs, rhs, start=c == 0, stop=c == KC - 1)
                        mm.then_inc(k.prod_a.sem, 1)

            @block.scalar
            def _(act):
                act.wait_ge(k.v_for_a.sem, k.v_for_a.at(1))
                act.dma_start(k.r_d[:, :, 0:CTX], zero[:, :].unsqueeze(1).to_broadcast([P, KC, CTX])).then_inc(
                    k.loaded[1].sem, 16)
                for m in order:
                    for g in range(groups[m]):
                        number = first[m] + g
                        act.wait_ge(k.prod_a.sem, k.prod_a.at(number + 1))
                        if m == RH:
                            banks = k.ps[:, number % 4 * 2:number % 4 * 2 + 1, :]
                            slot = st[:, number % 2, 0:SEQ]
                        elif m != VH:
                            banks = k.ps[:, number % 4 * 2:number % 4 * 2 + 2, 0:half]
                            slot = st[:, number % 2, :]
                        else:
                            banks = k.ps[:, number % 4 * 2:number % 4 * 2 + 2, :]
                            slot = vst[:, number % 2, :]
                        if number >= 2:
                            q = k.stored[number % 2]
                            act.wait_ge(q.sem, q.at(16 * (number // 2)))
                        f = {WH: ACT.Tanh, GH: ACT.Tanh}.get(m, ACT.Copy)
                        act.activation(slot.rearrange("p (a b) -> p a b", a=1 if m == RH else 2), banks, f,
                                       scale=0.5 if m == GH else 1.0)
                        act.drain().then_inc(k.free_a.sem, 1)
                        if m == VH:
                            dst = k.v_d[g * P:(g + 1) * P, :]
                        elif m in hid:
                            dst = k.hid_d[hid[m]]
                        elif m == RH:
                            dst = k.r_d[:, g, CTX:TOK]
                        else:
                            dst = k.k_d[:, g, :]
                        act.dma_start(dst, slot).then_inc(k.stored[number % 2].sem, 16)
                for q in range(2):
                    act.wait_ge(k.stored[q].sem, k.stored[q].at(16 * ((total + 1 - q) // 2)))
                act.wait_ge(k.loaded[1].sem, k.loaded[1].at(16))
        k.prod_a.base += total
        k.free_a.base += total
        k.v_for_t.base += len(order)
        k.v_for_a.base += 1
        k.loaded[1].base += 16
        for j in range(2):
            k.stored[j].base += 16 * ((total + 1 - j) // 2)
        for j in range(5):
            k.landed[j].base += 32
        k.landed[5].base += 16


def stage_key_directions(k):
    nc, t = k.nc, k.t
    half = TOK // 2
    H = D // RK_HEAD
    with ExitStack() as s:
        kk = k.sb("kk", [P, KC, TOK], stack=s)
        sqr = k.sb("kk_sq", [P, 2, TOK], stack=s)
        norm = k.sb("kk_norm", [H, 2, half], stack=s)
        rows = k.sb("kk_rows", [H, D], stack=s)
        halves = lambda m: m.rearrange("p (a b) -> p a b", a=2)
        with nc.Block() as block:
            @block.sync
            def _(sp):
                for n in range(2):
                    sp.dma_start(kk[:, n * 4:n * 4 + 4, :], k.k_d[:, n * 4:n * 4 + 4, :]).then_inc(k.loaded[n].sem, 16)
                sp.dma_start(rows[:, :], t["head_rows"]).then_inc(k.loaded[2].sem, 16)
                for n in range(2):
                    sp.wait_ge(k.v_for_t.sem, k.v_for_t.at(1 + 4 * (n + 1)))
                    sp.dma_start(k.kk_d[:, n * 4:n * 4 + 4, :], kk[:, n * 4:n * 4 + 4, :]).then_inc(k.stored[n].sem, 16)
                for n in range(2):
                    sp.wait_ge(k.stored[n].sem, k.stored[n].at(16))

            @block.vector
            def _(dve):
                for c in range(KC):
                    dve.wait_ge(k.loaded[c // 4].sem, k.loaded[c // 4].at(16))
                    dve.tensor_scalar(kk[:, c, :], kk[:, c, :], k.v("k_k")[:, c:c + 1], None, ALU.mult).then_inc(
                        k.v_for_a.sem, 1)
                dve.wait_ge(k.a_for_v.sem, k.a_for_v.at(1))
                dve.tensor_scalar(norm[:, :, :], norm[:, :, :], 1e-12, None, ALU.max)
                dve.drain()
                dve.reciprocal(norm[:, :, :], norm[:, :, :])
                dve.drain().then_inc(k.v_for_t.sem, 1)
                for c in range(KC):
                    dve.wait_ge(k.prod_v.sem, k.prod_v.at(c + 1))
                    b = 2 + c % 3 * 2
                    dve.tensor_tensor(halves(kk[:, c, :]), halves(kk[:, c, :]), k.ps[:, b:b + 2, 0:half],
                                      ALU.mult).then_inc(k.v_for_t.sem, 1)

            @block.scalar
            def _(act):
                for c in range(KC):
                    act.wait_ge(k.v_for_a.sem, k.v_for_a.at(c + 1))
                    act.wait_ge(k.prod_a.sem, k.prod_a.at(c - 1))
                    act.activation(sqr[:, c % 2, :], kk[:, c, :], ACT.Square).then_inc(k.a_for_t.sem, 1)
                act.wait_ge(k.prod_a.sem, k.prod_a.at(KC))
                act.activation(norm[:, :, :], k.ps[0:H, 0:2, 0:half], ACT.Sqrt).then_inc(k.a_for_v.sem, 1)

            @block.tensor
            def _(pe):
                for c in range(KC):
                    pe.wait_ge(k.a_for_t.sem, k.a_for_t.at(c + 1))
                    for part in range(2):
                        mm = pe.matmul(k.ps[0:H, part, 0:half], k.square("head_of")[:, c * H:(c + 1) * H],
                                       sqr[:, c % 2, part * half:(part + 1) * half], start=c == 0, stop=c == KC - 1)
                    mm.then_inc(k.prod_a.sem, 1)
                pe.wait_ge(k.loaded[2].sem, k.loaded[2].at(16))
                for c in range(KC):
                    pe.wait_ge(k.v_for_t.sem, k.v_for_t.at(max(1, c - 1)))
                    for part in range(2):
                        mm = pe.matmul(k.ps[:, 2 + c % 3 * 2 + part, 0:half], rows[:, c * P:(c + 1) * P],
                                       norm[:, part, :], start=True, stop=True)
                    mm.then_inc(k.prod_v.sem, 1)
    for n in range(3):
        k.loaded[n].base += 16
    for n in range(2):
        k.stored[n].base += 16
    k.v_for_a.base += KC
    k.a_for_t.base += KC
    k.a_for_v.base += 1
    k.prod_a.base += KC
    k.prod_v.base += KC
    k.v_for_t.base += 1 + KC




def stage_rwkv_scan(k, y):
    nc, t = k.nc, k.t
    HP = D // P
    NG = 2 * HP // HG
    LEVELS = (2, 4, 8, 16, 32)
    BEFORE = {0: ("le", "lt"), 1: ("ge", "gt")}
    with ExitStack() as s:
        def sb(name, shape):
            return k.sb(name, shape, stack=s)

        w2, a2, w0 = sb("w2", [P, D]), sb("a2", [P, D]), sb("w0", [P, D])
        a0h, kah, kar = sb("a0h", [P, 2, KC]), sb("kah", [P, KC]), sb("kar", [P, KC])
        rkk = sb("rkk", [P, 3, KC, P])
        V = sb("V", [P, 2, D])
        hid = sb("hid", [P, 2, 2, P])
        lw = sb("lw", [P, D])
        spare = [k.x[:, 2 * n:2 * n + 2, :].rearrange("p a (c n) -> p (a c) n", n=P) for n in range(4)]
        rate, e_ex, e_in, e_inv = ([sb(name, [P, KC, P])[:, :, :], spare[n]]
                                   for n, name in enumerate(("rate", "e_ex", "e_in", "e_inv")))
        tmp = sb("tmp", [P, KC, P])
        pend = sb("pend", [P, 2, KC, 2])
        tok = sb("tok", [P, 3, D])
        AT, BT, QT, GT, T, TT, X = (sb(n, [P, 2 * HP, P]) for n in ("AT", "BT", "QT", "GT", "T", "TT", "X"))
        bv, ub, tkt = sb("bv", [P, D]), sb("ub", [P, D]), sb("tkt", [P, HP, P])
        N = sb("N", [P, 2, 3, HP * 64])
        kappa, rr, beta, kt = e_ex, e_in, rate, e_inv

        with nc.Block() as block:
            @block.sync
            def _(sp):
                sp.dma_start(w2[:, :], t["rk_w2"][0].rearrange("z r d -> (z r) d")).then_inc(k.loaded[0].sem, 16)
                sp.dma_start(a2[:, :], t["rk_a2"][0].rearrange("z r d -> (z r) d")).then_inc(k.loaded[1].sem, 16)
                sp.wait_ge(k.v_for_t.sem, k.v_for_t.at(1))
                for z in range(2):
                    sp.dma_start(w0[z * 64:z * 64 + 1, :], t["rows"][0:1, z * D:(z + 1) * D]).then_inc(
                        k.loaded[2].sem, 16)
                for n in range(3):
                    sp.wait_ge(k.loaded[n].sem, k.loaded[n].at(16 if n < 2 else 32))

            @block.vector
            def _(dve):
                dve.memset(w0[:, :], 0.0).then_inc(k.v_for_t.sem, 1)
                dve.memset(N[:, :, :, :], 0.0)
                dve.memset(y[:, :, :], 0.0)
                for d in range(2):
                    dve.tensor_scalar(a0h[:, d, :], k.v(f"a0_{d}"), 0.5, None, ALU.mult)
                dve.tensor_scalar(kah[:, :], k.v("k_a"), 0.5, None, ALU.mult)
                dve.tensor_scalar(kar[:, :], k.v("k_a"), -0.5, 1.0, ALU.mult, ALU.add)
        for n in range(3):
            k.loaded[n].base += 16 if n < 2 else 32
        k.v_for_t.base += 1

        PREP = {"prep_t": 2, "prep_a": 3, "prep_v": 3}

        def first_row(i, d, tok0, count):
            return i * (P if d == 0 else -P) + (tok0 if d == 0 else tok0 + (count - 1) * P)

        def two(m):
            return m.rearrange("p (a c) n -> p a (c n)", a=2)

        def load_tile(sp, d, at0, w):
            sp.wait_ge(k.prep_v.sem, w("prep_v", 0))
            sp.sem_inc(k.sp_passed.sem, 1)
            for n, src in enumerate((k.r_d, k.k_d, k.kk_d)):
                sp.dma_start(rkk[:, n, :, :], src[:, :, bass.ds(at0, P)]).then_inc(k.loaded[n].sem, 16)
            sp.dma_start(V[:, d, :], k.v_d[bass.ds(at0, P), :]).then_inc(k.loaded[3 + d].sem, 16)
            sp.dma_start(hid[:, d, :, :], k.hid_d[0:2, :, bass.ds(at0, P)].rearrange("a p n -> p a n")).then_inc(
                k.loaded[5 + d].sem, 16)

        def prep_lora(pe, d, turn):
            lora = slice(d * RK_LORA, (d + 1) * RK_LORA)
            pe.wait_ge(k.loaded[5 + d].sem, turn * 16 + k.loaded[5 + d].at(16))
            for j in range(2):
                cols = slice(j * 512, (j + 1) * 512)
                pe.matmul(k.ps[:, 4 + j, :], hid[lora, d, 0, :], w2[lora, cols], start=True, stop=False)
                pe.matmul(k.ps[:, 4 + j, :], k.square("biasrows")[lora, :], w0[lora, cols], start=False, stop=True)
            for c in range(KC):
                mm = pe.matmul(k.ps[:, 6 + c // 4, c % 4 * P:c % 4 * P + P], a2[lora, c * P:(c + 1) * P],
                               hid[lora, d, 1, :], start=True, stop=True)
            mm.then_inc(k.prep_t.sem, 1)

        def prep_sums(pe, d, w):
            pe.wait_ge(k.prep_v.sem, w("prep_v", 1))
            pe.wait_ge(k.prep_a.sem, w("prep_a", 2))
            for q, mask in zip((4, 6), BEFORE[d]):
                for c in range(KC):
                    mm = pe.matmul(k.ps[:, q + c // 4, c % 4 * P:c % 4 * P + P], lw[:, c * P:(c + 1) * P],
                                   k.square(mask), start=True, stop=True)
            mm.then_inc(k.prep_t.sem, 1)

        def prep_tanh(act, d, w):
            act.wait_ge(k.prep_t.sem, w("prep_t", 1))
            act.activation(lw[:, :].rearrange("p (a b) -> p a b", a=2), k.ps[:, 4:6, :], ACT.Tanh, scale=0.5).then_inc(
                k.prep_a.sem, 1)
            for c in range(KC):
                act.activation(rate[d][:, c, :], k.ps[:, 6 + c // 4, c % 4 * P:c % 4 * P + P], ACT.Tanh,
                               bias=a0h[:, d, c:c + 1], scale=0.5)
            act.drain().then_inc(k.prep_a.sem, 1)

        def prep_exp(act, d, w):
            act.wait_ge(k.prep_t.sem, w("prep_t", 2))
            act.activation(two(e_in[d]), k.ps[:, 4:6, :], ACT.Exp)
            act.activation(two(e_ex[d]), k.ps[:, 6:8, :], ACT.Exp)
            act.activation(two(e_inv[d]), k.ps[:, 4:6, :], ACT.Exp, scale=-1.0)
            act.drain().then_inc(k.prep_a.sem, 1)

        def prep_decay(dve, w):
            dve.wait_ge(k.prep_a.sem, w("prep_a", 1))
            dve.tensor_scalar(lw[:, :], lw[:, :], -0.5 * RK_DECAY_SCALE, -0.5 * RK_DECAY_SCALE,
                              ALU.mult, ALU.add).then_inc(k.prep_v.sem, 1)

        def prep_rates(dve, d, item, w):
            for n in range(3):
                dve.wait_ge(k.loaded[n].sem, item * 16 + k.loaded[n].at(16))
            dve.wait_ge(k.prep_a.sem, w("prep_a", 2))
            kf, kk = rkk[:, 1, :, :], rkk[:, 2, :, :]
            dve.tensor_tensor(tmp[:, :, :], rate[d], chunkwise(kah[:, :], P), ALU.mult)
            dve.drain()
            dve.tensor_tensor(tmp[:, :, :], tmp[:, :, :], chunkwise(kar[:, :], P), ALU.add)
            dve.scalar_tensor_tensor(rate[d], rate[d], 1.0, kk, ALU.add, ALU.mult)
            dve.drain()
            dve.tensor_tensor(tmp[:, :, :], tmp[:, :, :], kf, ALU.mult)
            dve.drain().then_inc(k.prep_v.sem, 1)

        def prep_features(dve, d, w):
            dve.wait_ge(k.prep_a.sem, w("prep_a", 3))
            ends = (63, 127) if d == 0 else (0, 64)
            for c in range(2):
                dve.tensor_copy(pend[:, d, :, c:c + 1], e_in[d][:, :, ends[c]:ends[c] + 1])
            dve.tensor_tensor(kappa[d], e_ex[d], rkk[:, 2, :, :], ALU.mult)
            dve.scalar_tensor_tensor(beta[d], rate[d], 0.5, e_inv[d], ALU.mult, ALU.mult)
            dve.drain()
            dve.tensor_tensor(rr[d], e_in[d], rkk[:, 0, :, :], ALU.mult)
            dve.tensor_tensor(kt[d], e_inv[d], tmp[:, :, :], ALU.mult)
            dve.drain().then_inc(k.prep_v.sem, 1)

        w_first = lambda name, n: k.named[name].at(n)
        with nc.Block() as block:
            @block.sync
            def _(sp):
                load_tile(sp, 0, 0, w_first)

            @block.tensor
            def _(pe):
                prep_lora(pe, 0, 0)
                prep_sums(pe, 0, w_first)

            @block.scalar
            def _(act):
                prep_tanh(act, 0, w_first)
                prep_exp(act, 0, w_first)

            @block.vector
            def _(dve):
                prep_decay(dve, w_first)
                prep_rates(dve, 0, 0, w_first)
                prep_features(dve, 0, w_first)

        def tiles(tok0, count, want_y, final):
            kinds = 4 if want_y else 2
            NB = NG * kinds
            NL = 2 * len(LEVELS) * NG
            LA = NG
            cnt = {
                "prod_a": 1 + LA + 2, "a_for_t": 1 + LA + 2, "v_for_p": NG, "p_for_t": NG,
                "prod_v": NB + NL + 1 + 4 + want_y, "v_for_t": NB + NL + 1 + 4 + want_y,
            }

            def program(engine, body):
                def turn(i, last):
                    for d in range(2):
                        v = lambda name, n: i * (2 * cnt[name]) + k.named[name].at(d * cnt[name] + n)
                        w = lambda name, n: i * (2 * PREP[name]) + k.named[name].at((d + 1) * PREP[name] + n)
                        nxt = None
                        if not (last and d == 1):
                            nxt = (1 - d, first_row(i + d, 1 - d, tok0, count), i + d, i * 2 + (d + 1), w)
                        body(i, d, v, nxt)
                loops = count - 1 if final else count
                with engine.Fori(0, loops) as i:
                    turn(i, False)
                if final:
                    turn(loops, True)

            def heads(g):
                return [2 * (g // 2 * HG + q) + g % 2 for q in range(HG)]

            def slot(h):
                return (h // 2 // HG * 2 + h % 2) * HG + h // 2 % HG

            def half(h):
                return slice(h % 2 * 64, h % 2 * 64 + 64)

            def early(m, b, d):
                return m.rearrange("p (n s b) -> p n s b", s=2, b=b)[:, :, d, :]

            def late(m, b, d):
                return early(m, b, 1 - d)

            with nc.Block() as block:
                @block.sync
                def _(sp):
                    def body(i, d, v, nxt):
                        if nxt:
                            d2, at0, _, _, w = nxt
                            sp.wait_ge(k.v_for_t.sem, v("v_for_t", 0))
                            sp.sem_inc(k.sp_passed.sem, 1)
                            load_tile(sp, d2, at0, w)
                    program(sp, body)

                @block.tensor
                def _(pe):
                    def body(i, d, v, nxt):
                        prepared = i * (2 * PREP["prep_v"]) + k.prep_v.at((d + 1) * PREP["prep_v"])
                        pe.wait_ge(k.prep_v.sem, prepared)
                        pe.wait_ge(k.v_for_t.sem, v("v_for_t", 0))
                        for n, m in enumerate((beta[d], kt[d], kappa[d])):
                            for c in range(KC):
                                mm = pe.transpose(k.ps[:, 2 * n + c // 4, c % 4 * P:c % 4 * P + P], m[:, c, :],
                                                  k.square("ident"))
                        mm.then_inc(k.prod_a.sem, 1)
                        n = 0
                        for g in range(NG):
                            pairs = [(beta[d], kappa[d]), (kt[d], kappa[d]), (beta[d], rr[d]), (kt[d], rr[d])][:kinds]
                            for left, right in pairs:
                                bank = (6 + n) % 8
                                if n == 2:
                                    pe.wait_ge(k.a_for_t.sem, v("a_for_t", 1))
                                if n >= 8:
                                    pe.wait_ge(k.v_for_t.sem, v("v_for_t", n - 7))
                                for q, h in enumerate(heads(g)):
                                    mm = pe.matmul(k.ps[:, bank, q * P:(q + 1) * P], left[half(h), h // 2, :],
                                                   right[half(h), h // 2, :], start=True, stop=True)
                                mm.then_inc(k.prod_v.sem, 1)
                                n += 1

                        pe.wait_ge(k.v_for_t.sem, v("v_for_t", NB))
                        for g in range(NG):
                            pe.wait_ge(k.p_for_t.sem, v("p_for_t", g + 1))
                            for q, h in enumerate(heads(g)):
                                mm = pe.transpose(k.ps[:, g, q * P:(q + 1) * P], TT[:, slot(h), :], k.square("ident"))
                            mm.then_inc(k.prod_a.sem, 1)
                        for l, b in enumerate(LEVELS):
                            l0 = NB + 2 * NG * l
                            for g in range(NG):
                                if l == 0:
                                    pe.wait_ge(k.a_for_t.sem, v("a_for_t", 1 + g + 1))
                                else:
                                    pe.wait_ge(k.v_for_t.sem, v("v_for_t", l0 - NG + g + 1))
                                for q, h in enumerate(heads(g)):
                                    mm = pe.matmul(k.ps[:, g, q * P:(q + 1) * P], AT[:, slot(h), :], T[:, slot(h), :],
                                                   start=True, stop=True)
                                mm.then_inc(k.prod_v.sem, 1)
                            for g in range(NG):
                                pe.wait_ge(k.v_for_t.sem, v("v_for_t", l0 + g + 1))
                                for q, h in enumerate(heads(g)):
                                    if b != LEVELS[-1]:
                                        pe.matmul(k.ps[:, g, q * 64:(q + 1) * 64], TT[:, slot(h), :],
                                                  early(X[:, slot(h), :], b, d), start=True, stop=True)
                                    mm = pe.matmul(k.ps[:, g, 256 + q * 64:256 + (q + 1) * 64], X[:, slot(h), :],
                                                   late(TT[:, slot(h), :], b, d), start=True, stop=True)
                                mm.then_inc(k.prod_v.sem, 1)
                            if nxt and l == 0:
                                prep_lora(pe, nxt[0], nxt[2])
                            if nxt and l == 2:
                                prep_sums(pe, nxt[0], nxt[4])
                        done = NB + NL
                        pe.wait_ge(k.loaded[3 + d].sem, i * 16 + k.loaded[3 + d].at(16))
                        pe.wait_ge(k.v_for_t.sem, v("v_for_t", done))
                        for h in range(2 * HP):
                            mm = pe.matmul(k.ps[:, h // 8, h % 8 * 64:h % 8 * 64 + 64], BT[:, slot(h), :],
                                           V[:, d, h * 64:(h + 1) * 64], start=True, stop=True)
                        mm.then_inc(k.prod_a.sem, 1)
                        for h in range(2 * HP):
                            c = h // 2
                            mm = pe.matmul(k.ps[half(h), 2 + c // 4, c % 4 * P:c % 4 * P + P],
                                           tok[:, 2, h * 64:(h + 1) * 64], TT[:, slot(h), :], start=True, stop=True)
                        mm.then_inc(k.prod_a.sem, 1)
                        pe.wait_ge(k.a_for_t.sem, v("a_for_t", 1 + LA + 1))
                        if nxt:
                            pe.wait_ge(k.prep_a.sem, nxt[4]("prep_a", 3))
                        for h in range(2 * HP):
                            mm = pe.matmul(k.ps[:, 4 + h // 8, h % 8 * 64:h % 8 * 64 + 64], TT[:, slot(h), :],
                                           bv[:, h * 64:(h + 1) * 64], start=True, stop=True)
                        mm.then_inc(k.prod_v.sem, 1)

                        chunk = lambda step: step if d == 0 else 1 - step
                        of_chunk = lambda step: slice(chunk(step) * 64, chunk(step) * 64 + 64)

                        def from_state(step):
                            for h in range(2 * HP):
                                mm = pe.matmul(k.ps[of_chunk(step), 6 + h % 2, h // 2 * 64:h // 2 * 64 + 64],
                                               tkt[half(h), h // 2, of_chunk(step)],
                                               N[half(h), d, step, h // 2 * 64:h // 2 * 64 + 64], start=True, stop=True)
                            mm.then_inc(k.prod_v.sem, 1)

                        def old(bank, m):
                            pe.matmul(k.ps[:, bank, :], k.square("ident"), m, start=True, stop=False)

                        def to_state(step, m, part):
                            r = of_chunk(step)
                            for h in range(2 * HP):
                                cols = slice(h * 64, (h + 1) * 64)
                                mm = pe.matmul(k.ps[half(h), step, h // 2 * 64:h // 2 * 64 + 64], tok[r, part, cols],
                                               m[r, cols], start=False, stop=part == 0 and h >= 2 * HP - 2)
                            return mm

                        def output_of(h):
                            return k.ps[half(h), 2 + h // 2 // 4, h // 2 % 4 * P:h // 2 % 4 * P + P]

                        pe.wait_ge(k.a_for_t.sem, v("a_for_t", 1 + LA + 2))
                        for step in range(2):
                            if step:
                                pe.wait_ge(k.v_for_t.sem, v("v_for_t", done + 3))
                            pe.sem_inc(k.passed.sem, 1)
                            from_state(step)
                            old(step, N[:, d, step, :])
                            to_state(step, V[:, d, :], 1)
                            pe.wait_ge(k.v_for_t.sem, v("v_for_t", done + 2 + 2 * step))
                            pe.sem_inc(k.passed.sem, 1)
                            to_state(step, ub, 0).then_inc(k.prod_v.sem, 1)
                            if want_y and step == 0:
                                for b in range(2):
                                    old(2 + b, y[:, 4 * b:4 * b + 4, bass.ds(first_row(i, d, tok0 - CTX, count), P)])
                        if want_y:
                            for h in range(2 * HP):
                                o = output_of(h)
                                pe.matmul(o, V[:, d, h * 64:(h + 1) * 64], GT[:, slot(h), :], start=False, stop=False)
                                pe.matmul(o, ub[:, h * 64:(h + 1) * 64], QT[:, slot(h), :], start=False, stop=False)
                                for step in range(2):
                                    mm = pe.matmul(o[:, of_chunk(step)], N[half(h), d, step, h // 2 * 64:h // 2 * 64 + 64],
                                                   rr[d][half(h), h // 2, of_chunk(step)], start=False,
                                                   stop=step == 1 and h % 8 >= 6)
                            mm.then_inc(k.prod_v.sem, 1)
                    program(pe, body)

                @block.scalar
                def _(act):
                    def body(i, d, v, nxt):
                        e = 0

                        def taken(dst, src, f=ACT.Copy, scale=1.0):
                            nonlocal e
                            act.wait_ge(k.prod_a.sem, v("prod_a", e + 1))
                            act.activation(dst, src, f, scale=scale).then_inc(k.a_for_t.sem, 1)
                            e += 1

                        act.wait_ge(k.prod_a.sem, v("prod_a", 1))
                        for n in range(3):
                            act.activation(tok[:, n, :].rearrange("p (a b) -> p a b", a=2), k.ps[:, 2 * n:2 * n + 2, :],
                                           ACT.Copy, scale=-1.0 if n == 0 else 1.0)
                        act.drain().then_inc(k.a_for_t.sem, 1)
                        e = 1
                        bank = lambda g: k.ps[:, g, :].rearrange("p (a b) -> p a b", a=HG)
                        for g in range(NG):
                            taken(T[:, g * HG:(g + 1) * HG, :], bank(g))
                        if nxt:
                            prep_tanh(act, nxt[0], nxt[4])
                            prep_exp(act, nxt[0], nxt[4])
                        taken(bv[:, :].rearrange("p (a b) -> p a b", a=2), k.ps[:, 0:2, :])
                        taken(two(tkt[:, :, :]), k.ps[:, 2:4, :])
                    program(act, body)

                @block.gpsimd
                def _(pool):
                    def body(i, d, v, nxt):
                        for g in range(NG):
                            four = slice(g * HG, (g + 1) * HG)
                            pool.wait_ge(k.v_for_p.sem, v("v_for_p", g + 1))
                            pool.tensor_tensor(TT[:, four, :], AT[:, four, :],
                                               k.square(f"off1_{d}").unsqueeze(1).to_broadcast([P, HG, P]), ALU.mult)
                            pool.drain()
                            pool.tensor_tensor(TT[:, four, :], k.square("ident").unsqueeze(1).to_broadcast([P, HG, P]),
                                               TT[:, four, :], ALU.subtract).then_inc(k.p_for_t.sem, 1)
                    program(pool, body)

                @block.vector
                def _(dve):
                    def body(i, d, v, nxt):
                        incl, strict = BEFORE[d]
                        four = lambda m, g: m[:, g * HG:(g + 1) * HG, :]
                        wide = lambda name: k.square(name).unsqueeze(1).to_broadcast([P, HG, P])
                        bank4 = lambda b: k.ps[:, b, :].rearrange("p (a b) -> p a b", a=HG)
                        dve.tensor_copy(N[:, d, 0, :], N[:, d, 2, :])
                        n = 0
                        for g in range(NG):
                            for kind in range(kinds):
                                bank = bank4((6 + n) % 8)
                                dve.wait_ge(k.prod_v.sem, v("prod_v", n + 1))
                                if kind == 0:
                                    dve.tensor_tensor(four(AT, g), bank, wide(strict), ALU.mult)
                                    dve.drain().then_inc(k.v_for_p.sem, 1)
                                elif kind == 1:
                                    dve.tensor_tensor(four(BT, g), bank, wide(strict), ALU.mult)
                                elif kind == 2:
                                    dve.scalar_tensor_tensor(four(QT, g), bank, -1.0, wide(incl), ALU.mult, ALU.mult)
                                else:
                                    dve.tensor_tensor(four(GT, g), bank, wide(incl), ALU.mult)
                                dve.drain().then_inc(k.v_for_t.sem, 1)
                                n += 1
                        for l, b in enumerate(LEVELS):
                            l0 = NB + 2 * NG * l
                            for g in range(NG):
                                dve.wait_ge(k.prod_v.sem, v("prod_v", l0 + g + 1))
                                dve.tensor_tensor(four(X, g), bank4(g), wide(f"off{b}_{1 - d}"), ALU.mult).then_inc(
                                    k.v_for_t.sem, 1)
                            for g in range(NG):
                                dve.wait_ge(k.prod_v.sem, v("prod_v", l0 + NG + g + 1))
                                for m, side, at0 in ((T, d, 0), (TT, 1 - d, 256)):
                                    if m is T and b == LEVELS[-1]:
                                        continue
                                    cols = four(m, g).rearrange("p h (n s b) -> p h n s b", s=2, b=b)[:, :, :, side, :]
                                    change = k.ps[:, g, at0:at0 + 256].rearrange("p (h n b) -> p h n b", h=HG, b=b)
                                    ins = dve.tensor_tensor(cols, cols, change, ALU.subtract)
                                ins.then_inc(k.v_for_t.sem, 1)
                            if nxt and l == 1:
                                prep_decay(dve, nxt[4])
                            if nxt and l == 2:
                                prep_rates(dve, nxt[0], nxt[3], nxt[4])
                        e = NB + NL
                        if nxt:
                            prep_features(dve, nxt[0], nxt[4])
                        dve.wait_ge(k.prod_v.sem, v("prod_v", e + 1))
                        dve.tensor_copy(ub[:, :].rearrange("p (a b) -> p a b", a=2), k.ps[:, 4:6, :])
                        dve.drain().then_inc(k.v_for_t.sem, 1)
                        for step in range(2):
                            c = step if d == 0 else 1 - step
                            rows = slice(c * 64, c * 64 + 64)
                            dve.wait_ge(k.prod_v.sem, v("prod_v", e + 2 + 2 * step))
                            u = ub[rows, :].rearrange("p (c a b) -> p a c b", a=2, b=64)
                            dve.tensor_tensor(u, u, k.ps[rows, 6:8, :].rearrange("p a (c b) -> p a c b", b=64), ALU.add)
                            dve.drain().then_inc(k.v_for_t.sem, 1)
                            dve.wait_ge(k.prod_v.sem, v("prod_v", e + 3 + 2 * step))
                            dve.tensor_tensor(N[:, d, step + 1, :].rearrange("p (a b) -> p a b", a=HP),
                                              k.ps[:, step, :].rearrange("p (a b) -> p a b", a=HP),
                                              pend[:, d, :, c:c + 1].to_broadcast([P, HP, 64]), ALU.mult)
                            dve.drain().then_inc(k.v_for_t.sem, 1)
                        if want_y:
                            dve.wait_ge(k.prod_v.sem, v("prod_v", cnt["prod_v"]))
                            yt = y[:, :, bass.ds(first_row(i, d, tok0 - CTX, count), P)]
                            dve.tensor_copy(yt, k.ps[:, 2:4, :].rearrange("p a (c n) -> p (a c) n", n=P))
                            dve.drain().then_inc(k.v_for_t.sem, 1)
                    program(dve, body)
            for name, n in cnt.items():
                k.named[name].base += 2 * count * n
            for name, n in PREP.items():
                k.named[name].base += 2 * count * n
            for n in range(3):
                k.loaded[n].base += 32 * count
            for n in range(3, 7):
                k.loaded[n].base += 16 * count

        tiles(0, CTX // P, False, False)
        tiles(CTX, NT, True, True)


def load_projection(k, sp, wb, w):
    for j in range(2):
        sp.dma_start(wb[:, j, :, :], w[0].rearrange("(c p) n -> p c n", p=P)[:, :, j * 512:(j + 1) * 512]).then_inc(
            k.landed[j].sem, 16)


def stage_rwkv_out(k, y, wb, w):
    nc, t = k.nc, k.t
    H = D // RK_HEAD
    with ExitStack() as s:
        def sb(name, shape):
            return k.sb(name, shape, stack=s)

        r, kf, v = sb("o_r", [P, KC, SEQ]), sb("o_k", [P, KC, SEQ]), sb("o_v", [P, NT, D])
        a2, g2, hid = sb("o_a2", [P, D]), sb("o_g2", [P, D]), sb("o_hid", [P, 2, SEQ])
        a0h, kah, kar = sb("o_a0h", [P, 2, KC]), sb("o_kah", [P, KC]), sb("o_kar", [P, KC])
        rate = sb("o_rate", [P, 2, 2, SEQ])
        vt, sqr = (sb(n, [P, 2, SEQ]) for n in ("o_vt", "o_sqr"))
        rows, rstd = sb("o_rows", [H, D]), sb("o_rstd", [H, SEQ])
        lat = slice(CTX, TOK)
        with nc.Block() as block:
            @block.sync
            def _(sp):
                sp.dma_start(hid[:, :, :], k.hid_d[1:3, :, lat].rearrange("a p n -> p a n")).then_inc(
                    k.loaded[5].sem, 16)
                sp.dma_start(a2[:, :], t["rk_a2"][0].rearrange("z r d -> (z r) d")).then_inc(k.loaded[3].sem, 16)
                sp.dma_start(rows[:, :], t["head_rows"]).then_inc(k.loaded[7].sem, 16)
                sp.dma_start(r[:, :, :], k.r_d[:, :, lat]).then_inc(k.loaded[0].sem, 16)
                sp.dma_start(kf[:, :, :], k.k_d[:, :, lat]).then_inc(k.loaded[1].sem, 16)
                sp.dma_start(v[:, :, :], k.v_d[lat, :].rearrange("(t p) d -> p t d", p=P)).then_inc(k.loaded[2].sem, 16)
                sp.dma_start(g2[:, :], t["rk_g2"][0]).then_inc(k.loaded[4].sem, 16)
                sp.dma_start(k.x[:, :, :], t["xT"][:, :, lat]).then_inc(k.loaded[6].sem, 16)
                load_projection(k, sp, wb, w)
                sp.wait_ge(k.loaded[6].sem, k.loaded[6].at(16))

            @block.gpsimd
            def _(pool):
                for n in (0, 1):
                    pool.wait_ge(k.loaded[n].sem, k.loaded[n].at(16))
                for c in range(KC):
                    pool.tensor_tensor(r[:, c, :], r[:, c, :], kf[:, c, :], ALU.mult).then_inc(k.p_for_v.sem, 1)

            @block.vector
            def _(dve):
                for d in range(2):
                    dve.tensor_scalar(a0h[:, d, :], k.v(f"a0_{d}"), 0.5, None, ALU.mult)
                dve.tensor_scalar(kah[:, :], k.v("k_a"), 0.5, None, ALU.mult)
                dve.tensor_scalar(kar[:, :], k.v("k_a"), -1.0, 2.0, ALU.mult, ALU.add)
                dve.drain()
                dve.tensor_tensor(kah[:, :], kah[:, :], k.v("r_k"), ALU.mult)
                dve.tensor_tensor(kar[:, :], kar[:, :], k.v("r_k"), ALU.mult)
                dve.wait_ge(k.loaded[5].sem, k.loaded[5].at(16))
                dve.tensor_scalar(hid[:, 1, :], hid[:, 1, :], 0.5, 0.5, ALU.mult, ALU.add)
                dve.drain().then_inc(k.v_for_t.sem, 1)
                for c in range(KC):
                    dve.wait_ge(k.prod_v.sem, k.prod_v.at(c + 1))
                    dve.scalar_tensor_tensor(y[:, c, :], k.ps[:, c % 2, :], -1.0 / RK_HEAD, y[:, c, :], ALU.mult,
                                             ALU.add).then_inc(k.v_for_a.sem, 1)
                dve.wait_ge(k.a_for_v.sem, k.a_for_v.at(1))
                dve.reciprocal(rstd[:, :], rstd[:, :])
                dve.drain().then_inc(k.v_for_t.sem, 1)

                def bonus_parts(c):
                    j = c % 2
                    dve.wait_ge(k.a_for_v.sem, k.a_for_v.at(1 + 2 * c + 1))
                    dve.tensor_tensor(rate[:, j, 0, :], rate[:, j, 0, :], rate[:, j, 1, :], ALU.add)
                    dve.drain()
                    dve.tensor_scalar(rate[:, j, 0, :], rate[:, j, 0, :], kah[:, c:c + 1], kar[:, c:c + 1],
                                      ALU.mult, ALU.add)
                    dve.drain()
                    dve.wait_ge(k.p_for_v.sem, k.p_for_v.at(c + 1))
                    dve.tensor_tensor(r[:, c, :], r[:, c, :], rate[:, j, 0, :], ALU.mult).then_inc(k.v_for_t.sem, 1)

                bonus_parts(0)
                for c in range(KC):
                    if c + 1 < KC:
                        bonus_parts(c + 1)
                    dve.wait_ge(k.a_for_v.sem, k.a_for_v.at(1 + 2 * c + 2))
                    dve.wait_ge(k.prod_v.sem, k.prod_v.at(KC + c + 1))
                    dve.tensor_tensor(kf[:, c, :], vt[:, c % 2, :], k.ps[:, c % 2, :], ALU.mult).then_inc(
                        k.v_for_a.sem, 1)
                for c in range(KC):
                    dve.wait_ge(k.prod_v.sem, k.prod_v.at(2 * KC + c + 1))
                    dve.tensor_tensor(y[:, c, :], y[:, c, :], k.ps[:, 2 + c % 2, :], ALU.mult)
                    dve.drain()
                    dve.tensor_scalar(y[:, c, :], y[:, c, :], k.v("lnx_g")[:, c:c + 1], k.v("lnx_b")[:, c:c + 1],
                                      ALU.mult, ALU.add)
                    dve.drain()
                    dve.tensor_tensor(y[:, c, :], y[:, c, :], kf[:, c, :], ALU.add)
                    dve.drain()
                    dve.tensor_tensor(y[:, c, :], y[:, c, :], k.ps[:, 4 + c % 2, :], ALU.mult).then_inc(
                        k.v_for_t.sem, 1)

            @block.scalar
            def _(act):
                for c in range(KC):
                    act.wait_ge(k.v_for_a.sem, k.v_for_a.at(c + 1))
                    act.wait_ge(k.prod_a.sem, k.prod_a.at(c - 1))
                    act.activation(sqr[:, c % 2, :], y[:, c, :], ACT.Square).then_inc(k.a_for_t.sem, 1)
                act.wait_ge(k.prod_a.sem, k.prod_a.at(KC))
                act.activation(rstd[:, :], k.ps[0:H, 2, :], ACT.Sqrt, scale=1.0 / RK_HEAD,
                               bias=k.eps[0:H, 0:1]).then_inc(k.a_for_v.sem, 1)
                for c in range(KC):
                    j = c % 2
                    act.wait_ge(k.v_for_a.sem, k.v_for_a.at(KC + c - 1))
                    act.wait_ge(k.prod_a.sem, k.prod_a.at(KC + 2 * c + 1))
                    for d in range(2):
                        act.activation(rate[:, j, d, :], k.ps[:, 4 + d, :], ACT.Tanh, bias=a0h[:, d, c:c + 1], scale=0.5)
                    act.drain().then_inc(k.a_for_v.sem, 1)
                    act.wait_ge(k.prod_a.sem, k.prod_a.at(KC + 2 * c + 2))
                    act.activation(vt[:, j, :], k.ps[:, 6 + j, :], ACT.Copy).then_inc(k.a_for_v.sem, 1)

            @block.tensor
            def _(pe):
                def mean(c):
                    pe.wait_ge(k.v_for_a.sem, k.v_for_a.at(c - 1))
                    pe.matmul(k.ps[:, c % 2, :], k.square("headones"), y[:, c, :], start=True, stop=True).then_inc(
                        k.prod_v.sem, 1)

                mean(0)
                mean(1)
                for c in range(KC):
                    pe.wait_ge(k.a_for_t.sem, k.a_for_t.at(c + 1))
                    pe.matmul(k.ps[0:H, 2, :], k.square("head_of")[:, c * H:(c + 1) * H], sqr[:, c % 2, :],
                              start=c == 0, stop=c == KC - 1).then_inc(k.prod_a.sem, 1)
                    if c + 2 < KC:
                        mean(c + 2)

                def rates_and_v(c):
                    cols = slice(c * P, (c + 1) * P)
                    pe.wait_ge(k.a_for_v.sem, k.a_for_v.at(1 + 2 * c))
                    for d in range(2):
                        lora = slice(d * RK_LORA, (d + 1) * RK_LORA)
                        mm = pe.matmul(k.ps[:, 4 + d, :], a2[lora, cols], hid[lora, 0, :], start=True, stop=True)
                    mm.then_inc(k.prod_a.sem, 1)
                    for q in range(NT):
                        mm = pe.transpose(k.ps[:, 6 + c % 2, q * P:(q + 1) * P], v[:, q, cols], k.square("ident"))
                    mm.then_inc(k.prod_a.sem, 1)

                pe.wait_ge(k.v_for_t.sem, k.v_for_t.at(1))
                for n in (2, 3, 4, 7):
                    pe.wait_ge(k.loaded[n].sem, k.loaded[n].at(16))
                rates_and_v(0)
                for c in range(KC):
                    if c + 1 < KC:
                        rates_and_v(c + 1)
                    pe.wait_ge(k.v_for_t.sem, k.v_for_t.at(2 + c + 1))
                    pe.wait_ge(k.v_for_a.sem, k.v_for_a.at(KC + c - 1))
                    pe.matmul(k.ps[:, c % 2, :], k.square("headones"), r[:, c, :], start=True, stop=True).then_inc(
                        k.prod_v.sem, 1)
                pe.wait_ge(k.a_for_v.sem, k.a_for_v.at(1 + 2 * KC))
                for c in range(KC):
                    cols = slice(c * P, (c + 1) * P)
                    pe.wait_ge(k.v_for_t.sem, k.v_for_t.at(2 + KC + c - 1))
                    pe.matmul(k.ps[:, 2 + c % 2, :], rows[:, cols], rstd[:, :], start=True, stop=True)
                    pe.matmul(k.ps[:, 4 + c % 2, :], g2[:, cols], hid[:, 1, :], start=True, stop=True).then_inc(
                        k.prod_v.sem, 1)
    for n in range(8):
        k.loaded[n].base += 16
    k.prod_a.base += 3 * KC
    k.prod_v.base += 3 * KC
    k.a_for_v.base += 1 + 2 * KC
    k.a_for_t.base += KC
    k.v_for_t.base += 2 + 2 * KC
    k.v_for_a.base += 2 * KC
    k.p_for_v.base += KC


def stage_project_residual(k, wb, z, gate, alpha=DN_ALPHA):
    with k.nc.Block() as block:
        @block.tensor
        def _(pe):
            for o in range(KC):
                if o % 4 == 0:
                    pe.wait_ge(k.landed[o // 4].sem, k.landed[o // 4].at(16))
                for c in range(KC):
                    mm = pe.matmul(k.ps[:, o, :], wb[:, o // 4, c, o % 4 * P:o % 4 * P + P], z[:, c, :],
                                   start=c == 0, stop=c == KC - 1)
                mm.then_inc(k.prod_v.sem, 1)

        @block.vector
        def _(dve):
            if alpha != 1.0:
                dve.tensor_scalar(k.x[:, :, :], k.x[:, :, :], alpha, None, ALU.mult)
                dve.drain()
            for o in range(KC):
                dve.wait_ge(k.prod_v.sem, k.prod_v.at(o + 1))
                x = k.x[:, o, :]
                if gate is None:
                    dve.tensor_tensor(x, k.ps[:, o, :], x, ALU.add)
                else:
                    dve.scalar_tensor_tensor(x, k.ps[:, o, :], gate[:, o:o + 1], x, ALU.mult, ALU.add)
    k.prod_v.base += KC
    for j in range(2):
        k.landed[j].base += 16


def stage_layer_norm(k, i, j):
    g, b = k.v(f"ln_g{i}{j}"), k.v(f"ln_b{i}{j}")
    with ExitStack() as s:
        sqr = k.sb(f"ln_sq{i}{j}", [P, KC, SEQ], stack=s)
        mean, rstd = k.sb(f"ln_m{i}{j}", [P, SEQ], stack=s), k.sb(f"ln_r{i}{j}", [P, SEQ], stack=s)
        with k.nc.Block() as block:
            @block.tensor
            def _(pe):
                for c in range(KC):
                    mm = pe.matmul(k.ps[:, 0, :], k.square("ones"), k.x[:, c, :], start=c == 0, stop=c == KC - 1)
                mm.then_inc(k.prod_v.sem, 1)
                for c in range(KC):
                    pe.wait_ge(k.a_for_t.sem, k.a_for_t.at(c + 1))
                    mm = pe.matmul(k.ps[:, 1, :], k.square("ones"), sqr[:, c, :], start=c == 0, stop=c == KC - 1)
                mm.then_inc(k.prod_a.sem, 1)

            @block.vector
            def _(dve):
                dve.wait_ge(k.prod_v.sem, k.prod_v.at(1))
                dve.tensor_scalar(mean[:, :], k.ps[:, 0, :], 1.0 / D, None, ALU.mult)
                dve.drain()
                for c in range(KC):
                    dve.tensor_tensor(k.x[:, c, :], k.x[:, c, :], mean[:, :], ALU.subtract).then_inc(k.v_for_a.sem, 1)
                dve.wait_ge(k.a_for_v.sem, k.a_for_v.at(1))
                dve.reciprocal(rstd[:, :], rstd[:, :])
                dve.drain()
                for c in range(KC):
                    dve.tensor_tensor(k.x[:, c, :], k.x[:, c, :], rstd[:, :], ALU.mult).then_inc(k.v_for_a.sem, 1)

            @block.scalar
            def _(act):
                for c in range(KC):
                    act.wait_ge(k.v_for_a.sem, k.v_for_a.at(c + 1))
                    act.activation(sqr[:, c, :], k.x[:, c, :], ACT.Square).then_inc(k.a_for_t.sem, 1)
                act.wait_ge(k.prod_a.sem, k.prod_a.at(1))
                act.activation(rstd[:, :], k.ps[:, 1, :], ACT.Sqrt, scale=1.0 / D, bias=k.eps[:, 1:2])
                act.drain().then_inc(k.a_for_v.sem, 1)
                for c in range(KC):
                    act.wait_ge(k.v_for_a.sem, k.v_for_a.at(KC + c + 1))
                    act.activation(k.x[:, c, :], k.x[:, c, :], ACT.Identity, scale=g[:, c:c + 1], bias=b[:, c:c + 1])
    k.prod_v.base += 1
    k.prod_a.base += 1
    k.v_for_a.base += 2 * KC
    k.a_for_t.base += KC
    k.a_for_v.base += 1


def stage_modulate(k, dst, layer, part):
    with k.nc.Block() as block:
        @block.vector
        def _(dve):
            for c in range(KC):
                dve.tensor_scalar(dst[:, c, :], k.x[:, c, :], k.mod[:, layer, (part + 1) * KC + c, 0:1],
                                  k.mod[:, layer, part * KC + c, 0:1], ALU.mult, ALU.add)


def stage_ffn(k):
    nc, t = k.nc, k.t
    width = 2 * P
    pieces = D_FF // width
    FC = D_FF // P
    with ExitStack() as s:
        g = k.sb("ffn_g", [P, FC, SEQ], stack=s)
        with ExitStack() as s1:
            h = k.sb("ffn_h", [P, KC, SEQ], stack=s1)
            wb = k.sb("ffn_wb", [P, 2, 2, KC, width], stack=s1)
            th = k.sb("ffn_th", [P, 2, SEQ], stack=s1)
            stage_modulate(k, h, 0, 3)
            with nc.Block() as block:
                w13 = [t[n][0].rearrange("(c p) n -> p c n", p=P) for n in ("ffn_w1", "ffn_w3")]

                @block.sync
                def _(sp):
                    def piece(i, j):
                        sp.wait_ge(k.prod_a.sem, i * 4 + k.prod_a.at(2 * (j - 1)))
                        for q in range(2):
                            sp.dma_start(wb[:, j, q, :, :], w13[q][:, :, bass.ds(i * (2 * width) + j * width, width)])\
                                .then_inc(k.landed[2 * j + q].sem, 16)
                    with sp.Fori(0, pieces // 2) as i:
                        piece(i, 0)
                        piece(i, 1)
                    piece(pieces // 2, 0)

                @block.tensor
                def _(pe):
                    def piece(i, j):
                        for q in range(2):
                            pe.wait_ge(k.landed[2 * j + q].sem, i * 16 + k.landed[2 * j + q].at(16))
                        for o in range(2):
                            e = 2 * j + o
                            bank = 2 * (e % 4)
                            pe.wait_ge(k.free_v.sem, i * 4 + k.free_v.at(e - 3))
                            for q in range(2):
                                for c in range(KC):
                                    mm = pe.matmul(k.ps[:, bank + q, :], wb[:, j, q, c, o * P:(o + 1) * P], h[:, c, :],
                                                   start=c == 0, stop=c == KC - 1)
                            mm.then_inc(k.prod_a.sem, 1)
                    with pe.Fori(0, pieces // 2) as i:
                        piece(i, 0)
                        piece(i, 1)
                    piece(pieces // 2, 0)

                @block.scalar
                def _(act):
                    def chunk(i, e):
                        act.wait_ge(k.prod_a.sem, i * 4 + k.prod_a.at(e + 1))
                        act.wait_ge(k.free_v.sem, i * 4 + k.free_v.at(e - 1))
                        act.activation(th[:, e % 2, :], k.ps[:, 2 * (e % 4), :], ACT.Tanh, scale=0.5).then_inc(
                            k.a_for_v.sem, 1)
                    with act.Fori(0, pieces // 2) as i:
                        for e in range(4):
                            chunk(i, e)
                    for e in range(2):
                        chunk(pieces // 2, e)

                @block.vector
                def _(dve):
                    def chunk(i, e):
                        dst = g[:, bass.ds(i * 4 + e, 1), :].rearrange("p a n -> p (a n)")
                        bank = 2 * (e % 4)
                        dve.wait_ge(k.a_for_v.sem, i * 4 + k.a_for_v.at(e + 1))
                        dve.scalar_tensor_tensor(th[:, e % 2, :], th[:, e % 2, :], 1.0, k.ps[:, bank, :], ALU.add, ALU.mult)
                        dve.drain()
                        dve.scalar_tensor_tensor(dst, th[:, e % 2, :], 0.5, k.ps[:, bank + 1, :], ALU.mult, ALU.mult)\
                            .then_inc(k.free_v.sem, 1)
                    with dve.Fori(0, pieces // 2) as i:
                        for e in range(4):
                            chunk(i, e)
                    for e in range(2):
                        chunk(pieces // 2, e)
            k.prod_a.base += FC
            k.free_v.base += FC
            k.a_for_v.base += FC
            for j in range(2):
                for q in range(2):
                    k.landed[2 * j + q].base += 16 * ((pieces + 1 - j) // 2)
        wd = k.sb("ffn_wd", [P, 4, FC, P], stack=s)
        with nc.Block() as block:
            src = t["ffn_w2"][0].rearrange("(c p) n -> p c n", p=P)

            @block.sync
            def _(sp):
                with sp.Fori(0, KC // 4) as i:
                    for j in range(4):
                        sp.wait_ge(k.prod_v.sem, i * 4 + k.prod_v.at(j - 3))
                        sp.dma_start(wd[:, j, :, :], src[:, :, bass.ds(i * (4 * P) + j * P, P)]).then_inc(
                            k.landed[j].sem, 16)

            @block.tensor
            def _(pe):
                with pe.Fori(0, KC // 4) as i:
                    for j in range(4):
                        pe.wait_ge(k.landed[j].sem, i * 16 + k.landed[j].at(16))
                        pe.wait_ge(k.free_v.sem, i * 4 + k.free_v.at(j - 3))
                        for c in range(FC):
                            mm = pe.matmul(k.ps[:, j, :], wd[:, j, c, :], g[:, c, :], start=c == 0, stop=c == FC - 1)
                        mm.then_inc(k.prod_v.sem, 1)

            @block.vector
            def _(dve):
                dve.tensor_scalar(k.x[:, :, :], k.x[:, :, :], DN_ALPHA, None, ALU.mult)
                dve.drain()
                gate = k.mod[:, 0, 5 * KC:6 * KC, 0]
                with dve.Fori(0, KC // 4) as i:
                    for j in range(4):
                        o = i * 4 + j
                        x = k.x[:, bass.ds(o, 1), :].rearrange("p a n -> p (a n)")
                        dve.wait_ge(k.prod_v.sem, i * 4 + k.prod_v.at(j + 1))
                        dve.scalar_tensor_tensor(x, k.ps[:, j, :], gate[:, bass.ds(o, 1)], x, ALU.mult, ALU.add)\
                            .then_inc(k.free_v.sem, 1)
        k.prod_v.base += KC
        k.free_v.base += KC
        for j in range(4):
            k.landed[j].base += 16 * KC // 4


def stage_pool(k):
    nc, t = k.nc, k.t
    PAD = max(POOL_WINDOWS) // 2
    W = GRID_W + 2 * PAD
    GC = KC // len(POOL_WINDOWS)
    with ExitStack() as s:
        def sb(name, shape):
            return k.sb(name, shape, stack=s)

        h = sb("pl_h", [P, KC, SEQ])
        inv = sb("pl_inv", [P, len(POOL_WINDOWS), GRID_W])
        wp = sb("pl_w", [P, len(POOL_WINDOWS), GC, GC * P])
        gate = sb("pl_gate", [P, KC])
        pad = [sb(f"pl_{n}", [P, GC * ROWS, W]) for n in range(3)]
        stage_modulate(k, h, 1, 0)
        with nc.Block() as block:
            @block.sync
            def _(sp):
                sp.dma_start(inv[:, :, :].rearrange("p a b -> p (a b)"), t["pool_counts"]).then_inc(k.loaded[0].sem, 16)
                for g in range(len(POOL_WINDOWS)):
                    sp.dma_start(wp[:, g, :, :], t["pool_w"][0, g].rearrange("(c p) n -> p c n", p=P)).then_inc(
                        k.loaded[1].sem, 16)

            @block.vector
            def _(dve):
                dve.tensor_tensor(gate[:, :], k.mod[:, 1, 2 * KC:3 * KC, 0], k.v("pool_scale"), ALU.mult)
                dve.tensor_scalar(k.x[:, :, :], k.x[:, :, :], DN_ALPHA, None, ALU.mult)
                dve.memset(pad[0][:, :, :], 0.0)
                dve.wait_ge(k.loaded[0].sem, k.loaded[0].at(16))
                dve.drain()
                for g, window in enumerate(POOL_WINDOWS):
                    own = h[:, g * GC:(g + 1) * GC, :].rearrange("p c (r w) -> p (c r) w", w=GRID_W)
                    dve.tensor_copy(pad[0][:, :, PAD:PAD + GRID_W], own)
                    dve.drain()
                    src, size, lo, hi, n = pad[0], 1, 0, W, 1
                    while size < window:
                        dst = pad[n]
                        if size == 1:
                            lo += 1
                            dve.tensor_tensor(dst[:, :, lo:hi], src[:, :, lo - 1:hi - 1], src[:, :, lo:hi], ALU.add)
                        else:
                            q = size // 2
                            lo, hi = lo + q, hi - q
                            dve.tensor_tensor(dst[:, :, lo:hi], src[:, :, lo - q:hi - q], src[:, :, lo + q:hi + q],
                                              ALU.add)
                        dve.drain()
                        src, size, n = dst, 2 * size, 3 - n
                    mean = pad[n][:, :, PAD:PAD + GRID_W]
                    dve.tensor_tensor(mean, src[:, :, PAD:PAD + GRID_W],
                                      inv[:, g:g + 1, :].to_broadcast([P, GC * ROWS, GRID_W]), ALU.mult)
                    dve.drain()
                    dve.tensor_tensor(own, mean, own, ALU.subtract)
                    dve.drain().then_inc(k.v_for_t.sem, 1)
                for o in range(KC):
                    dve.wait_ge(k.prod_v.sem, k.prod_v.at(o + 1))
                    dve.scalar_tensor_tensor(k.x[:, o, :], k.ps[:, o, :], gate[:, o:o + 1], k.x[:, o, :],
                                             ALU.mult, ALU.add)

            @block.tensor
            def _(pe):
                pe.wait_ge(k.loaded[1].sem, k.loaded[1].at(16 * len(POOL_WINDOWS)))
                for g in range(len(POOL_WINDOWS)):
                    pe.wait_ge(k.v_for_t.sem, k.v_for_t.at(g + 1))
                    for o in range(GC):
                        for c in range(GC):
                            mm = pe.matmul(k.ps[:, g * GC + o, :], wp[:, g, c, o * P:(o + 1) * P], h[:, g * GC + c, :],
                                           start=c == 0, stop=c == GC - 1)
                        mm.then_inc(k.prod_v.sem, 1)
    k.loaded[0].base += 16
    k.loaded[1].base += 16 * len(POOL_WINDOWS)
    k.v_for_t.base += len(POOL_WINDOWS)
    k.prod_v.base += KC


class Moe:

    def __init__(self, name, experts, width, weights, layer, router, first_logit):
        self.name, self.E, self.F, self.weights, self.layer = name, experts, width, weights, layer
        self.router, self.first_logit = router, first_logit
        self.blocks = experts + (2 * SEQ - experts) // P
        self.slabs = [min(512, width - n) for n in range(0, width, 512)]
        self.chunks = width // P
        assert self.blocks % 2 == 1 and self.blocks > 3 and width % P == 0
        assert self.pieces * 2 % RING == 0

    @property
    def pieces(self):
        return 3 * len(self.slabs)


RING = 6


def stage_moe(k, m, h, gate, alpha):
    nc, t = k.nc, k.t
    E, NB = m.E, m.blocks
    S = len(m.slabs)
    GT_GROUPS = [min(4, m.chunks - n) for n in range(0, m.chunks, 4)]
    NG = len(GT_GROUPS)
    name = m.name

    def scratch(n, shape, dt=F32):
        return nc.dram_tensor(f"{name}_{n}", shape, dt, kind="Internal").ap()

    rows_d, slots_d, out_d = scratch("rows", [SEQ, D]), scratch("slots", [NB * P, 1], I32), scratch("out", [NB * P, D])
    with ExitStack() as keep:
        def sb(n, shape, dt=F32, stack=keep):
            return k.sb(f"{name}_{n}", shape, dt, stack=stack)

        dest = sb("dest", [P, NT * 2], I32)
        weight = sb("weight", [P, NT, 2])
        expert_of = sb("expert_of", [1, NB], I32)
        in_use = sb("in_use", [1, 1], I32)
        slot_token = sb("slot_token", [P, NB], I32)

        with ExitStack() as s:
            row = sb("row", [P, 2, D], stack=s)
            NLOG = m.router[-1][1] + m.router[-1][2]
            wr = sb("wr", [P, KC, NLOG], stack=s)
            bias = sb("bias", [P, NLOG], stack=s)
            iota = sb("iota", [P, 40], stack=s)
            tokid = sb("tokid", [P, NT], I32, stack=s)
            zero = sb("zero", [P, NB], I32, stack=s)
            log = sb("log", [P, NT, NLOG], stack=s)
            gl = sb("gl", [P, NT, 8], stack=s)
            lg = sb("lg", [P, NT, 8], stack=s)
            part = sb("part", [P, NT, 8], stack=s)
            top = sb("top", [P, NT, 8], stack=s)
            idx = sb("idx", [P, NT, 8], U32, stack=s)
            gidx = sb("gidx", [P, NT], stack=s)
            gsum = sb("gsum", [P, NT], stack=s)
            goh = sb("goh", [P, NT, 4], stack=s)
            ex = sb("ex", [P, NT, 2], stack=s)
            e1 = sb("e1", [P, NT], stack=s)
            oh = sb("oh", [P, NT * 2, E], stack=s)
            both = sb("both", [P, NT, E], stack=s)
            pos = sb("pos", [P, NT, E], stack=s)
            destf = sb("destf", [P, NT * 2], stack=s)
            cnt = sb("cnt", [E, P], stack=s)
            nb, nb2 = sb("nb", [E, P], stack=s), sb("nb2", [E, P], stack=s)
            ind = sb("ind", [E, NB + 1], stack=s)
            start = sb("start", [P, E], stack=s)
            grouped = m.first_logit > 0
            with nc.Block() as block:
                @block.sync
                def _(sp):
                    for src, lo, n in m.router:
                        if len(src.shape) == 3:
                            for g in range(src.shape[0]):
                                sp.dma_start(wr[:, :, lo + g * 8:lo + g * 8 + 8],
                                             src[g].rearrange("(c p) e -> p c e", p=P)).then_inc(k.loaded[0].sem, 16)
                        else:
                            sp.dma_start(wr[:, :, lo:lo + n], src.rearrange("(c p) e -> p c e", p=P)).then_inc(
                                k.loaded[0].sem, 16)
                    sp.dma_start(bias[:, :], m_bias(m, t).to_broadcast([P, NLOG])).then_inc(k.loaded[1].sem, 16)
                    sp.dma_start(iota[:, :], t["iotas"]).then_inc(k.loaded[2].sem, 16)
                    sp.dma_start(tokid[:, :], t["token_ids"]).then_inc(k.loaded[3].sem, 16)
                    sp.wait_ge(k.v_for_p.sem, k.v_for_p.at(1))
                    sp.dma_start(slots_d.rearrange("(p b) a -> p (b a)", p=P), zero[:, :]).then_inc(k.loaded[4].sem, 16)
                    for q in range(NT):
                        sp.wait_ge(k.a_for_v.sem, k.a_for_v.at(q + 1))
                        sp.dma_start(rows_d[q * P:(q + 1) * P, :], row[:, q % 2, :]).then_inc(k.stored[q % 2].sem, 16)
                    for j in range(2):
                        sp.wait_ge(k.stored[j].sem, k.stored[j].at(32))

                nrouter = sum(src.shape[0] if len(src.shape) == 3 else 1 for src, _, _ in m.router)

                @block.tensor
                def _(pe):
                    pe.wait_ge(k.loaded[0].sem, k.loaded[0].at(16 * nrouter))
                    for q in range(NT):
                        for c in range(KC):
                            mm = pe.matmul(k.ps[:, 0, q * NLOG:(q + 1) * NLOG], h[:, c, q * P:(q + 1) * P], wr[:, c, :],
                                           start=c == 0, stop=c == KC - 1)
                    mm.then_inc(k.prod_v.sem, 1)
                    for q in range(NT):
                        pe.wait_ge(k.a_for_v.sem, k.a_for_v.at(q - 1))
                        for c in range(KC):
                            mm = pe.transpose(k.ps[:, 4 + q % 2 * 2 + c // 4, c % 4 * P:c % 4 * P + P],
                                              h[:, c, q * P:(q + 1) * P], k.square("ident"))
                        mm.then_inc(k.prod_a.sem, 1)
                    pe.wait_ge(k.v_for_t.sem, k.v_for_t.at(1))
                    for q in range(NT):
                        for q2 in range(q + 1):
                            pe.matmul(k.ps[:, 1, q * E:(q + 1) * E], k.square("ones" if q2 < q else "earlier"),
                                      both[:, q2, :], start=q2 == 0, stop=q2 == q)
                    for q in range(NT):
                        mm = pe.matmul(k.ps[0:E, 2, 0:P], both[:, q, :], k.square("ones"), start=q == 0, stop=q == NT - 1)
                    mm.then_inc(k.prod_v.sem, 1)
                    pe.wait_ge(k.v_for_t.sem, k.v_for_t.at(2))
                    pe.matmul(k.ps[:, 3, 0:E], nb[:, :], k.square("earlier")[0:E, 0:E], start=True, stop=True)
                    pe.matmul(k.ps[0:E, 2, P:P + NB], k.square("le")[0:E, 0:E], nb[:, 0:NB], start=True, stop=True).then_inc(
                        k.prod_v.sem, 1)
                    pe.wait_ge(k.v_for_t.sem, k.v_for_t.at(3))
                    pe.matmul(k.ps[0:1, 2, 256:256 + NB + 1], k.square("ones")[0:E, 0:1], ind[:, :], start=True,
                              stop=True).then_inc(k.prod_v.sem, 1)

                @block.scalar
                def _(act):
                    for q in range(NT):
                        act.wait_ge(k.prod_a.sem, k.prod_a.at(q + 1))
                        if q >= 2:
                            act.wait_ge(k.stored[q % 2].sem, k.stored[q % 2].at(16))
                        act.activation(row[:, q % 2, :].rearrange("p (a b) -> p a b", a=2),
                                       k.ps[:, 4 + q % 2 * 2:6 + q % 2 * 2, :], ACT.Copy)
                        act.drain().then_inc(k.a_for_v.sem, 1)
                    act.wait_ge(k.v_for_a.sem, k.v_for_a.at(1))
                    act.activation(e1[:, :], e1[:, :], ACT.Exp)
                    if grouped:
                        act.activation(gl[:, :, 0:4], gl[:, :, 0:4], ACT.Exp)
                    act.drain().then_inc(k.a_for_v.sem, 1)

                @block.vector
                def _(dve):
                    dve.memset(zero[:, :], 0)
                    dve.memset(gl[:, :, :], -3e38)
                    dve.drain().then_inc(k.v_for_p.sem, 1)
                    for n in (1, 2):
                        dve.wait_ge(k.loaded[n].sem, k.loaded[n].at(16))
                    dve.wait_ge(k.prod_v.sem, k.prod_v.at(1))
                    dve.tensor_tensor(log[:, :, :], k.ps[:, 0, 0:NT * NLOG].rearrange("p (q e) -> p q e", q=NT),
                                      bias[:, :].unsqueeze(1).to_broadcast([P, NT, NLOG]), ALU.add)
                    dve.drain()
                    if grouped:
                        dve.tensor_copy(gl[:, :, 0:4], log[:, :, 0:4])
                        dve.drain()
                        for q in range(NT):
                            dve.max(top[:, q, :], gl[:, q, :])
                        dve.drain()
                        for q in range(NT):
                            dve.max_index(idx[:, q, :], top[:, q, :], gl[:, q, :])
                        dve.drain()
                        dve.tensor_copy(gidx[:, :].unsqueeze(2), idx[:, :, 0:1])
                        dve.tensor_tensor(gl[:, :, 0:4], gl[:, :, 0:4], top[:, :, 0:1].to_broadcast([P, NT, 4]),
                                          ALU.subtract)
                        dve.drain()
                        dve.tensor_tensor(goh[:, :, :], iota[:, 0:4].unsqueeze(1).to_broadcast([P, NT, 4]),
                                          gidx[:, :].unsqueeze(2).to_broadcast([P, NT, 4]), ALU.is_equal)
                        dve.drain()
                        for g in range(4):
                            src = log[:, :, 4 + 8 * g:12 + 8 * g]
                            o = lg if g == 0 else part
                            dve.tensor_tensor(o[:, :, :], src, goh[:, :, g:g + 1].to_broadcast([P, NT, 8]), ALU.mult)
                            dve.drain()
                            if g > 0:
                                dve.tensor_tensor(lg[:, :, :], lg[:, :, :], part[:, :, :], ALU.add)
                                dve.drain()
                    else:
                        dve.tensor_copy(lg[:, :, :], log[:, :, :])
                        dve.drain()
                    for q in range(NT):
                        dve.max(top[:, q, :], lg[:, q, :])
                    dve.drain()
                    for q in range(NT):
                        dve.max_index(idx[:, q, :], top[:, q, :], lg[:, q, :])
                    dve.tensor_tensor(e1[:, :].unsqueeze(2), top[:, :, 1:2], top[:, :, 0:1], ALU.subtract)
                    dve.drain().then_inc(k.v_for_a.sem, 1)
                    dve.tensor_copy(ex[:, :, :], idx[:, :, 0:2])
                    dve.drain()
                    if grouped:
                        dve.tensor_scalar(gidx[:, :], gidx[:, :], 8.0, None, ALU.mult)
                        dve.drain()
                        dve.tensor_tensor(ex[:, :, :], ex[:, :, :], gidx[:, :].unsqueeze(2).to_broadcast([P, NT, 2]),
                                          ALU.add)
                        dve.drain()
                    dve.tensor_tensor(oh[:, :, :], iota[:, 0:E].unsqueeze(1).to_broadcast([P, NT * 2, E]),
                                      ex[:, :, :].rearrange("p q j -> p (q j)").unsqueeze(2).to_broadcast(
                                          [P, NT * 2, E]), ALU.is_equal)
                    dve.drain()
                    o4 = oh[:, :, :].rearrange("p (q j) e -> p q j e", j=2)
                    dve.tensor_tensor(both[:, :, :], o4[:, :, 0, :], o4[:, :, 1, :], ALU.add)
                    dve.drain().then_inc(k.v_for_t.sem, 1)
                    dve.wait_ge(k.a_for_v.sem, k.a_for_v.at(NT + 1))
                    w0, w1 = weight[:, :, 0], weight[:, :, 1]
                    dve.tensor_scalar(w0, e1[:, :], 1.0, None, ALU.add)
                    dve.drain()
                    dve.reciprocal(w0, w0)
                    dve.drain()
                    if grouped:
                        dve.tensor_reduce(gsum[:, :], gl[:, :, 0:4], AX.X, ALU.add)
                        dve.drain()
                        dve.reciprocal(gsum[:, :], gsum[:, :])
                        dve.drain()
                        dve.tensor_tensor(w0, w0, gsum[:, :], ALU.mult)
                        dve.drain()
                    dve.tensor_tensor(w1, w0, e1[:, :], ALU.mult)
                    dve.wait_ge(k.prod_v.sem, k.prod_v.at(2))
                    dve.tensor_copy(cnt[:, :], k.ps[0:E, 2, 0:P])
                    dve.tensor_scalar(nb[:, :], k.ps[0:E, 2, 0:P], 0.0, None, ALU.is_gt)
                    dve.tensor_copy(pos[:, :, :], k.ps[:, 1, 0:NT * E].rearrange("p (q e) -> p q e", q=NT))
                    dve.drain()
                    for j in range(1, NT):
                        dve.tensor_scalar(nb2[:, :], cnt[:, :], float(P * j), None, ALU.is_gt)
                        dve.drain()
                        dve.tensor_tensor(nb[:, :], nb[:, :], nb2[:, :], ALU.add)
                        dve.drain()
                    dve.drain().then_inc(k.v_for_t.sem, 1)
                    dve.wait_ge(k.prod_v.sem, k.prod_v.at(3))
                    dve.tensor_scalar(start[:, :], k.ps[:, 3, 0:E], float(P), None, ALU.mult)
                    dve.tensor_copy(ind[:, NB:NB + 1], nb[:, 0:1])
                    dve.tensor_tensor(ind[:, 0:NB], iota[0:E, 0:NB], k.ps[0:E, 2, P:P + NB], ALU.is_ge)
                    dve.drain().then_inc(k.v_for_t.sem, 1)
                    dve.tensor_tensor(pos[:, :, :], pos[:, :, :], start[:, :].unsqueeze(1).to_broadcast([P, NT, E]),
                                      ALU.add)
                    dve.drain()
                    for j in range(2):
                        dve.tensor_tensor(o4[:, :, j, :], o4[:, :, j, :], pos[:, :, :], ALU.mult)
                    dve.drain()
                    dve.tensor_reduce(destf[:, :], oh[:, :, :], AX.X, ALU.add)
                    dve.drain()
                    dve.tensor_copy(dest[:, :], destf[:, :])
                    dve.wait_ge(k.prod_v.sem, k.prod_v.at(4))
                    dve.tensor_copy(in_use[:, :], k.ps[0:1, 2, 256 + NB:256 + NB + 1])
                    dve.tensor_scalar(expert_of[:, :], k.ps[0:1, 2, 256:256 + NB], float(E - 1), None, ALU.min)
                    dve.drain().then_inc(k.v_for_p.sem, 1)

                @block.gpsimd
                def _(pool):
                    pool.wait_ge(k.loaded[3].sem, k.loaded[3].at(16))
                    pool.wait_ge(k.loaded[4].sem, k.loaded[4].at(16))
                    pool.wait_ge(k.v_for_p.sem, k.v_for_p.at(2))
                    for q in range(NT):
                        for j in range(2):
                            pool.indirect_dma_start(
                                out=slots_d, out_offset=bass.IndirectOffsetOnAxis(
                                    ap=dest[:, 2 * q + j:2 * q + j + 1], axis=0),
                                in_=tokid[:, q:q + 1], in_offset=None).then_inc(k.scattered.sem, 16)
                    pool.wait_ge(k.scattered.sem, k.scattered.at(16 * 2 * NT))
                    pool.dma_start(slot_token[:, :], slots_d.rearrange("(b p) a -> p (b a)", p=P),
                                   allow_slow_non_contiguous=True).then_inc(k.slots_back.sem, 16)
                    pool.wait_ge(k.slots_back.sem, k.slots_back.at(16))
            k.loaded[0].base += 16 * nrouter
            for n in (1, 2, 3, 4):
                k.loaded[n].base += 16
            k.slots_back.base += 16
            k.scattered.base += 32 * NT
            k.prod_v.base += 4
            k.prod_a.base += NT
            k.a_for_v.base += NT + 1
            k.v_for_a.base += 1
            k.v_for_t.base += 3
            k.v_for_p.base += 2
            for j in range(2):
                k.stored[j].base += 32

        with ExitStack() as s:
            wb = sb("wb", [P, RING, 4096], stack=s)
            xg, xt = sb("xg", [P, 2, D], stack=s), sb("xt", [P, KC, P], stack=s)
            index = sb("index", [P, 2], I32, stack=s)
            th = sb("th", [P, 2, 512], stack=s)
            act_, actT = sb("act", [P, 2, m.F], stack=s), sb("actT", [P, m.chunks, P], stack=s)
            yb = sb("yb", [P, 2, D], stack=s)
            w1, w3, w2 = m.weights
            A, V = NG + 1, S + 1
            half_blocks = NB // 2
            turned_banks = S % 2 * 2

            def all_steps(engine, both, own, neither, end, no_end):
                count = engine.value_load(in_use[0:1, 0:1], min_val=1, max_val=NB)

                def step(i, j, last):
                    with engine.If(i * 2 + (j + 1) < count):
                        both(i, j, last)
                    with engine.Else():
                        with engine.If(i * 2 + j < count):
                            own(i, j, last)
                        with engine.Else():
                            neither(i, j, last)
                        engine.nop()

                with engine.Fori(0, half_blocks - 1) as i:
                    step(i, 0, False)
                    step(i, 1, False)
                step(half_blocks - 1, 0, False)
                step(half_blocks - 1, 1, True)
                with engine.If(count > NB - 1):
                    end()
                with engine.Else():
                    no_end()
                engine.nop()

            def count_on(engine, *signals):
                engine.drain()
                for signal, n in signals:
                    if n:
                        engine.sem_inc(signal.sem, n)

            def up(j, n, q):
                return 2 * n + q + (0 if j < 0 else 2 * S + j * m.pieces)

            def down(j, n, end):
                return 2 * S + j * m.pieces + (0 if end else 2 * S) + n

            with nc.Block() as block:
                @block.sync
                def _(sp):
                    def expert(i, j):
                        return sp.value_load(expert_of[0:1, bass.ds(i * 2 + j, 1)], min_val=0, max_val=E - 1)

                    def load(i, number, columns, rows, src):
                        slot = number % RING
                        sp.wait_ge(k.used.sem, i * (2 * m.pieces) + k.used.at(number + 1 - RING))
                        sp.dma_start(wb[:, slot, 0:rows * columns].rearrange("p (c n) -> p c n", c=rows), src).then_inc(
                            k.landed[slot].sem, 16)

                    def load_up(i, j, e):
                        for n, width in enumerate(m.slabs):
                            for q, w in enumerate((w1, w3)):
                                load(i, up(j, n, q), width, KC, w[bass.ds(e, 1), :, n * 512:n * 512 + width].rearrange(
                                    "a (c p) n -> p (a c) n", p=P))

                    def load_down(i, j, e, end):
                        for n, rows in enumerate(GT_GROUPS):
                            load(i, down(j, n, end), D, rows, w2[bass.ds(e, 1), n * 512:n * 512 + rows * P, :].rearrange(
                                "a (c p) n -> p (a c) n", p=P))

                    def leave_out(i, numbers):
                        for number in numbers:
                            slot = number % RING
                            sp.wait_ge(k.used.sem, i * (2 * m.pieces) + k.used.at(number + 1 - RING))
                            sp.sem_inc(k.landed[slot].sem, 16)

                    def ups(j):
                        return [up(j, n, q) for n in range(S) for q in range(2)]

                    def downs(j, end):
                        return [down(j, n, end) for n in range(NG)]

                    load_up(0, -1, expert(0, 0))

                    def both(i, j, last):
                        load_up(i, j, expert(i, j + 1))
                        load_down(i, j, expert(i, j), False)

                    def own(i, j, last):
                        leave_out(i, ups(j))
                        load_down(i, j, expert(i, j), False)

                    all_steps(sp, both, own,
                              lambda i, j, last: leave_out(i, ups(j) + downs(j, False)),
                              lambda: load_down(half_blocks, 0, expert(half_blocks, 0), True),
                              lambda: leave_out(half_blocks, downs(0, True)))

                per_turn = 2 * m.pieces // RING

                @block.gpsimd
                def _(pool):
                    def body(i, j):
                        pool.wait_ge(k.prod_v.sem, i * 2 + k.prod_v.at(j - 1))
                        pool.tensor_copy(index[:, j:j + 1], slot_token[:, bass.ds(i * 2 + j, 1)])
                        pool.drain()
                        pool.indirect_dma_start(
                            out=xg[:, j, :], out_offset=None, in_=rows_d,
                            in_offset=bass.IndirectOffsetOnAxis(ap=index[:, j:j + 1], axis=0)).then_inc(
                            k.gathered[j].sem, 16)

                    with pool.Fori(0, half_blocks) as i:
                        body(i, 0)
                        body(i, 1)
                    body(half_blocks, 0)

                @block.tensor
                def _(pe):
                    def turn(i, j):
                        pe.wait_ge(k.gathered[j].sem, i * 16 + k.gathered[j].at(16))
                        for c in range(KC):
                            mm = pe.transpose(k.ps[:, turned_banks + c // 4, c % 4 * P:c % 4 * P + P],
                                              xg[:, j, c * P:(c + 1) * P], k.square("ident"))
                        mm.then_inc(k.prod_v.sem, 1)

                    def piece(i, number):
                        slot = number % RING
                        pe.wait_ge(k.landed[slot].sem, i * (16 * per_turn) + k.landed[slot].at(16 * (number // RING + 1)))
                        return slot

                    def hidden(i, j, n, width):
                        if n >= 2:
                            pe.wait_ge(k.v_for_t.sem, i * (2 * V) + k.v_for_t.at(1 + (j + 1) * V + n - 1))
                        for q in range(2):
                            slot = piece(i, up(j, n, q))
                            for c in range(KC):
                                mm = pe.matmul(k.ps[:, n % 2 * 2 + q, 0:width], xt[:, c, :],
                                               wb[:, slot, c * width:(c + 1) * width], start=c == 0, stop=c == KC - 1)
                            mm.then_inc(k.used.sem, 1)

                    def turn_activations(i, j, n, rows):
                        if n >= 2:
                            pe.wait_ge(k.a_for_t.sem, i * (2 * A) + k.a_for_t.at(j * A + n - 1))
                        for q in range(rows):
                            c = 4 * n + q
                            mm = pe.transpose(k.ps[:, 4 + n % 2, q * P:(q + 1) * P], act_[:, j, c * P:(c + 1) * P],
                                              k.square("ident"))
                        mm.then_inc(k.prod_a.sem, 1)

                    def output(i, j, end):
                        pe.wait_ge(k.a_for_t.sem, i * (2 * A) + k.a_for_t.at(j * A))
                        for n, rows in enumerate(GT_GROUPS):
                            pe.wait_ge(k.a_for_t.sem, i * (2 * A) + k.a_for_t.at(j * A + n + 1))
                            slot = piece(i, down(j, n, end))
                            for q in range(rows):
                                c = 4 * n + q
                                for o in range(2):
                                    mm = pe.matmul(k.ps[:, 6 + o, :], actT[:, c, :],
                                                   wb[:, slot, q * D + o * 512:q * D + (o + 1) * 512],
                                                   start=c == 0, stop=c == m.chunks - 1)
                            mm.then_inc(k.used.sem, 1)

                    turn(0, 0)
                    pe.wait_ge(k.v_for_t.sem, k.v_for_t.at(1))
                    for n, width in enumerate(m.slabs):
                        hidden(0, -1, n, width)
                    if S > 1:
                        pe.wait_ge(k.v_for_t.sem, k.v_for_t.at(S))
                    turn(0, 1)

                    def both(i, j, last):
                        pe.wait_ge(k.v_for_t.sem, i * (2 * V) + k.v_for_t.at(1 + (j + 1) * V))
                        for n, width in enumerate(m.slabs):
                            hidden(i, j, n, width)
                            turn_activations(i, j, n, GT_GROUPS[n])
                        if not last:
                            if S > 1:
                                pe.wait_ge(k.v_for_t.sem, i * (2 * V) + k.v_for_t.at(1 + (j + 1) * V + S - 1))
                            turn(i + 1, j)
                        output(i, j, False)

                    def finish(i, j, end):
                        for n, rows in enumerate(GT_GROUPS):
                            turn_activations(i, j, n, rows)
                        output(i, j, end)

                    def own(i, j, last):
                        count_on(pe, (k.used, 2 * S), (k.prod_v, 0 if last else 1))
                        pe.wait_ge(k.v_for_t.sem, i * (2 * V) + k.v_for_t.at(1 + (j + 1) * V))
                        finish(i, j, False)

                    def end():
                        pe.wait_ge(k.v_for_t.sem, k.v_for_t.at(NB * V))
                        finish(half_blocks, 0, True)

                    all_steps(pe, both, own,
                              lambda i, j, last: count_on(pe, (k.used, m.pieces), (k.prod_a, NG),
                                                          (k.prod_v, 0 if last else 1)),
                              end, lambda: count_on(pe, (k.used, NG), (k.prod_a, NG)))

                @block.scalar
                def _(act):
                    def used(i, number):
                        return i * (2 * m.pieces) + k.used.at(number + 1)

                    def tanh(i, j, n, width):
                        act.wait_ge(k.used.sem, used(i, up(j, n, 0)))
                        if n >= 2:
                            act.wait_ge(k.v_for_t.sem, i * (2 * V) + k.v_for_t.at(1 + (j + 1) * V + n - 1))
                        act.activation(th[:, n % 2, 0:width], k.ps[:, n % 2 * 2, 0:width], ACT.Tanh,
                                       scale=0.5).then_inc(k.a_for_v.sem, 1)

                    def turned(i, j, n, rows):
                        act.wait_ge(k.prod_a.sem, i * (2 * NG) + k.prod_a.at(j * NG + n + 1))
                        act.activation(actT[:, 4 * n:4 * n + rows, :],
                                       k.ps[:, 4 + n % 2, 0:rows * P].rearrange("p (a b) -> p a b", b=P),
                                       ACT.Copy).then_inc(k.a_for_t.sem, 1)

                    def store(i, j):
                        act.dma_start(out_d[bass.ds(i * (2 * P) + j * P, P), :], yb[:, j, :]).then_inc(
                            k.stored[j].sem, 16)

                    def output(i, j, end):
                        act.wait_ge(k.used.sem, used(i, down(j, NG - 1, end)))
                        act.wait_ge(k.stored[j].sem, i * 16 + k.stored[j].at(0))
                        act.activation(yb[:, j, :].rearrange("p (a b) -> p a b", a=2), k.ps[:, 6:8, :], ACT.Copy)
                        act.drain().then_inc(k.a_for_t.sem, 1)
                        store(i, j)

                    for n, width in enumerate(m.slabs):
                        tanh(0, -1, n, width)

                    def both(i, j, last):
                        for n, width in enumerate(m.slabs):
                            tanh(i, j, n, width)
                            turned(i, j, n, GT_GROUPS[n])
                        output(i, j, False)

                    def finish(i, j, end):
                        for n, rows in enumerate(GT_GROUPS):
                            turned(i, j, n, rows)
                        output(i, j, end)

                    def own(i, j, last):
                        count_on(act, (k.a_for_v, S))
                        finish(i, j, False)

                    def neither(i, j, tanhs):
                        store(i, j)
                        count_on(act, (k.a_for_v, tanhs), (k.a_for_t, A))

                    all_steps(act, both, own, lambda i, j, last: neither(i, j, S),
                              lambda: finish(half_blocks, 0, True), lambda: neither(half_blocks, 0, 0))
                    act.wait_ge(k.stored[0].sem, k.stored[0].at(16 * (half_blocks + 1)))
                    act.wait_ge(k.stored[1].sem, k.stored[1].at(16 * half_blocks))

                @block.vector
                def _(dve):
                    def turned(n):
                        dve.wait_ge(k.prod_v.sem, n)
                        dve.tensor_copy(xt[:, :, :].rearrange("p (a c) n -> p a (c n)", a=2),
                                        k.ps[:, turned_banks:turned_banks + 2, :]).then_inc(k.v_for_t.sem, 1)

                    def activations(i, j):
                        for n, width in enumerate(m.slabs):
                            dve.wait_ge(k.a_for_v.sem, i * (2 * S) + k.a_for_v.at((j + 1) * S + n + 1))
                            dve.scalar_tensor_tensor(th[:, n % 2, 0:width], th[:, n % 2, 0:width], 1.0,
                                                     k.ps[:, n % 2 * 2, 0:width], ALU.add, ALU.mult)
                            dve.drain()
                            dve.wait_ge(k.used.sem, i * (2 * m.pieces) + k.used.at(up(j, n, 1) + 1))
                            dve.scalar_tensor_tensor(act_[:, (j + 1) % 2, n * 512:n * 512 + width], th[:, n % 2, 0:width],
                                                     0.5, k.ps[:, n % 2 * 2 + 1, 0:width], ALU.mult,
                                                     ALU.mult).then_inc(k.v_for_t.sem, 1)

                    turned(k.prod_v.at(1))
                    activations(0, -1)
                    turned(k.prod_v.at(2))

                    def both(i, j, last):
                        activations(i, j)
                        if not last:
                            turned(i * 2 + k.prod_v.at(j + 3))

                    def left_out(i, j, last):
                        count_on(dve, (k.v_for_t, S if last else V))

                    all_steps(dve, both, left_out, left_out, dve.nop, dve.nop)
            k.used.base += NB * m.pieces
            k.prod_v.base += NB
            k.prod_a.base += NB * NG
            k.a_for_v.base += NB * S
            k.v_for_t.base += NB * V
            k.a_for_t.base += NB * (NG + 1)
            total = NB * m.pieces
            for q in range(RING):
                k.landed[q].base += 16 * ((total - q + RING - 1) // RING)
            for j in range(2):
                k.stored[j].base += 16 * (half_blocks + 1 - j)
                k.gathered[j].base += 16 * (half_blocks + 1 - j)

        with ExitStack() as s:
            yg = sb("yg", [P, 2, 2, D], stack=s)
            with nc.Block() as block:
                @block.gpsimd
                def _(pool):
                    for q in range(NT):
                        pool.wait_ge(k.prod_v.sem, k.prod_v.at(q - 1))
                        for j in range(2):
                            pool.indirect_dma_start(
                                out=yg[:, q % 2, j, :], out_offset=None, in_=out_d,
                                in_offset=bass.IndirectOffsetOnAxis(ap=dest[:, 2 * q + j:2 * q + j + 1], axis=0)
                            ).then_inc(k.gathered[q % 2].sem, 16)

                @block.vector
                def _(dve):
                    def add(q):
                        dve.wait_ge(k.prod_v.sem, k.prod_v.at(q + 1))
                        for c in range(KC):
                            x = k.x[:, c, q * P:(q + 1) * P]
                            src = k.ps[:, q % 2 * 2 + c // 4, c % 4 * P:c % 4 * P + P]
                            if gate is None:
                                dve.tensor_tensor(x, src, x, ALU.add)
                            else:
                                dve.scalar_tensor_tensor(x, src, gate[:, c:c + 1], x, ALU.mult, ALU.add)
                        dve.drain().then_inc(k.free_v.sem, 1)

                    if alpha != 1.0:
                        dve.tensor_scalar(k.x[:, :, :], k.x[:, :, :], alpha, None, ALU.mult)
                        dve.drain()
                    for q in range(NT):
                        a, b = yg[:, q % 2, 0, :], yg[:, q % 2, 1, :]
                        dve.wait_ge(k.gathered[q % 2].sem, k.gathered[q % 2].at(32 * (q // 2 + 1)))
                        dve.tensor_scalar(a, a, weight[:, q, 0:1], None, ALU.mult)
                        dve.drain()
                        dve.scalar_tensor_tensor(a, b, weight[:, q, 1:2], a, ALU.mult, ALU.add)
                        dve.drain().then_inc(k.v_for_t.sem, 1)
                        if q:
                            add(q - 1)
                    add(NT - 1)

                @block.tensor
                def _(pe):
                    for q in range(NT):
                        pe.wait_ge(k.v_for_t.sem, k.v_for_t.at(q + 1))
                        pe.wait_ge(k.free_v.sem, k.free_v.at(q - 1))
                        for c in range(KC):
                            mm = pe.transpose(k.ps[:, q % 2 * 2 + c // 4, c % 4 * P:c % 4 * P + P],
                                              yg[:, q % 2, 0, c * P:(c + 1) * P], k.square("ident"))
                        mm.then_inc(k.prod_v.sem, 1)
            k.prod_v.base += NT
            k.free_v.base += NT
            k.v_for_t.base += NT
            for j in range(2):
                k.gathered[j].base += 16 * NT


def m_bias(m, t):
    lo = {"moe": 0, "hier": 8}[m.name]
    n = m.router[-1][1] + m.router[-1][2]
    return t["router_rows"][0:1, lo:lo + n]


def stage_first_moe(k):
    m = Moe("moe", 8, 1408, [k.t[n][0] for n in ("moe_w1", "moe_w3", "moe_w2")], 1,
            [(k.t["moe_router_w"][0], 0, 8)], 0)
    with ExitStack() as s:
        h = k.sb("moe_h", [P, KC, SEQ], stack=s)
        stage_modulate(k, h, 1, 3)
        stage_moe(k, m, h, k.mod[:, 1, 5 * KC:6 * KC, 0], DN_ALPHA)


def stage_rms_norm(k, dst, weight, sync=None):
    name = dst.name
    with ExitStack() as s:
        sqr, rstd = k.sb(f"rms_sq_{name}", [P, KC, SEQ], stack=s), k.sb(f"rms_r_{name}", [P, SEQ], stack=s)
        with k.nc.Block() as block:
            if sync:
                block.sync(sync)

            @block.scalar
            def _(act):
                for c in range(KC):
                    act.activation(sqr[:, c, :], k.x[:, c, :], ACT.Square).then_inc(k.a_for_t.sem, 1)
                act.wait_ge(k.prod_a.sem, k.prod_a.at(1))
                act.activation(rstd[:, :], k.ps[:, 0, :], ACT.Sqrt, scale=1.0 / D, bias=k.eps[:, 2:3]).then_inc(
                    k.a_for_v.sem, 1)

            @block.tensor
            def _(pe):
                for c in range(KC):
                    pe.wait_ge(k.a_for_t.sem, k.a_for_t.at(c + 1))
                    mm = pe.matmul(k.ps[:, 0, :], k.square("ones"), sqr[:, c, :], start=c == 0, stop=c == KC - 1)
                mm.then_inc(k.prod_a.sem, 1)

            @block.vector
            def _(dve):
                dve.wait_ge(k.a_for_v.sem, k.a_for_v.at(1))
                dve.reciprocal(rstd[:, :], rstd[:, :])
                dve.drain()
                for c in range(KC):
                    dve.scalar_tensor_tensor(dst[:, c, :], k.x[:, c, :], weight[:, c:c + 1], rstd[:, :],
                                             ALU.mult, ALU.mult).then_inc(k.normed.sem, 1)
    k.normed.base += KC
    k.a_for_t.base += KC
    k.prod_a.base += 1
    k.a_for_v.base += 1


def stage_in_projection(k, fm, tm, lr):
    nc, t = k.nc, k.t
    att = 2 * GLA_KEY + 2 * GLA_HEADS * GLA_DV + 2 * GLA_RANK
    pieces = [("fm", 0, 0), ("tm", 0, 512), ("fm", 1, 1024), ("fm", 2, att), ("fm", 3, att + 512), ("tm", 1, att + 1024)]
    with ExitStack() as s:
        u = k.sb("in_u", [P, KC, SEQ], stack=s)
        wb = k.sb("in_wb", [P, 3, KC, 512], stack=s)
        wl = k.sb("in_wl", [P, KC, 2 * GLA_RANK], stack=s)
        src = t["w_in_2"][0].rearrange("(c p) n -> p c n", p=P)

        def load(sp, n):
            col = pieces[n][2]
            sp.dma_start(wb[:, n % 3, :, :], src[:, :, col:col + 512]).then_inc(k.landed[n % 3].sem, 16)

        def load_first(sp):
            for n in range(3):
                load(sp, n)
            sp.dma_start(wl[:, :, :], src[:, :, att - 2 * GLA_RANK:att]).then_inc(k.loaded[0].sem, 16)

        stage_rms_norm(k, u, k.v("norm1"), load_first)
        with nc.Block() as block:
            @block.sync
            def _(sp):
                for n in range(3, len(pieces)):
                    sp.wait_ge(k.prod_a.sem, k.prod_a.at(4 * (n - 2)))
                    load(sp, n)

            @block.tensor
            def _(pe):
                for n, (kind, _, _) in enumerate(pieces):
                    pe.wait_ge(k.landed[n % 3].sem, k.landed[n % 3].at(16 * (n // 3 + 1)))
                    for g in range(4):
                        e = 4 * n + g
                        pe.wait_ge(k.a_for_t.sem, k.a_for_t.at(e - 5))
                        for c in range(KC):
                            own, tokens = wb[:, n % 3, c, :], u[:, c, :]
                            piece = slice(g * P, (g + 1) * P)
                            mm = pe.matmul(k.ps[:, e % 6, :], own[:, piece] if kind == "fm" else tokens[:, piece],
                                           tokens if kind == "fm" else own, start=c == 0, stop=c == KC - 1)
                        mm.then_inc(k.prod_a.sem, 1)
                pe.wait_ge(k.loaded[0].sem, k.loaded[0].at(16))
                for d in range(2):
                    for c in range(KC):
                        mm = pe.matmul(k.ps[32 * d:32 * d + GLA_RANK, 6, :], wl[:, c, d * GLA_RANK:(d + 1) * GLA_RANK],
                                       u[:, c, :], start=c == 0, stop=c == KC - 1)
                mm.then_inc(k.prod_v.sem, 1)

            @block.scalar
            def _(act):
                for n, (kind, q, _) in enumerate(pieces):
                    for g in range(4):
                        e = 4 * n + g
                        act.wait_ge(k.prod_a.sem, k.prod_a.at(e + 1))
                        act.activation((fm[q] if kind == "fm" else tm[q])[:, g, :], k.ps[:, e % 6, :], ACT.Copy)\
                            .then_inc(k.a_for_t.sem, 1)

            @block.vector
            def _(dve):
                dve.memset(lr[:, :], 1.0)
                dve.drain()
                dve.wait_ge(k.prod_v.sem, k.prod_v.at(1))
                for d in range(2):
                    dve.tensor_copy(lr[32 * d:32 * d + GLA_RANK, :], k.ps[32 * d:32 * d + GLA_RANK, 6, :])
    k.loaded[0].base += 16
    for n in range(3):
        k.landed[n].base += 32
    k.prod_a.base += 4 * len(pieces)
    k.a_for_t.base += 4 * len(pieces)
    k.prod_v.base += 1


def stage_linear_attention(k, qk, gg, v, lr, mixed):
    nc, t = k.nc, k.t
    KK = GLA_KEY // P
    BEFORE = {0: ("le", "gt"), 1: ("ge", "lt")}
    with ExitStack() as s:
        def sb(name, shape):
            return k.sb(name, shape, stack=s)

        wg = sb("gl_wg", [64, GLA_KEY])
        la, az, mz = (sb(n, [P, NT, 2 * GLA_KEY]) for n in ("gl_la", "gl_az", "gl_mz"))
        eb, ei, ea = ([sb(f"{n}{d}", [P, KK, P]) for d in range(2)] for n in ("gl_eb", "gl_ei", "gl_ea"))
        dec = [sb(f"gl_dec{d}", [P, KK, 2]) for d in range(2)]
        vt = sb("gl_vt", [P, 2, GLA_HEADS * GLA_DV])
        lat = sb("gl_lat", [P, 2, 2 * GLA_KEY])
        kend = [sb(f"gl_kend{d}", [P, GLA_KEY]) for d in range(2)]
        att = [sb(f"gl_att{d}", [P, GLA_HEADS, P]) for d in range(2)]
        S = sb("gl_S", [P, 2, 3, KK * GLA_DV])
        o = mixed[:, 0:GLA_HEADS, :]
        K1 = GLA_RANK + 1
        with nc.Block() as block:
            @block.sync
            def _(sp):
                for d, n in enumerate(("gla_fwd_gate_w_2", "gla_bwd_gate_w_2")):
                    sp.dma_start(wg[32 * d:32 * d + GLA_RANK, :], t[n][0]).then_inc(k.loaded[0].sem, 16)
                    sp.dma_start(wg[32 * d + GLA_RANK:32 * d + K1, :],
                                 t["rows"][0:1, 2 * D + d * GLA_KEY:2 * D + (d + 1) * GLA_KEY]).then_inc(
                        k.loaded[0].sem, 16)

            @block.tensor
            def _(pe):
                pe.wait_ge(k.loaded[0].sem, k.loaded[0].at(64))
                for q in range(NT):
                    for d in range(2):
                        rows = slice(32 * d, 32 * d + K1)
                        mm = pe.matmul(k.ps[:, 2 * q + d, 0:GLA_KEY], lr[rows, q * P:(q + 1) * P], wg[rows, :],
                                       start=True, stop=True)
                mm.then_inc(k.prod_v.sem, 1)

            @block.vector
            def _(dve):
                dve.memset(S[:, :, :, :], 0.0)
                dve.memset(o, 0.0)
                dve.wait_ge(k.prod_v.sem, k.prod_v.at(1))
                z = k.ps[:, :, 0:GLA_KEY]
                flat = lambda m: m[:, :, :].rearrange("p q (d n) -> p (q d) n", d=2)
                dve.tensor_scalar(flat(mz), z, 0.0, None, ALU.min)
                dve.tensor_scalar(flat(az), z, 0.0, None, ALU.max)
                dve.drain()
                dve.tensor_tensor(az[:, :, :], az[:, :, :], mz[:, :, :], ALU.subtract)
                dve.drain().then_inc(k.v_for_a.sem, 1)
                dve.wait_ge(k.a_for_v.sem, k.a_for_v.at(1))
                dve.tensor_tensor(la[:, :, :], mz[:, :, :], la[:, :, :], ALU.subtract)
                dve.drain()
                dve.tensor_scalar(la[:, :, :], la[:, :, :], 1.0 / GLA_TAU, None, ALU.mult)

            @block.scalar
            def _(act):
                act.wait_ge(k.v_for_a.sem, k.v_for_a.at(1))
                act.activation(az[:, :, :], az[:, :, :], ACT.Exp, scale=-1.0)
                act.drain()
                act.activation(la[:, :, :], az[:, :, :], ACT.Ln, bias=k.eps[:, 3:4])
                act.drain().then_inc(k.a_for_v.sem, 1)
        k.loaded[0].base += 64
        k.prod_v.base += 1
        k.v_for_a.base += 1
        k.a_for_v.base += 1

        cnt = {"prod_a": 2, "a_for_v": 1, "a_for_t": 1, "prod_v": 4, "v_for_t": 5, "p_for_t": 2}

        def program(engine, *steps):
            with engine.Fori(0, NT) as i:
                for step in steps:
                    for d in range(2):
                        step(d, i * (1 if d == 0 else -1) + (0 if d == 0 else NT - 1),
                             i * (P if d == 0 else -P) + (0 if d == 0 else SEQ - P),
                             lambda name, n, turn=0, d=d: i * (2 * cnt[name]) + k.named[name].at(
                                 2 * (n - 1) + d + 1 + turn * 2 * cnt[name]))

        def half(h):
            return slice(h % 2 * 64, h % 2 * 64 + 64)

        def cols(c):
            return slice(c * P, (c + 1) * P)

        def state_bank(d, step):
            return 4 * d + (3 if step == 0 else 0)

        def chunk(d, step):
            return step if d == 0 else 1 - step

        with nc.Block() as block:
            @block.gpsimd
            def _(pool):
                def decays(d, q, at0, v):
                    pool.wait_ge(k.prod_a.sem, v("prod_a", 1, -1))
                    pool.tensor_copy(lat[:, d, :], la[:, bass.ds(q, 1), :].rearrange("p a n -> p (a n)")).then_inc(
                        k.p_for_t.sem, 1)

                def values(d, q, at0, at):
                    pool.wait_ge(k.prod_v.sem, at("prod_v", 4, -1))
                    pool.tensor_copy(vt[:, d, :], v[:, bass.ds(q, 1), :].rearrange("p a n -> p (a n)")).then_inc(
                        k.p_for_t.sem, 1)
                program(pool, decays, values)

            @block.tensor
            def _(pe):
                def sums(d, q, at0, v):
                    pe.wait_ge(k.v_for_t.sem, v("v_for_t", 4, -1))
                    pe.wait_ge(k.p_for_t.sem, v("p_for_t", 1))
                    for j, mask in enumerate(k.square(n) for n in BEFORE[d]):
                        for c in range(KK):
                            n = d * GLA_KEY + c * P
                            mm = pe.matmul(k.ps[:, 4 * d, (2 * j + c) * P:(2 * j + c + 1) * P], lat[:, d, n:n + P], mask,
                                           start=True, stop=True)
                    mm.then_inc(k.prod_a.sem, 1)

                def scores(d, q, at0, v):
                    pe.wait_ge(k.v_for_t.sem, v("v_for_t", 1))
                    for c in range(KK):
                        mm = pe.transpose(k.ps[:, 4 * d, cols(c)], ea[d][:, c, :], k.square("ident"))
                    mm.then_inc(k.prod_a.sem, 1)
                    for h in range(GLA_HEADS):
                        mm = pe.matmul(k.ps[:, 4 * d + 1 + h % 2, cols(h // 2)], ei[d][half(h), h // 2, :],
                                       eb[d][half(h), h // 2, :], start=True, stop=True)
                    mm.then_inc(k.prod_v.sem, 1)

                def state(step):
                    def of_chunk(d, q, at0, v):
                        pe.wait_ge(k.p_for_t.sem, v("p_for_t", 2))
                        pe.wait_ge(k.a_for_t.sem, v("a_for_t", 1))
                        pe.sem_inc(k.passed.sem, 1)
                        rows = slice(chunk(d, step) * 64, chunk(d, step) * 64 + 64)
                        for h in range(GLA_HEADS):
                            mm = pe.matmul(k.ps[half(h), state_bank(d, step), cols(h // 2)],
                                           kend[d][rows, h * 64:(h + 1) * 64], vt[rows, d, h * P:(h + 1) * P],
                                           start=True, stop=True)
                        mm.then_inc(k.prod_v.sem, 1)
                    return of_chunk

                def outputs(d, q, at0, v):
                    pe.wait_ge(k.v_for_t.sem, v("v_for_t", 4))
                    for h in range(GLA_HEADS):
                        bank, col = 4 * d + 1 + h % 2, h // 2 * P
                        pe.matmul(k.ps[:, bank, col:col + P], vt[:, d, h * P:(h + 1) * P], att[d][:, h, :],
                                  start=True, stop=False)
                        for step in range(2):
                            c = chunk(d, step)
                            mm = pe.matmul(k.ps[:, bank, col + c * 64:col + c * 64 + 64],
                                           S[half(h), d, step, h // 2 * P:(h // 2 + 1) * P],
                                           eb[d][half(h), h // 2, c * 64:c * 64 + 64], start=False, stop=step == 1)
                    mm.then_inc(k.prod_v.sem, 1)
                program(pe, sums, scores, state(0), state(1), outputs)

            @block.scalar
            def _(act):
                def exponentials(d, q, at0, v):
                    act.wait_ge(k.prod_a.sem, v("prod_a", 1))
                    act.wait_ge(k.v_for_t.sem, v("v_for_t", 5, -1))
                    sums = k.ps[:, 4 * d, :].rearrange("p (j c n) -> p j c n", j=2, c=KK)
                    act.activation(eb[d][:, :, :], sums[:, 0, :, :], ACT.Exp)
                    act.activation(ei[d][:, :, :], sums[:, 0, :, :], ACT.Exp, scale=-1.0)
                    act.activation(ea[d][:, :, :], sums[:, 1, :, :], ACT.Exp)
                    act.drain().then_inc(k.a_for_v.sem, 1)

                def keys(d, q, at0, v):
                    act.wait_ge(k.prod_a.sem, v("prod_a", 2))
                    act.activation(kend[d][:, :], k.ps[:, 4 * d, 0:GLA_KEY], ACT.Copy).then_inc(k.a_for_t.sem, 1)
                program(act, exponentials, keys)

            @block.vector
            def _(dve):
                def features(d, q, at0, v):
                    dve.wait_ge(k.a_for_v.sem, v("a_for_v", 1))
                    dve.tensor_copy(S[:, d, 0, :], S[:, d, 2, :])
                    ends = (63, 127) if d == 0 else (0, 64)
                    for c in range(2):
                        dve.tensor_copy(dec[d][:, :, c:c + 1], eb[d][:, :, ends[c]:ends[c] + 1])
                    dve.drain()
                    qt, kt = qk[:, 0:KK, bass.ds(at0, P)], qk[:, KK:2 * KK, bass.ds(at0, P)]
                    dve.tensor_scalar(eb[d][:, :, :], eb[d][:, :, :], GLA_DK ** -0.5, None, ALU.mult)
                    dve.tensor_tensor(ei[d][:, :, :], ei[d][:, :, :], kt, ALU.mult)
                    dve.tensor_tensor(ea[d][:, :, :], ea[d][:, :, :], kt, ALU.mult)
                    dve.drain()
                    dve.tensor_tensor(eb[d][:, :, :], eb[d][:, :, :], qt, ALU.mult)
                    dve.drain().then_inc(k.v_for_t.sem, 1)

                def masked(d, q, at0, v):
                    dve.wait_ge(k.prod_v.sem, v("prod_v", 1))
                    incl = k.square(BEFORE[d][0]).unsqueeze(1).to_broadcast([P, 2, P])
                    a4 = att[d][:, :, :].rearrange("p (c j) n -> p j c n", j=2)
                    for j in range(2):
                        dve.tensor_tensor(a4[:, j, :, :],
                                          k.ps[:, 4 * d + 1 + j, 0:2 * P].rearrange("p (c n) -> p c n", c=2),
                                          incl, ALU.mult)
                    dve.drain().then_inc(k.v_for_t.sem, 1)

                def state(step):
                    def of_chunk(d, q, at0, v):
                        c = chunk(d, step)
                        now = S[:, d, step, :].rearrange("p (c n) -> p c n", c=KK)
                        nxt = S[:, d, step + 1, :].rearrange("p (c n) -> p c n", c=KK)
                        dve.tensor_tensor(nxt, now, dec[d][:, :, c:c + 1].to_broadcast([P, KK, GLA_DV]), ALU.mult)
                        dve.drain()
                        dve.wait_ge(k.prod_v.sem, v("prod_v", 2 + step))
                        dve.tensor_tensor(nxt, nxt, k.ps[:, state_bank(d, step), 0:KK * P].rearrange(
                            "p (c n) -> p c n", c=KK), ALU.add)
                        dve.drain().then_inc(k.v_for_t.sem, 1)
                    return of_chunk

                def outputs(d, q, at0, v):
                    dve.wait_ge(k.prod_v.sem, v("prod_v", 4))
                    o4 = mixed[:, 0:GLA_HEADS, bass.ds(at0, P)].rearrange("p (c j) n -> p j c n", j=2)
                    dve.tensor_tensor(o4, o4, k.ps[:, 4 * d + 1:4 * d + 3, 0:2 * P].rearrange(
                        "p j (c n) -> p j c n", c=2), ALU.add)
                    dve.drain().then_inc(k.v_for_t.sem, 1)
                program(dve, features, masked, state(0), state(1), outputs)
        for name, n in cnt.items():
            k.named[name].base += 2 * NT * n

        with nc.Block() as block:
            @block.scalar
            def _(act):
                sqr = la
                act.activation(sqr[:, :, :], o, ACT.Square).then_inc(k.a_for_t.sem, 1)
                act.activation(az[:, :, :], gg, ACT.Tanh, scale=0.5)
                act.wait_ge(k.prod_a.sem, k.prod_a.at(1))
                act.activation(mz[:, :, :], k.ps[:, 0:GLA_HEADS, :], ACT.Sqrt, scale=1.0 / GLA_DV, bias=k.eps[:, 2:3])
                act.drain().then_inc(k.a_for_v.sem, 1)

            @block.tensor
            def _(pe):
                pe.wait_ge(k.a_for_t.sem, k.a_for_t.at(1))
                for h in range(GLA_HEADS):
                    mm = pe.matmul(k.ps[:, h, :], k.square("ones"), la[:, h, :], start=True, stop=True)
                mm.then_inc(k.prod_a.sem, 1)

            @block.vector
            def _(dve):
                dve.wait_ge(k.a_for_v.sem, k.a_for_v.at(1))
                dve.reciprocal(mz[:, :, :], mz[:, :, :])
                dve.scalar_tensor_tensor(az[:, :, :], az[:, :, :], 1.0, gg, ALU.add, ALU.mult)
                dve.drain()
                dve.scalar_tensor_tensor(o, o, k.v("gla_norm"), mz[:, :, :], ALU.mult, ALU.mult)
                dve.drain()
                dve.scalar_tensor_tensor(o, az[:, :, :], 0.5, o, ALU.mult, ALU.mult)
        k.a_for_t.base += 1
        k.prod_a.base += 1
        k.a_for_v.base += 1


def stage_attention(k, q_, k_, v, mixed, wb, w):
    nc, t = k.nc, k.t
    HC = ATT_HEADS // 2
    with ExitStack() as s:
        def sb(name, shape):
            return k.sb(name, shape, stack=s)

        rope = sb("at_rope", [P, 2, SEQ])
        logs = sb("at_logs", [P, NT, SEQ])
        tmp = sb("at_tmp", [P, 2, SEQ])
        with nc.Block() as block:
            @block.sync
            def _(sp):
                sp.dma_start(rope[:, :, :].rearrange("p a n -> p (a n)"), t["rope"]).then_inc(k.loaded[0].sem, 16)
                sp.dma_start(logs[:, :, :].rearrange("p a n -> p (a n)"), t["pattern_logs"]).then_inc(
                    k.loaded[1].sem, 16)
                load_projection(k, sp, wb, w)
                sp.wait_ge(k.loaded[1].sem, k.loaded[1].at(16))

            @block.tensor
            def _(pe):
                for n in range(2 * HC):
                    src = (q_, k_)[n // HC][:, n % HC, :]
                    mm = pe.matmul(k.ps[:, n, :], k.square("rope"), src, start=True, stop=True)
                    mm.then_inc(k.prod_v.sem, 1)

            @block.vector
            def _(dve):
                dve.wait_ge(k.loaded[0].sem, k.loaded[0].at(16))
                for n in range(2 * HC):
                    x = (q_, k_)[n // HC][:, n % HC, :]
                    dve.wait_ge(k.prod_v.sem, k.prod_v.at(n + 1))
                    dve.tensor_tensor(tmp[:, n % 2, :], k.ps[:, n, :], rope[:, 1, :], ALU.mult)
                    dve.tensor_tensor(x, x, rope[:, 0, :], ALU.mult)
                    dve.drain()
                    dve.tensor_tensor(x, x, tmp[:, n % 2, :], ALU.add)
        for n in range(2):
            k.loaded[n].base += 16
        k.prod_v.base += 2 * HC

        qz, kp = sb("at_qz", [P, 2, 2, SEQ]), sb("at_kp", [P, 2, SEQ])
        vh = sb("at_vh", [P, 2, NT, P])
        R = 3
        sc, pr = sb("at_sc", [P, R, SEQ]), sb("at_pr", [P, R, SEQ])
        pt = sb("at_pt", [P, 2, NT, P])
        mx, z, rz = sb("at_mx", [P, R, 1]), sb("at_z", [P, R, 1]), sb("at_rz", [P, R, 1])
        G = 4
        U = G * NT
        TURNS = HC // 2

        def rows(h):
            return slice(h % 2 * 64, h % 2 * 64 + 64)

        with nc.Block() as block:
            @block.gpsimd
            def _(pool):
                pool.memset(qz[:, :, :, :], 0.0)
                pool.drain()
                with pool.Fori(0, TURNS) as i:
                    for j in range(2):
                        pool.wait_ge(k.used.sem, i * G + k.used.at(2 * j + 2 - G))
                        for h in range(2):
                            pool.tensor_copy(qz[rows(h), j, h, :],
                                             q_[rows(h), bass.ds(i * 2 + j, 1), :].rearrange("p a n -> p (a n)"))
                            pool.drain()
                        pool.tensor_copy(kp[:, j, :], k_[:, bass.ds(i * 2 + j, 1), :].rearrange("p a n -> p (a n)"))
                        pool.tensor_copy(vh[:, j, :, :], v[:, :, bass.ds(i * (2 * P) + j * P, P)])
                        pool.drain().then_inc(k.p_for_t.sem, 1)

            @block.tensor
            def _(pe):
                with pe.Fori(0, TURNS) as i:
                    def scores(n):
                        h, q = n // NT, n % NT
                        if n % (2 * NT) == 0:
                            pe.wait_ge(k.p_for_t.sem, i * 2 + k.p_for_t.at(h // 2 + 1))
                        pe.wait_ge(k.v_for_a.sem, i * U + k.v_for_a.at(n - 3))
                        pe.matmul(k.ps[:, n % 4, :], qz[:, h // 2, h % 2, q * P:(q + 1) * P], kp[:, h // 2, :],
                                  start=True, stop=True).then_inc(k.prod_v.sem, 1)

                    def turn(n):
                        pe.wait_ge(k.v_for_t.sem, i * U + k.v_for_t.at(n + 1))
                        pe.wait_ge(k.a_for_t.sem, i * U + k.a_for_t.at(n - 1))
                        for j in range(NT):
                            mm = pe.transpose(k.ps[:, 4 + n % 2, j * P:(j + 1) * P], pr[:, n % R, j * P:(j + 1) * P],
                                              k.square("ident"))
                        mm.then_inc(k.prod_a.sem, 1)

                    def values(n):
                        h, q = n // NT, n % NT
                        pe.wait_ge(k.a_for_t.sem, i * U + k.a_for_t.at(n + 1))
                        if q == 0:
                            pe.wait_ge(k.free_v.sem, i * G + k.free_v.at(h - 1))
                        for j in range(NT):
                            mm = pe.matmul(k.ps[rows(h), 6 + h % 2, q * P:(q + 1) * P], vh[:, h // 2, j, rows(h)],
                                           pt[:, n % 2, j, :], start=j == 0, stop=j == NT - 1)
                        if q == NT - 1:
                            mm.then_inc(k.used.sem, 1)

                    scores(0)
                    scores(1)
                    for n in range(U):
                        if n + 2 < U:
                            scores(n + 2)
                        turn(n)
                        if n:
                            values(n - 1)
                    values(U - 1)

            @block.vector
            def _(dve):
                with dve.Fori(0, TURNS) as i:
                    def softmax(n):
                        j = n % R
                        dve.wait_ge(k.prod_v.sem, i * U + k.prod_v.at(n + 1))
                        dve.wait_ge(k.a_for_v.sem, i * U + k.a_for_v.at(n + 1 - R))
                        dve.scalar_tensor_tensor(sc[:, j, :], k.ps[:, n % 4, :], ATT_HEAD ** -0.5, logs[:, n % NT, :],
                                                 ALU.mult, ALU.add)
                        dve.drain()
                        dve.tensor_reduce(mx[:, j, :], sc[:, j, :], AX.X, ALU.max)
                        dve.drain()
                        dve.tensor_scalar(mx[:, j, :], mx[:, j, :], -1.0, None, ALU.mult)
                        dve.drain().then_inc(k.v_for_a.sem, 1)

                    def normalise(n):
                        j = n % R
                        dve.wait_ge(k.a_for_v.sem, i * U + k.a_for_v.at(n + 1))
                        dve.reciprocal(rz[:, j, :], z[:, j, :])
                        dve.drain()
                        dve.tensor_scalar(pr[:, j, :], pr[:, j, :], rz[:, j, :], None, ALU.mult).then_inc(
                            k.v_for_t.sem, 1)

                    def head(h):
                        dve.wait_ge(k.used.sem, i * G + k.used.at(h + 1))
                        dve.tensor_copy(mixed[rows(h), bass.ds(i * 2 + (GLA_HEADS + h // 2), 1), :].rearrange(
                            "p a n -> p (a n)"), k.ps[rows(h), 6 + h % 2, :]).then_inc(k.free_v.sem, 1)

                    softmax(0)
                    for n in range(U):
                        if n + 1 < U:
                            softmax(n + 1)
                        normalise(n)
                        if n % NT == 1 and n > NT:
                            head(n // NT - 1)
                    head(G - 1)

            @block.scalar
            def _(act):
                with act.Fori(0, TURNS) as i:
                    def turned(n):
                        act.wait_ge(k.prod_a.sem, i * U + k.prod_a.at(n + 1))
                        act.activation(pt[:, n % 2, :, :].rearrange("p j n -> p (j n)"), k.ps[:, 4 + n % 2, :],
                                       ACT.Copy).then_inc(k.a_for_t.sem, 1)

                    for n in range(U):
                        act.wait_ge(k.v_for_a.sem, i * U + k.v_for_a.at(n + 1))
                        act.wait_ge(k.prod_a.sem, i * U + k.prod_a.at(n + 1 - R))
                        act.activation(pr[:, n % R, :], sc[:, n % R, :], ACT.Exp, bias=mx[:, n % R, :],
                                       accum_out=z[:, n % R, :])
                        act.drain().then_inc(k.a_for_v.sem, 1)
                        if n:
                            turned(n - 1)
                    turned(U - 1)
        for name, n in (("prod_v", U), ("prod_a", U), ("v_for_a", U), ("v_for_t", U), ("a_for_t", U), ("a_for_v", U),
                        ("free_v", G), ("used", G), ("p_for_t", 2)):
            k.named[name].base += TURNS * n


def stage_second_mixer(k):
    with ExitStack() as s:
        mixed = k.sb("mixed", [P, KC, SEQ], stack=s)
        with ExitStack() as s1:
            fm = [k.sb(f"fm{n}", [P, 4, SEQ], stack=s1) for n in range(4)]
            tm = [k.sb(f"tm{n}", [P, NT, 512], stack=s1) for n in range(2)]
            lr = k.sb("lr", [64, SEQ], stack=s1)
            stage_in_projection(k, fm, tm, lr)
            stage_linear_attention(k, fm[0][:, :, :], fm[1][:, :, :], tm[0], lr, mixed)
            wb = k.sb("wb_w_out", [P, 2, KC, 512], stack=s1)
            stage_attention(k, fm[2], fm[3], tm[1], mixed, wb, k.t["w_out_2"])
            stage_project_residual(k, wb, mixed, None, alpha=1.0)


def stage_second_moe(k):
    t = k.t
    m = Moe("hier", 32, 512, [t[n][0] for n in ("expert_w_gate_2", "expert_w_up_2", "expert_w_down_2")], 1,
            [(t["router_group_w_2"][0], 0, 4), (t["router_expert_w_2"][0], 4, 32)], 4)
    with ExitStack() as s:
        h = k.sb("hier_h", [P, KC, SEQ], stack=s)
        stage_rms_norm(k, h, k.v("norm2"))
        stage_moe(k, m, h, None, 1.0)


def stage_output(k):
    with ExitStack() as s:
        y = k.sb("out_y", [P, KC, SEQ], stack=s)

        def store(sp):
            for n in range(2):
                sp.wait_ge(k.normed.sem, k.normed.at(4 * (n + 1)))
                sp.dma_start(k.out[:, 4 * n:4 * n + 4, :], y[:, 4 * n:4 * n + 4, :]).then_inc(k.stored[n].sem, 16)
            for n in range(2):
                sp.wait_ge(k.stored[n].sem, k.stored[n].at(16))

        stage_rms_norm(k, y, k.v("final_norm"), store)
        for n in range(2):
            k.stored[n].base += 16


WEIGHTS = ["ada_w", "rk_w_rkv", "rk_w1", "rk_w2", "rk_a1", "rk_a2", "rk_g1", "rk_g2", "rk_w_o", "pool_w",
           "ffn_w1", "ffn_w3", "ffn_w2", "moe_router_w", "moe_w1", "moe_w3", "moe_w2", "w_in_2", "w_out_2",
           "router_group_w_2", "router_expert_w_2", "expert_w_gate_2", "expert_w_up_2", "expert_w_down_2",
           "gla_fwd_gate_w_2", "gla_bwd_gate_w_2"]


def lay_out(inputs):
    a = {n: np.ascontiguousarray(inputs[n]) for n in WEIGHTS}
    both = np.concatenate([np.asarray(inputs["ctx"])[0], np.asarray(inputs["x"])[0]], axis=0)
    a["xT"] = np.ascontiguousarray(both.T.reshape(KC, P, TOK).transpose(1, 0, 2))
    columns = {
        "c": inputs["c"], "c_ctx": inputs["c_ctx"], "k_k": inputs["rk_k_k"], "k_a": inputs["rk_k_a"],
        "r_k": inputs["rk_r_k"], "lnx_g": inputs["rk_lnx_g"], "lnx_b": inputs["rk_lnx_b"],
        "pool_scale": inputs["pool_scale"], "norm1": inputs["norm1_w_2"], "norm2": inputs["norm2_w_2"],
        "final_norm": inputs["final_norm_w_2"], "gla_norm": inputs["gla_norm_w_2"],
    }
    for i in range(2):
        columns[f"ada_b{i}"] = inputs["ada_b"][i]
        columns[f"a0_{i}"] = inputs["rk_a0"][0, i]
        for j in range(2):
            columns[f"ln_g{i}{j}"] = inputs["ln_g"][i, j]
            columns[f"ln_b{i}{j}"] = inputs["ln_b"][i, j]
    for m in range(6):
        columns[f"mu{m}"] = inputs["rk_mu"][0, m]
    a["vectors"] = np.ascontiguousarray(
        np.concatenate([np.asarray(columns[n]).reshape(-1, P).T for n in VECTORS], axis=1))
    a["rows"] = np.concatenate([np.asarray(inputs[n]).reshape(1, -1) for n in
                                ("rk_w0", "gla_fwd_gate_b_2", "gla_bwd_gate_b_2")], axis=1)
    a["router_rows"] = np.concatenate([np.asarray(inputs[n]).reshape(1, -1) for n in
                                       ("moe_router_b", "router_group_b_2", "router_expert_b_2")], axis=1)
    a["squares"] = square_constants()
    a["head_rows"] = head_rows()
    a["rope"] = rope_tables()
    a["pattern_logs"] = pattern_logs()
    a["pool_counts"] = pool_counts()
    a["iotas"] = np.tile(np.arange(40, dtype=np.float32)[None], (P, 1))
    a["token_ids"] = np.ascontiguousarray(np.arange(SEQ, dtype=np.int32).reshape(NT, P).T)
    return a


def kernel(**inputs):
    import concourse.bacc as bacc
    from concourse.bass_utils import run_bass_kernel_spmd

    nc = bacc.Bacc("TRN2", target_bir_lowering=False, num_devices=1)
    arrays = {f"in_{n}": a for n, a in lay_out(inputs).items()}
    t = {n[3:]: nc.dram_tensor(n, a.shape, mybir.dt.from_np(a.dtype), kind="ExternalInput").ap()
         for n, a in arrays.items()}
    out = nc.dram_tensor("outT", (P, KC, SEQ), F32, kind="ExternalOutput").ap()
    build(nc, t, out)
    r = run_bass_kernel_spmd(nc, [arrays], core_ids=[0])
    got = r.results[0]["outT"]
    return np.ascontiguousarray(got.transpose(1, 0, 2).reshape(D, SEQ).T)[None]
```
